# Optimizing a Trainium2 kernel written in Bass

```python
import math, functools
import jax, jax.numpy as jnp
from jax import lax
import numpy as np

D_MODEL = 1024
BATCH = 1
SEQ = 1024
DEPTH = 1
DEC_BATCH = 8
DEC_SEQ = 4
PAST_LEN = 4096
PAGE_SIZE = 128

MLA_HEADS = 16
QK_NOPE = 64
QK_ROPE = 32
V_HEAD = 64
Q_LORA = 384
KV_LORA = 256
ROPE_THETA = 10000.0
Q_BLOCK = 128
ATTN_SCALE = (QK_NOPE + QK_ROPE) ** -0.5
SSM_EXPAND = 2
D_INNER = SSM_EXPAND * D_MODEL
SSM_HEADDIM = 64
SSM_HEADS = D_INNER // SSM_HEADDIM
SSM_GROUPS = 4
SSM_STATE = 128
CONV_WIDTH = 4
CONV_DIM = D_INNER + 2 * SSM_GROUPS * SSM_STATE
SSD_CHUNK = 256
D_FF = ((8 * D_MODEL // 3 + 255) // 256) * 256
ALPHA = (2.0 * DEPTH) ** 0.25
BETA = (8.0 * DEPTH) ** -0.25
IN_SPLITS = (Q_LORA, KV_LORA, QK_ROPE, D_INNER, CONV_DIM, SSM_HEADS, 2 * D_MODEL)
IN_OFFSETS = tuple(sum(IN_SPLITS[:i + 1]) for i in range(len(IN_SPLITS) - 1))
D_IN_PROJ = sum(IN_SPLITS)

kernel_name = "hybrid_mla_ssd_gated_deepnorm_step"

def rms_norm(x, g, eps):
    xf = x.astype(jnp.float32)
    xf = xf * lax.rsqrt(jnp.mean(xf * xf, axis=-1, keepdims=True) + eps)
    return (xf * g.astype(jnp.float32)).astype(x.dtype)

def layer_norm(x, g, b, eps=1e-5):
    xf = x.astype(jnp.float32)
    mu = jnp.mean(xf, axis=-1, keepdims=True)
    var = jnp.mean(jnp.square(xf - mu), axis=-1, keepdims=True)
    out = (xf - mu) * lax.rsqrt(var + eps) * g.astype(jnp.float32) + b.astype(jnp.float32)
    return out.astype(x.dtype)

def apply_rope(x, pos):
    inv = ROPE_THETA ** (-jnp.arange(0, QK_ROPE, 2, dtype=jnp.float32) / QK_ROPE)
    ang = pos.astype(jnp.float32)[:, None] * inv[None, :]
    cos = jnp.cos(ang)[None, :, None, :]
    sin = jnp.sin(ang)[None, :, None, :]
    xf = x.astype(jnp.float32)
    x1, x2 = xf[..., :QK_ROPE // 2], xf[..., QK_ROPE // 2:]
    out = jnp.concatenate([x1 * cos - x2 * sin, x2 * cos + x1 * sin], axis=-1)
    return out.astype(x.dtype)

def mla_project(c_q, c_kv, k_pe, pos, q_norm_g, kv_norm_g, w_uq):
    B, T, _ = c_q.shape
    q = jnp.einsum('btr,re->bte', rms_norm(c_q, q_norm_g, 1e-6), w_uq)
    q = q.reshape(B, T, MLA_HEADS, QK_NOPE + QK_ROPE)
    q_nope = q[..., :QK_NOPE]
    q_pe = apply_rope(q[..., QK_NOPE:], pos)
    c_kv = rms_norm(c_kv, kv_norm_g, 1e-6)
    k_pe = apply_rope(k_pe[:, :, None, :], pos)[:, :, 0, :]
    return q_nope, q_pe, c_kv, k_pe

def mla_prompt_attention(q_nope, q_pe, c_kv, k_pe, w_ukv):
    B, S, _, _ = q_nope.shape
    kv = jnp.einsum('bsc,ce->bse', c_kv, w_ukv).reshape(B, S, MLA_HEADS, QK_NOPE + V_HEAD)
    k_nope, v = kv[..., :QK_NOPE], kv[..., QK_NOPE:]
    key_pos = jnp.arange(S)

    def block(i):
        start = i * Q_BLOCK
        qn = lax.dynamic_slice_in_dim(q_nope, start, Q_BLOCK, axis=1)
        qp = lax.dynamic_slice_in_dim(q_pe, start, Q_BLOCK, axis=1)
        s = (jnp.einsum('bqhd,bkhd->bhqk', qn, k_nope)
             + jnp.einsum('bqhr,bkr->bhqk', qp, k_pe)).astype(jnp.float32) * ATTN_SCALE
        q_pos = start + jnp.arange(Q_BLOCK)
        mask = key_pos[None, :] <= q_pos[:, None]
        s = jnp.where(mask, s, jnp.finfo(jnp.float32).min)
        p = jax.nn.softmax(s, axis=-1).astype(v.dtype)
        return jnp.einsum('bhqk,bkhd->bqhd', p, v)

    out = lax.map(block, jnp.arange(S // Q_BLOCK))
    return out.transpose(1, 0, 2, 3, 4).reshape(B, S, MLA_HEADS * V_HEAD)

def mla_sample_attention(q_nope, q_pe, c_kv_new, k_pe_new, cache_ckv, cache_kpe, layer, page_table, w_ukv):
    B, T, _, _ = q_nope.shape
    w = w_ukv.reshape(KV_LORA, MLA_HEADS, QK_NOPE + V_HEAD)
    w_uk, w_uv = w[..., :QK_NOPE], w[..., QK_NOPE:]
    past_ckv = cache_ckv[layer, page_table].reshape(B, -1, KV_LORA)
    past_kpe = cache_kpe[layer, page_table].reshape(B, -1, QK_ROPE)
    past_len = past_ckv.shape[1]
    q_lat = jnp.einsum('bthd,chd->bthc', q_nope, w_uk)
    s_past = (jnp.einsum('bthc,bkc->bhtk', q_lat, past_ckv)
              + jnp.einsum('bthr,bkr->bhtk', q_pe, past_kpe)).astype(jnp.float32)
    s_new = (jnp.einsum('bthc,bsc->bhts', q_lat, c_kv_new)
             + jnp.einsum('bthr,bsr->bhts', q_pe, k_pe_new)).astype(jnp.float32)
    causal = jnp.arange(T)[None, :] <= jnp.arange(T)[:, None]
    s_new = jnp.where(causal, s_new, jnp.finfo(jnp.float32).min)
    s = jnp.concatenate([s_past, s_new], axis=-1) * ATTN_SCALE
    p = jax.nn.softmax(s, axis=-1).astype(c_kv_new.dtype)
    o_lat = (jnp.einsum('bhtk,bkc->bthc', p[..., :past_len], past_ckv)
             + jnp.einsum('bhts,bsc->bthc', p[..., past_len:], c_kv_new))
    o = jnp.einsum('bthc,chd->bthd', o_lat, w_uv)
    return o.reshape(B, T, MLA_HEADS * V_HEAD)

def causal_conv(xbc, conv_state, conv_w, conv_b):
    T = xbc.shape[1]
    xpad = jnp.concatenate([conv_state.astype(xbc.dtype), xbc], axis=1)
    out = conv_b + sum(xpad[:, k:k + T] * conv_w[k] for k in range(CONV_WIDTH))
    return jax.nn.silu(out), xpad[:, xpad.shape[1] - (CONV_WIDTH - 1):]

def ssd_scan(x, dt, a, b, c, init_state):
    Bsz, L = x.shape[0], x.shape[1]
    chunk = min(SSD_CHUNK, L)
    pad = (-L) % chunk
    if pad:
        pw = lambda t: jnp.pad(t, [(0, 0), (0, pad)] + [(0, 0)] * (t.ndim - 2))
        x, dt, b, c = pw(x), pw(dt), pw(b), pw(c)
    nc = (L + pad) // chunk
    G, Hg = SSM_GROUPS, SSM_HEADS // SSM_GROUPS
    xr = x.reshape(Bsz, nc, chunk, G, Hg, SSM_HEADDIM)
    dtr = dt.reshape(Bsz, nc, chunk, G, Hg)
    br = b.reshape(Bsz, nc, chunk, G, SSM_STATE)
    cr = c.reshape(Bsz, nc, chunk, G, SSM_STATE)
    a_cum = jnp.cumsum(dtr * a.reshape(G, Hg), axis=2)
    xdt = xr * dtr[..., None]
    seg = a_cum[:, :, :, None] - a_cum[:, :, None, :]
    tril = (jnp.arange(chunk)[:, None] >= jnp.arange(chunk)[None, :])[:, :, None, None]
    decay = jnp.exp(jnp.where(tril, seg, -jnp.inf))
    cb = jnp.einsum('bclgn,bcsgn->bclsg', cr, br)
    y_diag = jnp.einsum('bclsg,bclsgh,bcsghp->bclghp', cb, decay, xdt)
    decay_to_end = jnp.exp(a_cum[:, :, -1:] - a_cum)
    chunk_states = jnp.einsum('bclgn,bclgh,bclghp->bcghpn', br, decay_to_end, xdt)
    chunk_decay = jnp.exp(a_cum[:, :, -1])

    def step(state, inp):
        cs, cd = inp
        return state * cd[..., None, None] + cs, state

    init = init_state.astype(jnp.float32).reshape(Bsz, G, Hg, SSM_HEADDIM, SSM_STATE)
    final, prev = lax.scan(step, init, (jnp.swapaxes(chunk_states, 0, 1).astype(jnp.float32),
                                        jnp.swapaxes(chunk_decay, 0, 1)))
    prev = jnp.swapaxes(prev, 0, 1)
    y_off = jnp.einsum('bclgn,bcghpn,bclgh->bclghp', cr, prev, jnp.exp(a_cum))
    y = (y_diag + y_off).reshape(Bsz, nc * chunk, SSM_HEADS, SSM_HEADDIM)[:, :L]
    return y.astype(x.dtype), final.reshape(Bsz, SSM_HEADS, SSM_HEADDIM, SSM_STATE).astype(init_state.dtype)

def mamba2_branch(z, xbc, dt_raw, conv_state, ssm_state, conv_w, conv_b, dt_bias, a_log, d_skip, ssm_norm_g):
    B, T, _ = z.shape
    xbc_c, new_conv = causal_conv(xbc, conv_state, conv_w, conv_b)
    xs = xbc_c[..., :D_INNER].reshape(B, T, SSM_HEADS, SSM_HEADDIM)
    bs = xbc_c[..., D_INNER:D_INNER + SSM_GROUPS * SSM_STATE].reshape(B, T, SSM_GROUPS, SSM_STATE)
    cs = xbc_c[..., D_INNER + SSM_GROUPS * SSM_STATE:].reshape(B, T, SSM_GROUPS, SSM_STATE)
    dt = jax.nn.softplus(dt_raw.astype(jnp.float32) + dt_bias.astype(jnp.float32))
    a = -jnp.exp(a_log.astype(jnp.float32))
    y, new_ssm = ssd_scan(xs, dt, a, bs, cs, ssm_state)
    y = (y + xs * d_skip[:, None]).reshape(B, T, D_INNER)
    yg = (y * jax.nn.silu(z)).reshape(B, T, SSM_GROUPS, D_INNER // SSM_GROUPS)
    yg = rms_norm(yg, ssm_norm_g.reshape(SSM_GROUPS, D_INNER // SSM_GROUPS), 1e-5)
    return yg.reshape(B, T, D_INNER), new_conv, new_ssm

def swiglu_ffn(h, w_ffn_gate, w_ffn_up, w_ffn_down):
    g = jnp.einsum('btd,df->btf', h, w_ffn_gate)
    u = jnp.einsum('btd,df->btf', h, w_ffn_up)
    return jnp.einsum('btf,fd->btd', jax.nn.silu(g) * u, w_ffn_down)

def hybrid_layer(x, pos, conv_state, ssm_state, attend, w_in, b_gate, q_norm_g, kv_norm_g, w_uq,
                 conv_w, conv_b, dt_bias, a_log, d_skip, ssm_norm_g, w_branch_a, w_branch_b, w_out,
                 ln1_g, ln1_b, w_ffn_gate, w_ffn_up, w_ffn_down, ln2_g, ln2_b):
    proj = jnp.einsum('btd,de->bte', x, w_in)
    c_q, c_kv, k_pe, z, xbc, dt_raw, g_logits = jnp.split(proj, IN_OFFSETS, axis=-1)
    q_nope, q_pe, c_kv, k_pe = mla_project(c_q, c_kv, k_pe, pos, q_norm_g, kv_norm_g, w_uq)
    attn = attend(q_nope, q_pe, c_kv, k_pe)
    ssm_out, new_conv, new_ssm = mamba2_branch(z, xbc, dt_raw, conv_state, ssm_state, conv_w, conv_b,
                                               dt_bias, a_log, d_skip, ssm_norm_g)
    gates = jax.nn.sigmoid(g_logits + b_gate)
    g_a, g_b = gates[..., :D_MODEL], gates[..., D_MODEL:]
    merged = (g_a * jnp.einsum('bte,ed->btd', attn, w_branch_a)
              + g_b * jnp.einsum('bte,ed->btd', ssm_out, w_branch_b))
    mix = jnp.einsum('btd,de->bte', merged, w_out)
    h = layer_norm(ALPHA * x + mix, ln1_g, ln1_b)
    y = layer_norm(ALPHA * h + swiglu_ffn(h, w_ffn_gate, w_ffn_up, w_ffn_down), ln2_g, ln2_b)
    return y, c_kv, k_pe, new_conv, new_ssm

def setup_inputs(seed: int = 0) -> dict:
    key = jax.random.key(seed)
    ks = jax.random.split(key, 40)
    f32 = jnp.float32
    n_pages = PAST_LEN // PAGE_SIZE
    n_used = DEC_BATCH * n_pages
    n_pool = -(-5 * n_used // 4)
    nrm = lambda k, shape, s: jax.random.normal(k, shape, f32) * s
    dt0 = jnp.exp(jax.random.uniform(ks[12], (DEPTH, SSM_HEADS), f32, math.log(1e-3), math.log(1e-1)))
    page_table = jax.random.permutation(ks[6], n_pool)[:n_used].reshape(DEC_BATCH, n_pages).astype(jnp.int32)
    return {
        "x_prompt": nrm(ks[0], (BATCH, SEQ, D_MODEL), 1.0),
        "x_sample": nrm(ks[1], (DEC_BATCH, DEC_SEQ, D_MODEL), 1.0),
        "cache_ckv": nrm(ks[2], (DEPTH, n_pool, PAGE_SIZE, KV_LORA), 1.0),
        "cache_kpe": nrm(ks[3], (DEPTH, n_pool, PAGE_SIZE, QK_ROPE), 1.0),
        "state_ssm": nrm(ks[4], (DEPTH, DEC_BATCH, SSM_HEADS, SSM_HEADDIM, SSM_STATE), 0.1),
        "state_conv": nrm(ks[5], (DEPTH, DEC_BATCH, CONV_WIDTH - 1, CONV_DIM), 1.0),
        "page_table": page_table,
        "w_in": nrm(ks[7], (DEPTH, D_MODEL, D_IN_PROJ), D_MODEL ** -0.5),
        "b_gate": nrm(ks[8], (DEPTH, 2 * D_MODEL), 0.1),
        "q_norm_g": 1.0 + nrm(ks[9], (DEPTH, Q_LORA), 0.02),
        "kv_norm_g": 1.0 + nrm(ks[10], (DEPTH, KV_LORA), 0.02),
        "w_uq": nrm(ks[11], (DEPTH, Q_LORA, MLA_HEADS * (QK_NOPE + QK_ROPE)), Q_LORA ** -0.5),
        "w_ukv": nrm(ks[13], (DEPTH, KV_LORA, MLA_HEADS * (QK_NOPE + V_HEAD)), KV_LORA ** -0.5),
        "conv_w": nrm(ks[14], (DEPTH, CONV_WIDTH, CONV_DIM), CONV_WIDTH ** -0.5),
        "conv_b": nrm(ks[15], (DEPTH, CONV_DIM), 0.02),
        "dt_bias": dt0 + jnp.log(-jnp.expm1(-dt0)),
        "a_log": jnp.log(jax.random.uniform(ks[16], (DEPTH, SSM_HEADS), f32, 1.0, 16.0)),
        "d_skip": 1.0 + nrm(ks[17], (DEPTH, SSM_HEADS), 0.1),
        "ssm_norm_g": 1.0 + nrm(ks[18], (DEPTH, D_INNER), 0.02),
        "w_branch_a": nrm(ks[19], (DEPTH, MLA_HEADS * V_HEAD, D_MODEL), (MLA_HEADS * V_HEAD) ** -0.5),
        "w_branch_b": nrm(ks[20], (DEPTH, D_INNER, D_MODEL), D_INNER ** -0.5),
        "w_out": nrm(ks[21], (DEPTH, D_MODEL, D_MODEL), BETA * D_MODEL ** -0.5),
        "ln1_g": 1.0 + nrm(ks[22], (DEPTH, D_MODEL), 0.02),
        "ln1_b": nrm(ks[23], (DEPTH, D_MODEL), 0.02),
        "w_ffn_gate": nrm(ks[24], (DEPTH, D_MODEL, D_FF), D_MODEL ** -0.5),
        "w_ffn_up": nrm(ks[25], (DEPTH, D_MODEL, D_FF), D_MODEL ** -0.5),
        "w_ffn_down": nrm(ks[26], (DEPTH, D_FF, D_MODEL), BETA * D_FF ** -0.5),
        "ln2_g": 1.0 + nrm(ks[27], (DEPTH, D_MODEL), 0.02),
        "ln2_b": nrm(ks[28], (DEPTH, D_MODEL), 0.02),
    }

def reference(x_prompt, x_sample, cache_ckv, cache_kpe, state_ssm, state_conv, page_table,
              w_in, b_gate, q_norm_g, kv_norm_g, w_uq, w_ukv, conv_w, conv_b, dt_bias, a_log, d_skip,
              ssm_norm_g, w_branch_a, w_branch_b, w_out, ln1_g, ln1_b, w_ffn_gate, w_ffn_up, w_ffn_down,
              ln2_g, ln2_b):
    B, S, _ = x_prompt.shape
    T = x_sample.shape[1]
    past_len = page_table.shape[1] * PAGE_SIZE
    pos_p = jnp.arange(S)
    pos_s = past_len + jnp.arange(T)
    xp, xs = x_prompt, x_sample
    ckv_p, kpe_p, ssm_p, conv_p = [], [], [], []
    ckv_s, kpe_s, ssm_s, conv_s = [], [], [], []
    for l in range(DEPTH):
        lw = (w_in[l], b_gate[l], q_norm_g[l], kv_norm_g[l], w_uq[l], conv_w[l], conv_b[l], dt_bias[l],
              a_log[l], d_skip[l], ssm_norm_g[l], w_branch_a[l], w_branch_b[l], w_out[l], ln1_g[l], ln1_b[l],
              w_ffn_gate[l], w_ffn_up[l], w_ffn_down[l], ln2_g[l], ln2_b[l])
        conv0 = jnp.zeros((B, CONV_WIDTH - 1, CONV_DIM), xp.dtype)
        ssm0 = jnp.zeros((B, SSM_HEADS, SSM_HEADDIM, SSM_STATE), xp.dtype)
        attend_p = functools.partial(mla_prompt_attention, w_ukv=w_ukv[l])
        attend_s = functools.partial(mla_sample_attention, cache_ckv=cache_ckv, cache_kpe=cache_kpe,
                                     layer=l, page_table=page_table, w_ukv=w_ukv[l])
        xp, a1, a2, a3, a4 = hybrid_layer(xp, pos_p, conv0, ssm0, attend_p, *lw)
        xs, b1, b2, b3, b4 = hybrid_layer(xs, pos_s, state_conv[l], state_ssm[l], attend_s, *lw)
        ckv_p.append(a1); kpe_p.append(a2); conv_p.append(a3); ssm_p.append(a4)
        ckv_s.append(b1); kpe_s.append(b2); conv_s.append(b3); ssm_s.append(b4)
    return (xp, xs, jnp.stack(ckv_p), jnp.stack(kpe_p), jnp.stack(ssm_p), jnp.stack(conv_p),
            jnp.stack(ckv_s), jnp.stack(kpe_s), jnp.stack(ssm_s), jnp.stack(conv_s))


_drawn_inputs = setup_inputs


def setup_inputs(seed=0):
    import zlib

    import numpy as np

    out = dict(_drawn_inputs(seed))
    spreads = {}
    factors = {'cache_ckv': 7.969,
     'cache_kpe': 8.0,
     'b_gate': 5.331,
     'q_norm_g': 8.0,
     'kv_norm_g': 7.404,
     'd_skip': 4.074,
     'ssm_norm_g': 21.794,
     'ln1_g': 2.704,
     'ln1_b': 2.793,
     'ln2_g': 29.746,
     'ln2_b': 26.339}
    for name, (base, spread) in spreads.items():
        noise = np.random.default_rng([zlib.crc32(name.encode()), seed]).standard_normal(out[name].shape)
        drawn = base * np.exp(spread * noise) if base else spread * noise
        out[name] = __import__('jax').numpy.asarray(drawn.astype(out[name].dtype))
    for name, factor in factors.items():
        out[name] = (out[name] * factor).astype(out[name].dtype)
    return out
```

```python
from contextlib import ExitStack, contextmanager
import math

import numpy as np
import concourse.bass as bass
from concourse import mybir

F32 = mybir.dt.float32
F32R = mybir.dt.float32r
BF16 = mybir.dt.bfloat16
I32 = mybir.dt.int32
ALU = mybir.AluOpType
ACT = mybir.ActivationFunctionType
AX = mybir.AxisListType.X

P = 128
D_MODEL, SEQ, NB, NT = 1024, 1024, 8, 4
NS = NB * NT
TOK = SEQ + NS
CH = TOK // 3
HEADS, NOPE, ROPE, VH = 16, 64, 32, 64
QH = NOPE + ROPE
QL, KL = 384, 256
PAGE, PAST = 128, 4096
NPG = PAST // PAGE
DI, SH, SP_, SG, SN = 2048, 32, 64, 4, 128
CONV, CW = DI + 2 * SG * SN, 4
FF = 2816
ALPHA = 2.0 ** 0.25
SCALE = QH ** -0.5
KT = D_MODEL // P
C_Q, C_KV, C_PE = 0, QL, QL + KL
C_Z = C_PE + ROPE
C_XBC = C_Z + DI
C_DT = C_XBC + CONV
C_G = C_DT + SH
UNIT = 1024
RAW, SPLIT = 4, 2


class Tally:

    def __init__(self, sem):
        self.sem, self.n, self.loops = sem, 0, []

    def value(self, back=0):
        v = self.n - back
        for reg, per, _ in self.loops:
            v = reg * per + v
        return v

    def adds(self, by):
        self.n += by
        return by

    def next(self, by=1):
        self.n += by
        return self.value()

    def same(self):
        return self.value()

    def held(self, by=1):
        self.n += by
        return self.value(by)

    def ahead(self):
        return self.value(-1)


def pairs(k, d):
    return {k[f"{n}{b}"]: v for n, v in d.items() for b in range(2)}


@contextmanager
def looped(eng, count, per):
    begun = {t: t.n for t in per}
    with eng.Fori(0, count) as i:
        for t, p in per.items():
            t.loops.append((i, p, t.n))
        yield i
    wrong = {t.sem.name: t.n - begun[t] for t, p in per.items() if t.n - begun[t] != p}
    assert not wrong, wrong
    for t, p in per.items():
        t.loops.pop()
        t.n += p * (count - 1)


UNITS = {1: 6, 2: 18, 3: 74, 4: 74, 5: 74, 6: 74}
TOTAL_UNITS = 74 + 6 * 4 + 8 + 6 * (FF // 256)


def constants():
    half = ROPE // 2
    inv = (np.float32(10000.0) ** (-np.arange(0, ROPE, 2, dtype=np.float32) / np.float32(ROPE))).astype(np.float32)
    pos = np.concatenate([np.arange(SEQ), np.tile(PAST + np.arange(NT), NB)]).astype(np.float32)
    ang = (inv[:, None] * pos[None, :]).astype(np.float32)
    rope = np.zeros((2, P, TOK), np.float32)
    rope[0, NOPE:QH] = np.tile(np.cos(ang), (2, 1))
    rope[1, NOPE:QH] = np.tile(np.sin(ang), (2, 1))
    c = {"ident": np.eye(P), "ones": np.ones((P, P))}
    at = np.arange(P)
    c["causal"] = (at[:, None] <= at[None, :]) * 1.0
    s = np.arange(NS)
    same = (s[:, None] // NT == s[None, :] // NT)
    c["causal_s"] = np.zeros((P, NS))
    c["causal_s"][:NS] = same & (s[:, None] <= s[None, :])
    c["same_s"] = np.zeros((P, NS))
    c["same_s"][:NS] = same
    c["after"] = np.where(at[None, :] <= at[:, None], 0.0, -1e30)
    c["turn"] = np.zeros((P, ROPE))
    for i in range(half):
        c["turn"][NOPE + half + i, i] = -1.0
        c["turn"][NOPE + i, half + i] = 1.0
    c["spread"] = np.zeros((P, DI // P, P))
    for h in range(SH):
        c["spread"][h, h // 2, 64 * (h % 2):64 * (h % 2) + 64] = 1.0
    c["quarter"] = (at % 4)[:, None] * 1.0
    c["batch"] = np.zeros((P, NB))
    c["batch"][s, s // NT] = 1.0
    c["newkeys"] = np.full((P, NB, HEADS, NT), -1e30)
    for i in s:
        for t in range(i % NT, NT):
            c["newkeys"][i, i // NT, :, t] = 0.0
    names = ["ident", "ones", "causal", "causal_s", "same_s", "after", "turn", "spread", "quarter", "batch", "newkeys"]
    parts = [c[n].reshape(P, -1).astype(np.float32) for n in names]
    where, at = {}, 0
    for n, a in zip(names, parts):
        where[n] = (at, a.shape[1])
        at += a.shape[1]
    return np.ascontiguousarray(np.concatenate(parts, 1)), where, rope


OUTS = {"y_prompt": (1, SEQ, D_MODEL), "y_sample": (NB, NT, D_MODEL), "ckv_prompt": (1, 1, SEQ, KL),
        "kpe_prompt": (1, 1, SEQ, ROPE), "ssm_prompt": (1, 1, SH, SP_, SN), "conv_prompt": (1, 1, CW - 1, CONV),
        "ckv_sample": (1, NB, NT, KL), "kpe_sample": (1, NB, NT, ROPE), "ssm_sample": (1, NB, SH, SP_, SN),
        "conv_sample": (1, NB, CW - 1, CONV)}


def build(nc, a, o, stop=99, debug=None):
    sems = {}
    taken = {"yt_full0": ("x_full0", 80), "yt_full1": ("x_full1", 64), "gt_full0": ("st_full", 48),
             "gt_full1": ("rope_full", 32), "tok_stored0": ("x_stored", 32), "tok_stored1": ("prep_full", 48),
             "tok_turned": ("x_turned", 9), "g_hi": ("x_hi", 9), "g_split": ("x_split", 9),
             "affine_ready": ("keys_turned", 9), "scaled": ("keys_out", 9), "centred": ("crow_turned", 6),
             "mean_ready": ("crow_ready", 6), "srow_ready": ("kn_split", 2), "yg_ready": ("qn_split", 3),
             "f_hi": ("cw_ready", 2), "f_split": ("st_turned", 2), "bank_read0": ("vecs_ready", 2),
             "bank_read1": ("qn_hi", 3), "ssq_ready": ("sq_ready", 5), "ssq_used": ("sq_used", 5),
             "res_half": ("x_whole", 8), "res_free0": ("half_done", 8), "res_free1": ("key_turned", 1),
             "yt_free0": ("qn_normed", 3), "yt_free1": ("kn_normed", 2), "gt_free0": ("q_turned", 16),
             "gt_free1": ("v_turned", 16)}

    def sem(name):
        if name in taken:
            return sem(taken[name][0])
        if name not in sems:
            sems[name] = nc.alloc_semaphore(name)
        return sems[name]

    credit = {f"{name}{b}": by for name, by in (("keys_stored", 32), ("q_stored", 16), ("k_stored", 16),
                                                ("v_stored", 16), ("v_free", 1), ("cv_free", 1),
                                                ("so_stored", 16), ("zo_stored", 16),
                                                ("y_out", 1), ("y_stored", 16), ("pre_read", 2),
                                                ("new_out", 1), ("new_stored", 16),
                                                ("s_read", 1), ("o_read", 1), ("pt_read", 1),
                                                ("gr_read", 2))
              for b in range(2)} | {"st_stored": 16, "att_stored": 16, "t_ready0": 1, "scores_read": 1}

    class Counts(dict):

        def __missing__(self, name):
            self[name] = Tally(sem(name))
            self[name].n = taken[name][1] if name in taken else credit.get(name, 0)
            return self[name]

    def scratch(name, shape):
        if debug is not None and name in debug:
            return nc.dram_tensor(name, shape, F32, kind="ExternalOutput").ap()
        return nc.dram_tensor(name, shape, F32, kind="Internal").ap()

    base = -(-nc.sbuf_base // 64) * 64

    class Arena:

        def __init__(self, at):
            self.at = at

        def __call__(self, name, shape, dt=F32):
            size = 2 if dt == BF16 else 4
            n = size * math.prod(shape[1:])
            t = nc.alloc_sbuf_tensor_at(name, list(shape), dt, offset=self.at)
            self.at += -(-n // 64) * 64
            assert self.at <= nc.sbuf_usable_end, (name, self.at)
            return t

    fixed = Arena(base)
    raw = fixed("raw", [P, RAW, UNIT])
    whi = [fixed(f"whi{s}", [P, UNIT], F32R) for s in range(SPLIT)]
    wlo = [fixed(f"wlo{s}", [P, UNIT], F32R) for s in range(SPLIT)]
    table, where, _ = constants()
    cst = fixed("cst", [P, table.shape[1]])
    vecs = fixed("vecs", [P, 96])
    dskip = fixed("dskip", [P, DI // P])
    epsc = fixed("epsc", [P, 4])
    xhi = fixed("xhi", [P, KT, TOK], F32R)
    xlo = fixed("xlo", [P, KT, TOK], F32R)
    floor = fixed.at

    def const(name):
        at, n = where[name]
        return cst[:, at:at + n]

    ident, ones = const("ident"), const("ones")
    V_GATE, V_QN, V_KVN, V_SSM, V_L1G, V_L1B, V_L2G, V_L2B, V_END = 0, 16, 19, 21, 37, 45, 53, 61, 69

    ps = nc.alloc_psum_tensor("ps", [P, 8, 512], F32)

    def out3(b, n=P):
        return ps[0:n, 3 * b:3 * b + 3, 0:CH]

    def thirds(ap):
        return ap.rearrange("p (c n) -> p c n", c=3)

    d_xbc = scratch("d_xbc", [CONV, TOK])
    d_z = scratch("d_z", [DI, TOK])
    d_g = scratch("d_g", [2 * D_MODEL, TOK])
    d_q = scratch("d_q", [HEADS, QH, TOK])
    d_k = scratch("d_k", [HEADS, NOPE, SEQ])
    d_v = scratch("d_v", [HEADS, P, SEQ // P * VH])
    d_kr = scratch("d_kr", [ROPE, TOK])
    d_kvs = scratch("d_kvs", [KL, NS])
    d_small = scratch("d_small", [SH, TOK])
    d_y = scratch("d_y", [DI, TOK])
    d_att = scratch("d_att", [HEADS * VH, TOK])
    d_acum = scratch("d_acum", [SH, TOK])
    d_x = scratch("d_x", [D_MODEL, TOK])

    w_in = a["w_in"][0]
    w_uq, w_ukv = a["w_uq"][0], a["w_ukv"][0]
    w_a, w_b, w_o = a["w_branch_a"][0], a["w_branch_b"][0], a["w_out"][0]
    w_g, w_u, w_d = a["w_ffn_gate"][0], a["w_ffn_up"][0], a["w_ffn_down"][0]

    ar = Arena(floor)
    xst = [ar(f"xst{b}", [P, D_MODEL]) for b in range(2)]
    rows = ar("rows", [V_END, P])
    drow = ar("drow", [DI // P, 2])
    drow2 = ar("drow2", [DI // P, P])
    ar = Arena(floor)
    small = ar("small", [P, TOK])
    cq = ar("cq", [P, 3, TOK])
    ckv = ar("ckv", [P, 2, TOK])
    qn_hi, qn_lo = ar("qn_hi", [P, 3, TOK], F32R), ar("qn_lo", [P, 3, TOK], F32R)
    kn_hi, kn_lo = ar("kn_hi", [P, 2, TOK], F32R), ar("kn_lo", [P, 2, TOK], F32R)
    rope_t = ar("rope_t", [P, 2, TOK])
    sq = ar("sq", [P, 2, TOK])
    rs = ar("rs", [P, 2, TOK])
    tokst = [sq[:, b, 0:KL + ROPE] for b in range(2)]
    qh = [cq[:, 0], cq[:, 1]]
    kvh = [ckv[:, b, 0:SEQ] for b in range(2)]
    vst = [cq[:, 2, b * 512:(b + 1) * 512] for b in range(2)]
    rot = [rs[:, b] for b in range(2)]
    R0, R1 = NOPE, QH

    ar = Arena(floor + 6 * 64 * (-(-TOK * 4 // 64)))
    NCONV = CONV // P
    st = ar("st", [CW + 1 + NB * (CW - 1), CONV])
    cw = ar("cw", [P, NCONV, CW + 1 + NB * (CW - 1)])
    xraw = [ar(f"xraw{b}", [P, CW - 1 + TOK]) for b in range(2)]
    xs7 = [ar(f"xs7{b}", [P, NB, CW - 1 + NT]) for b in range(2)]
    cv = [ar(f"cv{b}", [P, TOK]) for b in range(2)]
    so = [ar(f"so{b}", [P, TOK]) for b in range(2)]
    ccol = ar("ccol", [P, NCONV, (NB + 1) * (CW - 1)])
    crow = ar("crow", [(NB + 1) * (CW - 1), CONV])
    ar = Arena(floor)
    zo = [ar(f"zo{b}", [P, TOK]) for b in range(2)]
    xo = ar("xo", [P, 4, TOK])

    low = floor - 2 * 64 * (-(-KT * TOK * 4 // 64))
    ar = Arena(low)
    dtr = ar("dtr", [SH, TOK])
    act_ = ar("act_", [SH, TOK])
    hb = ar("hb", [P, 2, SH])
    dt_, da, acs, dte, cdb, sp_u, sp_z, sp_w, sp_p = (ar(n, [P, 9, SH]) for n in
        ("dt_", "da", "acs", "dte", "cdb", "sp_u", "sp_z", "sp_w", "sp_p"))
    cdp = ar("cdp", [P, DI // P, NB])
    HG = SH // SG
    s_x = [ar(f"s_x{b}", [P, 4, P]) for b in range(2)]
    s_b = [ar(f"s_b{b}", [P, P]) for b in range(2)]
    s_c = [ar(f"s_c{b}", [P, P]) for b in range(2)]
    s_a = [ar(f"s_a{b}", [P, HG, P]) for b in range(2)]
    s_g = [ar(f"s_g{b}", [P, HG, P]) for b in range(2)]
    s_e = [ar(f"s_e{b}", [P, HG, P]) for b in range(2)]
    s_xd = [ar(f"s_xd{b}", [P, HG, SP_]) for b in range(2)]
    s_xe = [ar(f"s_xe{b}", [P, HG, SP_]) for b in range(2)]
    s_bt = [ar(f"s_bt{b}", [P, P]) for b in range(2)]
    s_cb = [ar(f"s_cb{b}", [P, P]) for b in range(2)]
    s_y = [ar(f"s_y{b}", [P, 4, P]) for b in range(2)]
    state = ar("state", [P, HG, SP_])
    stout = ar("stout", [P, 4, P])
    s_in = [ar(f"s_in{b}", [P, 4, P]) for b in range(2)]
    s_it = [ar(f"s_it{b}", [P, 4, P]) for b in range(2)]
    s_u = [ar(f"s_u{b}", [NS, HG * SP_]) for b in range(2)]
    s_new = [ar(f"s_new{b}", [P, 4, P]) for b in range(2)]

    ar = Arena(low)
    QG = NB * HEADS
    HT = HEADS * NT
    kvb = [ar("kvb0", [P, NPG, KL]), None]
    kpb = [ar("kpb0", [P, NPG, ROPE]), None]
    wkv = ar("wkv", [P, 2, HEADS * P])
    ukt = ar("ukt", [NOPE, HEADS, KL])
    qs = ar("qs", [NOPE, HEADS, NS])
    qps = ar("qps", [ROPE, HEADS, NS])
    qpb = ar("qpb", [ROPE, NB, HT])
    qlat = ar("qlat", [P, 2, NB, HT])
    olat = ar("olat", [P, 2, HEADS, NS])
    kns = ar("kns", [P, 2, NS])
    krs = ar("krs", [ROPE, NS])
    kts = ar("kts", [NS, KL])
    pgi, pgf = ar("pgi", [P, NB], I32), ar("pgf", [P, NB])
    pgx = ar("pgx", [P, NB], mybir.dt.uint32)
    oats = ar("oats", [P, HEADS // 2, NS])
    kvt = [ar(f"kvt{b}", [P, 4, P]) for b in range(2)]
    kpt = [ar(f"kpt{b}", [ROPE, 2, P]) for b in range(2)]
    pb_ = ar("pb_", [P, NPG + 1, HT])
    snew = ar("snew", [P, HT])
    mx_, mb_, ls_, ri_ = (ar(n, [P, HT]) for n in ("mx_", "mb_", "ls_", "ri_"))
    mcol = ar("mcol", [HT, 1])
    mdiag = ar("mdiag", [HT, HT])
    qcur = ar("qcur", [P, 2, HT])
    qpcur = ar("qpcur", [ROPE, HT])
    at_g = ar.at
    kvb[1], kpb[1] = ar("kvb1", [P, NPG, KL]), ar("kpb1", [P, NPG, ROPE])
    ar = Arena(at_g)
    qb = [ar(f"qb{b}", [QH, SEQ]) for b in range(2)]
    kb = [ar(f"kb{b}", [QH, SEQ]) for b in range(2)]
    vb = [ar(f"vb{b}", [P, SEQ // P, VH]) for b in range(2)]
    pr = [ar(f"pr{b}", [P, SEQ]) for b in range(2)]
    ptb = [ar(f"ptb{b}", [P, SEQ]) for b in range(2)]
    ob = ar("ob", [P, SEQ // P, 2 * VH])
    att = ar("att", [P, SEQ])
    rowmax, negmax, rowsum, rowinv = (ar(n, [P, 16]) for n in ("rowmax", "negmax", "rowsum", "rowinv"))
    ident_b, after_b = ar("ident_b", [P, P], BF16), ar("after_b", [P, P], BF16)
    NQ = SEQ // P
    ar = Arena(low)
    ahi, alo = ar("ahi", [P, KT, TOK], F32R), ar("alo", [P, KT, TOK], F32R)
    mm = ar("mm", [P, KT, TOK])
    srow, sq2, murow, rsrow = ar("srow", [P, TOK]), ar("sq2", [P, 2, TOK]), ar("murow", [P, TOK]), ar("rsrow", [P, TOK])
    at_j = ar.at
    yt = [ar(f"yt{b}", [P, TOK]) for b in range(2)]
    gt = [ar(f"gt{b}", [P, TOK]) for b in range(2)]
    yz = ar("yz", [P, 4, TOK])
    ar = Arena(at_j)
    fhi, flo = ar("fhi", [P, 4, TOK], F32R), ar("flo", [P, 4, TOK], F32R)
    sq4 = [sq2[:, 0], sq2[:, 1], srow[:, :], murow[:, :]]
    fg = [sq2[:, 0], sq2[:, 1]]
    ff = [srow, rsrow]
    ytok = [Arena(low + b * 4096)(f"ytok{b}", [P, D_MODEL]) for b in range(2)]
    NF = FF // 256

    block = nc.Block()
    o_ckv = [o["ckv_prompt"][0, 0], o["ckv_sample"][0].rearrange("b t c -> (b t) c")]
    o_kpe = [o["kpe_prompt"][0, 0], o["kpe_sample"][0].rearrange("b t c -> (b t) c")]

    ctx = ExitStack()
    ctx.enter_context(block)

    @block.sync
    def _(sp):
        k = Counts()
        for name, by in credit.items():
            sp.sem_inc(sem(name), by)
        sp.dma_start(cst[:, :], a["table"]).then_inc(sem("cst_full"), 16)
        for name, at, n in (("b_gate", V_GATE, 16), ("q_norm_g", V_QN, 3), ("kv_norm_g", V_KVN, 2),
                            ("ssm_norm_g", V_SSM, 16), ("ln1_g", V_L1G, 8), ("ln1_b", V_L1B, 8),
                            ("ln2_g", V_L2G, 8), ("ln2_b", V_L2B, 8)):
            sp.dma_start(rows[at:at + n, :], a[name][0].rearrange("(n p) -> n p", p=P)).then_inc(sem("rows_full"), 16)
        sp.dma_start(drow[:, :], a["d_skip"][0].rearrange("(n p) -> n p", p=2)).then_inc(sem("rows_full"), 16)

        unit = [0]

        def weights(pieces):
            s = unit[0] % RAW
            if unit[0] >= RAW:
                sp.wait_ge(sem("unit_split"), k["unit_split"].next())
            for view, src in pieces:
                sp.dma_start(view(raw[:, s]), src).then_inc(sem(f"raw_full{s}"), k[f"raw_full{s}"].adds(16))
            unit[0] += 1

        def columns(n):
            return lambda r: r.rearrange("p (k n) -> p k n", n=n)

        def tile_of(w, col, n=P):
            return w[:, bass.ds(col, n)].rearrange("(k p) n -> p k n", p=P)

        def x_tile(i, b, rows_=P, src=None):
            sp.dma_start(xst[b][0:rows_, :], src).then_inc(sem(f"x_full{b}"), k[f"x_full{b}"].adds(16))

        xp = a["x_prompt"][0]
        x_tile(0, 0, src=xp[0:P, :])
        x_tile(1, 1, src=xp[P:2 * P, :])

        def small_unit():
            def part(j):
                return lambda r: r.rearrange("p (k n) -> p k n", n=P)[:, :, 32 * j:32 * j + 32]
            weights([(part(0), tile_of(w_in, C_DT, 32)), (part(1), tile_of(w_in, C_DT, 32)),
                     (part(2), tile_of(w_in, C_PE, 32)), (part(3), tile_of(w_in, C_PE, 32))])

        small_unit()
        for j in range(3):
            weights([(columns(P), tile_of(w_in, C_Q + j * P))])
        with looped(sp, 3, {k["x_turned"]: 2, k["x_full0"]: 16, k["x_full1"]: 16}) as i:
            for b in range(2):
                sp.wait_ge(sem("x_turned"), k["x_turned"].next())
                x_tile(0, b, src=xp[bass.ds((i * 2 + 2 + b) * P, P), :])
        sp.wait_ge(sem("x_turned"), k["x_turned"].next())
        x_tile(8, 0, NS, a["x_sample"].rearrange("b t d -> (b t) d"))

        for j in range(2):
            weights([(columns(P), tile_of(w_in, C_KV + j * P))])
        for j in range(2):
            sp.dma_start(rope_t[R0:R1, j, :], a["rope"][j, R0:R1, :]).then_inc(sem("rope_full"), k["rope_full"].adds(16))
        with looped(sp, 2, {k["unit_split"]: 4} | {k[f"raw_full{s}"]: 16 for s in range(RAW)}) as i:
            for j in range(4):
                weights([(lambda r: r[:, 0:3 * 2 * QH].rearrange("p (k n) -> p k n", k=3),
                          tile_of(w_uq, (i * 4 + j) * 2 * QH, 2 * QH))])
        unit[0] += 4
        for j in range(4):
            weights([(columns(512), tile_of(w_ukv, j * 512, 512))])
        if stop < 3:
            return
        sp.wait_ge(sem("unit_done"), 14)
        sp.dma_start(st[0:CW, :], a["conv_w"][0]).then_inc(sem("st_full"), 16)
        sp.dma_start(st[CW:CW + 1, :], a["conv_b"]).then_inc(sem("st_full"), 16)
        sp.dma_start(st[CW + 1:, :], a["state_conv"][0].rearrange("b t c -> (b t) c")).then_inc(sem("st_full"), 16)
        all_raw = {k["unit_split"]: 4} | {k[f"raw_full{s}"]: 16 for s in range(RAW)}
        for col, n in ((C_XBC, CONV), (C_Z, DI), (C_G, 2 * D_MODEL)):
            with looped(sp, n // P // 4, all_raw) as i:
                for j in range(4):
                    weights([(columns(P), tile_of(w_in, (i * 4 + j) * P + col))])
            unit[0] += n // P - 4
        if stop < 4:
            return

        sp.wait_ge(sem("unit_done"), 74)
        for b in range(2):
            sp.wait_ge(sem(f"zo_stored{b}"), 17 * 16)
        sp.dma_start(dtr[:, :], d_small).then_inc(sem("prep_full"), k["prep_full"].adds(16))
        sp.dma_start(hb[:, 0], a["dt_bias"][0].partition_broadcast(P)).then_inc(sem("prep_full"), k["prep_full"].adds(16))
        sp.dma_start(hb[:, 1], a["a_log"][0].partition_broadcast(P)).then_inc(sem("prep_full"), k["prep_full"].adds(16))
        sp.wait_ge(sem("so_stored0"), 13 * 16)
        sp.wait_ge(sem("so_stored1"), 13 * 16)
        sp.wait_ge(sem("acum_stored"), 16)
        sp.wait_ge(sem("x_stored"), 32)

        def step(b, g, at, n=P):
            sp.wait_ge(sem(f"y_out{b}"), k[f"y_out{b}"].held())
            for dst, src in ((s_x[b][:, :, 0:n], d_xbc[bass.ds(g * 512, 512), bass.ds(at, n)].rearrange("(j p) n -> p j n", p=P)),
                             (s_b[b][:, 0:n], d_xbc[bass.ds(g * P + DI, P), bass.ds(at, n)]),
                             (s_c[b][:, 0:n], d_xbc[bass.ds(g * P + DI + SG * SN, P), bass.ds(at, n)]),
                             (s_a[b][:, :, 0:n], d_acum[bass.ds(g * HG, HG), bass.ds(at, n)].partition_broadcast(P))):
                sp.dma_start(dst, src).then_inc(sem(f"step_full{b}"), k[f"step_full{b}"].adds(16))

        with looped(sp, SG, {k[f"{n}{b}"]: by + (b == 0) * more for b in range(2)
                             for n, by, more in (("y_out", 4, 1), ("step_full", 256, 64), ("new_out", 4, 0), ("si_full", 64, 0))}) as g:
            with looped(sp, 4, {k[f"{n}{b}"]: by for b in range(2) for n, by in (("y_out", 1), ("step_full", 64))}) as c:
                for b in range(2):
                    step(b, g, (c * 2 + b) * P)
            step(0, g, SEQ, NS)
            for q in range(NB):
                sp.wait_ge(sem(f"new_out{q % 2}"), k[f"new_out{q % 2}"].held())
                src = a["state_ssm"][0, q].rearrange("h p n -> (h p) n")
                sp.dma_start(s_in[q % 2][:, :, :], src[bass.ds(g * 512, 512), :].rearrange("(j p) n -> p j n", p=P)).then_inc(sem(f"si_full{q % 2}"), k[f"si_full{q % 2}"].adds(16))
        if stop < 5:
            return

        sp.wait_ge(sem("ssm_over"), 1)
        for b in range(2):
            sp.dma_start(kb[b][NOPE:QH, :], d_kr[:, 0:SEQ]).then_inc(sem("kr_full"), k["kr_full"].adds(16))

        def head(b, h):
            one = lambda d: d[bass.ds(h, 1)].rearrange("a p n -> (a p) n")
            sp.dma_start(qb[b][:, :], one(d_q)[:, 0:SEQ]).then_inc(sem(f"head_full{b}"), k[f"head_full{b}"].adds(16))
            sp.dma_start(kb[b][0:NOPE, :], one(d_k)).then_inc(sem(f"head_full{b}"), k[f"head_full{b}"].adds(16))
            sp.dma_start(vb[b][:, :, :].rearrange("p a n -> p (a n)"), one(d_v)).then_inc(sem(f"head_full{b}"), k[f"head_full{b}"].adds(16))

        head(0, 0)
        head(1, 1)
        with nc.allow_non_contiguous_dma(reason="a page number for each quarter page, 4 KB in all"):
            for q in range(NB):
                src = a["page_table"][q].unsqueeze(1).broadcast_to([NPG, P // NPG])
                sp.dma_start(pgi[:, q:q + 1], src).then_inc(sem("pages_full"), k["pages_full"].adds(16))
            for dst, src in ((wkv[:, :, :], w_ukv.rearrange("(k p) n -> p k n", p=P)),
                             (qs[:, :, :], d_q[:, 0:NOPE, SEQ:TOK].rearrange("h p n -> p h n")),
                             (qps[:, :, :], d_q[:, NOPE:QH, SEQ:TOK].rearrange("h p n -> p h n")),
                             (kns[:, :, :], d_kvs.rearrange("(k p) n -> p k n", p=P)),
                             (krs[:, :], d_kr[:, SEQ:TOK]), (kts[:, :], o_ckv[1])):
                sp.dma_start(dst, src).then_inc(sem("late_full"), k["late_full"].adds(16))
        with looped(sp, HEADS // 2 - 1, {k["o_ready"]: 16} | pairs(k, {"head_full": 48})) as i:
            for b in range(2):
                sp.wait_ge(sem("o_ready"), k["o_ready"].next(NQ))
                head(b, i * 2 + 2 + b)
        if stop < 7:
            return

        to_load = []

        def row_units(w, row, rows_, cols):
            return [[(columns(cols), w[bass.ds(row, rows_), c:c + cols].rearrange("(k p) n -> p k n", p=P))]
                    for c in range(0, D_MODEL, cols)]

        def gate_up(blk):
            return [[(columns(P), tile_of(w, blk * 256 + j * P))] for j in range(2) for w in (w_g, w_u)]

        def next_weights(n):
            for _ in range(n):
                weights(to_load.pop(0))

        for g in range(4):
            to_load += row_units(w_b, g * 512, 512, 256)
        for g in range(2):
            to_load += row_units(w_a, g * 512, 512, 256)
        to_load += [[(columns(P), tile_of(w_o, e * P))] for e in range(KT)] + gate_up(0)
        next_weights(4)
        sp.wait_ge(sem("samples_over"), 1)

        def load_tile(name, buffer, j, src):
            sp.wait_ge(sem(f"{name}_free{j % 2}"), k[f"{name}_free{j % 2}"].held())
            sp.dma_start(buffer[j % 2][:, :], src).then_inc(sem(f"{name}_full{j % 2}"), k[f"{name}_full{j % 2}"].adds(16))

        def y_and_z(g):
            for j in range(4):
                at = slice((g * 4 + j) * P, (g * 4 + j + 1) * P)
                load_tile("yt", yt, j, d_y[at, :])
                sp.dma_start(gt[j % 2][:, :], d_z[at, :]).then_inc(sem(f"yt_full{j % 2}"), k[f"yt_full{j % 2}"].adds(16))

        def att_tile(g, j):
            load_tile("yt", yt, j, d_att[(g * 4 + j) * P:(g * 4 + j + 1) * P, :])

        def features(d, row, units, att_g=None):
            for e in range(0, KT, 2):
                if att_g is not None and e in (0, 4):
                    for j in range(2):
                        att_tile(att_g, e // 2 + j)
                for j in range(2):
                    load_tile("gt", gt, j, d[row + (e + j) * P:row + (e + j + 1) * P, :])
                next_weights(units)

        y_and_z(0)
        for g in range(1, 4):
            y_and_z(g)
            next_weights(4)
        for b in range(2):
            sp.wait_ge(sem(f"yt_free{b}"), k[f"yt_free{b}"].same())
        features(d_g, D_MODEL, 1, 0)
        features(d_g, 0, 1, 1)
        features(d_g, 0, 1)
        features(d_x, 0, 2)

        with looped(sp, (NF - 1) // 2, {k["unit_split"]: 12} | {k[f"raw_full{s}"]: 48 for s in range(RAW)}) as i:
            for v in range(2):
                to_load += gate_up(i * 2 + v + 1) + row_units(w_d, (i * 2 + v) * 256, 256, 512)
                next_weights(6)
        unit[0] += 12 * ((NF - 1) // 2 - 1)
        to_load += row_units(w_d, (NF - 1) * 256, 256, 512)
        next_weights(2)

    @block.gpsimd
    def _(pool):
        k = Counts()
        pool.memset(epsc[:, 0:1], 1e-6)
        pool.memset(epsc[:, 1:2], 1e-5).then_inc(sem("eps_ready"), 1)
        pool.wait_ge(sem("cst_full"), 16)

        def split(u, s, first=False):
            pool.wait_ge(sem(f"raw_full{u}"), k[f"raw_full{u}"].next(16 * (4 if first else 1)))
            if k["unit_split"].n >= SPLIT or k["unit_split"].loops:
                pool.wait_ge(sem("unit_done"), k["unit_done"].next())
            pool.tensor_tensor(whi[s][:, :], raw[:, u], ones[:, 0:1].broadcast_to([P, UNIT]), ALU.mult).then_inc(sem("unit_hi"), k["unit_hi"].adds(1))
            pool.wait_ge(sem("unit_hi"), k["unit_hi"].same())
            pool.tensor_tensor(wlo[s][:, :], raw[:, u], whi[s][:, :].bitcast(F32), ALU.subtract).then_inc(sem("unit_split"), k["unit_split"].adds(1))

        split(0, 0, True)
        for u in range(1, 4):
            split(u % RAW, u % SPLIT)

        def split_units(first, end):
            turns, rest = divmod(end - first, RAW)
            if turns:
                with looped(pool, turns, {k["unit_split"]: 4, k["unit_hi"]: 4, k["unit_done"]: 4} |
                            {k[f"raw_full{s}"]: 16 for s in range(RAW)}):
                    for u in range(first, first + RAW):
                        split(u % RAW, u % SPLIT)
            for u in range(end - rest, end):
                split(u % RAW, u % SPLIT)

        split_units(4, UNITS.get(stop, 74))
        if stop < 5:
            return
        pool.wait_ge(sem("index_ready"), k["index_ready"].next())

        def cached(b, col):
            if b == 1:
                pool.wait_ge(sem("prompt_over"), 1)
            for dst, src in ((kvb[b], a["cache_ckv"][0]), (kpb[b], a["cache_kpe"][0])):
                pool.indirect_dma_start(
                    out=dst[:, :, :].rearrange("p r c -> p (r c)"), out_offset=None,
                    in_=src.rearrange("n (j r) c -> (n j) (r c)", j=4),
                    in_offset=bass.IndirectOffsetOnAxis(ap=col, axis=0)).then_inc(sem(f"kv_full{b}"), k[f"kv_full{b}"].adds(16))

        for q in range(NB):
            if q >= 2:
                pool.wait_ge(sem("olat_read"), k["olat_read"].next())
            cached(q % 2, pgx[:, q:q + 1])
        if stop >= 7:
            split_units(74, TOTAL_UNITS)

    @block.tensor
    def _(pe):
        k = Counts()
        pe.wait_ge(sem("cst_full"), 16)

        def transposes(b, n):
            for j in range(KT):
                at = ps[:, 2 * b + j // 4, (j % 4) * n:(j % 4) * n + n] if n == P else ps[:, 2 * b, j * n:j * n + n]
                last = pe.transpose(at, xst[b][0:n, j * P:(j + 1) * P], ident[0:n, 0:n])
            last.then_inc(sem("x_turned"), k["x_turned"].adds(1))

        for b in range(2):
            pe.wait_ge(sem(f"x_full{b}"), k[f"x_full{b}"].next(16))
            transposes(b, P)
        with looped(pe, 3, {k["x_full0"]: 16, k["x_full1"]: 16, k["x_split"]: 2, k["x_turned"]: 2}):
            for b in range(2):
                pe.wait_ge(sem(f"x_full{b}"), k[f"x_full{b}"].next(16))
                pe.wait_ge(sem("x_split"), k["x_split"].next())
                transposes(b, P)
        pe.wait_ge(sem("x_full0"), k["x_full0"].next(16))
        pe.wait_ge(sem("x_split"), k["x_split"].next())
        transposes(0, NS)
        pe.wait_ge(sem("rows_full"), 16 * 9)
        pe.transpose(ps[:, 6, 0:V_END], rows[:, :], ident[0:V_END, 0:V_END])
        pe.wait_ge(sem("drow_wide"), 1)
        pe.transpose(ps[:, 6, 128:144], drow2[:, :], ident[0:16, 0:16]).then_inc(sem("vecs_turned"), 1)
        pe.wait_ge(sem("x_split"), k["x_split"].next(2))

        out_free = ["out_free"]

        def products(b, hi, lo, xh, xl, kt, chunks, m=P):
            n = 3 * kt
            for i in range(n):
                j, part = i // 3, i % 3
                w, x = ((hi, xh), (hi, xl), (lo, xh))[part]
                for c, (at, width) in enumerate(chunks):
                    last = pe.matmul(ps[0:m, 3 * b + c, 0:width], w(j), x[:, j, at:at + width],
                                     start=i == 0, stop=i == n - 1)
            return last

        all_tokens = [(c * CH, CH) for c in range(3)]

        def dense(u, b, xh, xl, kt, wait_free=True):
            pe.wait_ge(sem("unit_split"), k["unit_split"].next())
            if wait_free:
                pe.wait_ge(sem(f"{out_free[0]}{b}"), k[f"{out_free[0]}{b}"].next())
            s = u % SPLIT
            view = lambda t: lambda j: t[:, j * P:(j + 1) * P]
            products(b, view(whi[s]), view(wlo[s]), xh, xl, kt, all_tokens).then_inc(sem("unit_done"), k["unit_done"].adds(1))

        for u in range(6):
            dense(u, u % 2, xhi, xlo, KT, wait_free=u >= 2)
        if stop < 2:
            return

        def sum_rows(b, n):
            pe.wait_ge(sem(f"out_free{b}"), k[f"out_free{b}"].next())
            for i in range(n):
                pe.wait_ge(sem("sq_ready"), k["sq_ready"].next())
                for c, (at, width) in enumerate(all_tokens):
                    last = pe.matmul(ps[:, 3 * b + c, 0:width], ones, sq[:, k["sq_ready"].n % 2 ^ 1, at:at + width],
                                     start=i == 0, stop=i == n - 1)
                last.then_inc(sem("sq_used"), k["sq_used"].adds(1))

        def turn(b, src):
            for c, (at, width) in enumerate(all_tokens):
                last = pe.matmul(ps[R0:R1, 3 * b + c, 0:width], const("turn")[0:R1, :], src[0:R1, at:at + width],
                                 start=True, stop=True)
            last.then_inc(sem("rot_ready"), k["rot_ready"].adds(1))

        sum_rows(0, 3)
        sum_rows(1, 2)
        pe.wait_ge(sem("out_free0"), k["out_free0"].next())
        turn(0, small)
        pe.wait_ge(sem("kn_split"), k["kn_split"].next(2))
        pe.wait_ge(sem("key_turned"), k["key_turned"].next(1))
        for i in range(9):
            n = P if i < 8 else NS
            if i >= 2:
                pe.wait_ge(sem("keys_out"), k["keys_out"].next())
            for j in range(2):
                pe.transpose(ps[0:n, 6 + i % 2, j * P:(j + 1) * P], ckv[:, j, i * P:i * P + n], ident[:, :])
            last = pe.transpose(ps[0:n, 6 + i % 2, KL:KL + ROPE], small[R0:R1, i * P:i * P + n], ident[R0:R1, R0:R1])
            last.then_inc(sem("keys_turned"), k["keys_turned"].adds(1))

        def query_pair(s, first=False):
            pe.wait_ge(sem("unit_split"), k["unit_split"].next())
            for b in range(2):
                pe.wait_ge(sem(f"out_free{b}"), k[f"out_free{b}"].next())
                view = lambda t: lambda j: t[:, j * 2 * QH + b * QH:j * 2 * QH + (b + 1) * QH]
                last = products(b, view(whi[s]), view(wlo[s]), qn_hi, qn_lo, 3, all_tokens, QH)
                last.then_inc(sem("half_done" if b == 0 else "unit_done"), k["half_done" if b == 0 else "unit_done"].adds(1))
            for b in range(2):
                pe.wait_ge(sem(f"out_free{b}"), k[f"out_free{b}"].next())
                turn(b, qh[b])

        pe.wait_ge(sem("qn_split"), k["qn_split"].next(3))
        pe.wait_ge(sem("keys_out"), k["keys_out"].next(2))
        with looped(pe, 4, {k["unit_split"]: 2, k["unit_done"]: 2, k["half_done"]: 2, k["out_free0"]: 4,
                            k["out_free1"]: 4, k["rot_ready"]: 4}):
            for s in range(2):
                query_pair(s)

        def turn_values(b):
            pe.wait_ge(sem(f"v_free{b}"), k[f"v_free{b}"].held())
            for j in range(SEQ // P):
                last = pe.matmul(ps[:, 6 + b, j * VH:(j + 1) * VH], kvh[b][:, j * P:(j + 1) * P], ident[:, NOPE:P],
                                 start=True, stop=True)
            last.then_inc(sem("v_turned"), k["v_turned"].adds(1))

        with looped(pe, 2, {k["unit_split"]: 2, k["unit_done"]: 2, k["sub_done"]: 6, k["out_free0"]: 4,
                            k["out_free1"]: 4, k["v_turned"]: 8, k["v_free0"]: 4, k["v_free1"]: 4}):
            for s in range(2):
                pe.wait_ge(sem("unit_split"), k["unit_split"].next())
                for h in range(4):
                    b = h % 2
                    pe.wait_ge(sem(f"out_free{b}"), k[f"out_free{b}"].next())
                    view = lambda t: lambda j: t[:, j * 512 + h * P:j * 512 + (h + 1) * P]
                    last = products(b, view(whi[s]), view(wlo[s]), kn_hi, kn_lo, 2, [(0, 512), (512, 512)])
                    last.then_inc(sem("sub_done" if h < 3 else "unit_done"), k["sub_done" if h < 3 else "unit_done"].adds(1))
                    if h % 2:
                        for v in range(2):
                            pe.wait_ge(sem(f"out_free{v}"), k[f"out_free{v}"].ahead())
                            turn_values(v)
        if stop < 3:
            return

        pe.wait_ge(sem("st_full"), 48)
        for v in range(2):
            pe.wait_ge(sem(f"v_free{v}"), k[f"v_free{v}"].same())
            for j in range(NCONV // 2):
                n = CW + 1 + NB * (CW - 1)
                last = pe.transpose(ps[:, 6 + v, j * n:(j + 1) * n], st[:, (v * 12 + j) * P:(v * 12 + j + 1) * P],
                                    ident[0:n, 0:n])
            last.then_inc(sem("st_turned"), k["st_turned"].adds(1))

        def dense_fours(n, xh, xl):
            with looped(pe, n, {k["unit_split"]: 4, k["unit_done"]: 4, k[out_free[0] + "0"]: 2, k[out_free[0] + "1"]: 2}):
                for u in range(4):
                    dense(u, u % 2, xh, xl, KT)

        dense_fours(NCONV // 4, xhi, xlo)
        dense_fours(4, xhi, xlo)
        pe.wait_ge(sem("cw_ready"), k["cw_ready"].next(2))
        pe.wait_ge(sem("conv_done1"), k["conv_done1"].next(NCONV // 2))
        n = (NB + 1) * (CW - 1)
        for i in range(6):
            if i >= 2:
                pe.wait_ge(sem("crow_ready"), k["crow_ready"].next())
            for j in range(4):
                last = pe.transpose(ps[0:n, 6 + i % 2, j * P:(j + 1) * P], ccol[:, i * 4 + j, :], ident)
            last.then_inc(sem("crow_turned"), k["crow_turned"].adds(1))
        dense_fours(4, xhi, xlo)
        if stop < 4:
            return

        pe.wait_ge(sem("prep_full"), k["prep_full"].next(48))
        pe.wait_ge(sem("crow_ready"), k["crow_ready"].next(2))
        for b in range(2):
            pe.wait_ge(sem(f"out_free{b}"), k[f"out_free{b}"].next())
        for i in range(9):
            n = P if i < 8 else NS
            last = pe.transpose(ps[0:n, 6, i * SH:(i + 1) * SH], dtr[:, i * P:i * P + n], ident[0:SH, 0:SH])
        last.then_inc(sem("dt_turned"), k["dt_turned"].adds(1))
        pe.wait_ge(sem("da_ready"), k["da_ready"].next())
        flat = lambda t: t[:, 0:8, :].rearrange("p a b -> p (a b)")
        pe.matmul(ps[:, 0, 0:256], const("causal"), flat(da), start=True, stop=True)
        pe.matmul(ps[0:NS, 0, 256:288], const("causal_s")[0:NS], da[0:NS, 8], start=True, stop=True)
        pe.matmul(ps[:, 1, 0:256], ones, flat(da), start=True, stop=True)
        pe.matmul(ps[0:NS, 1, 256:288], const("same_s")[0:NS], da[0:NS, 8], start=True, stop=True)
        for i in range(8):
            pe.matmul(ps[0:SH, 2 + i // 4, i % 4 * P:(i % 4 + 1) * P], da[:, i, :], const("causal"), start=True, stop=True)
        last = pe.matmul(ps[0:SH, 4, 0:NS], da[0:NS, 8, :], const("causal_s")[0:NS], start=True, stop=True)
        last.then_inc(sem("sums_ready"), k["sums_ready"].adds(1))
        pe.wait_ge(sem("act_ready"), k["act_ready"].next())
        spread = const("spread")
        for j in range(DI // P):
            last = pe.matmul(ps[:, 5, j * NS:(j + 1) * NS], spread[0:SH, j * P:(j + 1) * P], act_[:, SEQ:TOK],
                             start=True, stop=True)
        last.then_inc(sem("rows_ready"), k["rows_ready"].adds(1))
        pe.wait_ge(sem("prep_read"), k["prep_read"].next(3))

        def ssm_pre(b, n=P):
            pe.wait_ge(sem(f"step_full{b}"), k[f"step_full{b}"].next(64))
            pe.wait_ge(sem(f"pre_read{b}"), k[f"pre_read{b}"].held(2))
            for j in range(4):
                pe.transpose(ps[0:n, 2 * b, j * P:(j + 1) * P], s_x[b][:, j, 0:n], ident)
            pe.transpose(ps[0:n, 2 * b + 1, 0:P], s_b[b][:, 0:n], ident)
            pe.matmul(ps[0:n, 2 * b + 1, P:P + n], s_b[b][:, 0:n], s_c[b][:, 0:n], start=True, stop=True).then_inc(sem("pre_ready"), k["pre_ready"].adds(1))

        def ssm_main(b):
            pe.wait_ge(sem("g_ready"), k["g_ready"].next())
            pe.wait_ge(sem(f"y_out{b}"), k[f"y_out{b}"].held())
            pe.wait_ge(sem("state_ready"), k["state_ready"].next())
            for h in range(HG):
                r = 64 * (h % 2)
                out = ps[r:r + 64, 4 + b, h // 2 * P:(h // 2 + 1) * P]
                pe.matmul(out, s_xd[b][:, h], s_g[b][:, h], start=True, stop=False)
                last = pe.matmul(out, state[:, h], s_e[b][:, h], start=False, stop=True)
            last.then_inc(sem("y_ready"), k["y_ready"].adds(1))
            pe.matmul(ps[:, 6, :], s_bt[b][:, :], s_xe[b][:, :].rearrange("p h q -> p (h q)"), start=True, stop=True).then_inc(sem("prod_ready"), k["prod_ready"].adds(1))

        def ssm_samples():
            pe.wait_ge(sem("g_ready"), k["g_ready"].next())
            pe.wait_ge(sem("y_out0"), k["y_out0"].held())
            for h in range(HG):
                r = 64 * (h % 2)
                pe.matmul(ps[r:r + 64, 4, h // 2 * NS:(h // 2 + 1) * NS], s_xd[0][0:NS, h], s_g[0][0:NS, h, 0:NS],
                          start=h < 2, stop=False, skip_group_check=True)
            for q in range(NB + 1):
                if q < NB:
                    b = q % 2
                    pe.wait_ge(sem(f"si_full{b}"), k[f"si_full{b}"].next(16))
                    for j in range(4):
                        last = pe.transpose(ps[:, 2 + b, j * P:(j + 1) * P], s_in[b][:, j], ident)
                    last.then_inc(sem(f"it_turned"), k[f"it_turned"].adds(1))
                if q:
                    b = (q - 1) % 2
                    pe.wait_ge(sem(f"it_ready{b}"), k[f"it_ready{b}"].next())
                    for h in range(HG):
                        r = 64 * (h % 2)
                        c = h // 2 * NS + (q - 1) * NT
                        last = pe.matmul(ps[r:r + 64, 4, c:c + NT], s_it[b][:, h // 2, r:r + 64], s_e[0][:, h, (q - 1) * NT:q * NT],
                                         start=False, stop=h == HG - 1, skip_group_check=True)
                    last.then_inc(sem("off_done"), k["off_done"].adds(1))
                    pe.wait_ge(sem("u_ready"), k["u_ready"].next())
                    pe.wait_ge(sem(f"new_out{b}"), k[f"new_out{b}"].held())
                    for j in range(4):
                        last = pe.matmul(ps[:, 6 + b, j * P:(j + 1) * P], s_u[b][:, j * P:(j + 1) * P], s_bt[0][0:NS, :],
                                         start=True, stop=True)
                    last.then_inc(sem("upd_ready"), k["upd_ready"].adds(1))

        two = lambda d: pairs(k, d)
        per_g = ({k["pre_ready"]: 9, k["g_ready"]: 9, k["state_ready"]: 9, k["y_ready"]: 8, k["prod_ready"]: 8,
                  k["it_turned"]: 8, k["off_done"]: 8, k["u_ready"]: 8, k["upd_ready"]: 8,
                  k["end_turned"]: 1, k["step_full0"]: 5 * 64, k["step_full1"]: 4 * 64,
                  k["pre_read0"]: 10, k["pre_read1"]: 8, k["y_out0"]: 5, k["y_out1"]: 4} |
                 two({"si_full": 64, "it_ready": 4, "new_out": 4}))
        per_c = {k["pre_ready"]: 2, k["g_ready"]: 2, k["state_ready"]: 2, k["y_ready"]: 2, k["prod_ready"]: 2} | two({"step_full": 64, "pre_read": 2, "y_out": 1})
        with looped(pe, SG, per_g):
            ssm_pre(0)
            with looped(pe, 3, per_c):
                ssm_pre(1)
                ssm_main(0)
                ssm_pre(0)
                ssm_main(1)
            ssm_pre(1)
            ssm_main(0)
            ssm_pre(0, NS)
            ssm_main(1)
            pe.wait_ge(sem("state_ready"), k["state_ready"].next())
            for j in range(4):
                last = pe.transpose(ps[:, 7, j * P:(j + 1) * P], state[:, 2 * j:2 * j + 2].rearrange("p h q -> p (h q)"), ident)
            last.then_inc(sem("end_turned"), k["end_turned"].adds(1))
            ssm_samples()
        if stop < 5:
            return

        pe.wait_ge(sem("kr_full"), k["kr_full"].next(32))
        pe.wait_ge(sem("bf_ready"), k["bf_ready"].next(2))

        def scores(n):
            b, q = n // NQ, n % NQ
            if q == 0:
                pe.wait_ge(sem(f"head_full{b}"), k[f"head_full{b}"].next(48))
            pe.wait_ge(sem(f"s_read{n % 2}"), k[f"s_read{n % 2}"].held())
            length = (q + 1) * P
            for c in range(0, length, 512):
                w = min(512, length - c)
                pe.matmul(ps[:, 2 * (n % 2) + c // 512, 0:w], qb[b][:, q * P:(q + 1) * P], kb[b][:, c:c + w], start=True, stop=True)
            at = q * P
            last = pe.matmul(ps[:, 2 * (n % 2) + at // 512, at % 512:at % 512 + P], ident_b[:, :], after_b[:, :], start=False, stop=True,
                             skip_group_check=True)
            last.then_inc(sem("s_ready"), k["s_ready"].adds(1))

        def turn_probs(n):
            q = n % NQ
            pe.wait_ge(sem(f"s_read{n % 2}"), k[f"s_read{n % 2}"].same())
            for part in range(1 + (q >= 4)):
                pe.wait_ge(sem(f"pt_read{part}"), k[f"pt_read{part}"].held())
                for j in range(part * 4, min(q + 1, part * 4 + 4)):
                    last = pe.transpose(ps[:, 4 + part, j % 4 * P:(j % 4 + 1) * P], pr[n % 2][:, j * P:(j + 1) * P], ident)
                last.then_inc(sem(f"t_ready{part}"), k[f"t_ready{part}"].adds(1))

        def weigh(n):
            b, q = n // NQ, n % NQ
            for part in range(1 + (q >= 4)):
                pe.wait_ge(sem(f"pt_read{part}"), k[f"pt_read{part}"].same())
            pe.wait_ge(sem(f"o_read{n % 2}"), k[f"o_read{n % 2}"].held())
            for j in range(q + 1):
                last = pe.matmul(ps[:, 6 + n % 2, 0:VH], ptb[n % 2][:, j * P:(j + 1) * P], vb[b][:, j], start=j == 0, stop=j == q)
            last.then_inc(sem("o_ready"), k["o_ready"].adds(1))

        def attention_pair(final):
            for n in range(16):
                if n < 15:
                    scores(n + 1)
                elif not final:
                    scores(0)
                if n:
                    weigh(n - 1)
                turn_probs(n)
            weigh(15)
            for b in range(2):
                pe.wait_ge(sem(f"o_read{b}"), k[f"o_read{b}"].same())
            for part in range(2):
                pe.wait_ge(sem(f"pt_read{part}"), k[f"pt_read{part}"].held())
                for j in range(4):
                    last = pe.transpose(ps[:, 4 + part, j * P:(j + 1) * P], ob[:, part * 4 + j, :], ident)
                last.then_inc(sem(f"t_ready{part}"), k[f"t_ready{part}"].adds(1))

        g_per = {k["s_ready"]: 16, k["o_ready"]: 16, k["pt_read0"]: 17, k["t_ready0"]: 17,
                 k["pt_read1"]: 9, k["t_ready1"]: 9} | pairs(k, {"head_full": 48, "s_read": 8, "o_read": 8})
        scores(0)
        with looped(pe, HEADS // 2 - 1, g_per):
            attention_pair(False)
        attention_pair(True)
        if stop < 6:
            return

        pe.wait_ge(sem("late_full"), k["late_full"].next(96))
        for b in range(2):
            pe.wait_ge(sem(f"s_read{b}"), k[f"s_read{b}"].same())
            pe.wait_ge(sem(f"pt_read{b}"), k[f"pt_read{b}"].same())
            pe.wait_ge(sem(f"o_read{b}"), k[f"o_read{b}"].same())
        for h in range(HEADS):
            for j in range(2):
                last = pe.transpose(ps[0:NOPE, h // 2, (h % 2 * 2 + j) * P:(h % 2 * 2 + j + 1) * P],
                                    wkv[:, j, h * P:h * P + NOPE], ident)
            if h % 2:
                last.then_inc(sem("uk_turned"), k["uk_turned"].adds(1))
        pe.wait_ge(sem("uk_ready"), k["uk_ready"].next(8))
        for j in range(2):
            for h in range(HEADS):
                last = pe.matmul(ps[:, j, h * NS:(h + 1) * NS], ukt[:, h, j * P:(j + 1) * P], qs[:, h, :], start=True, stop=True)
        last.then_inc(sem("lat_ready"), k["lat_ready"].adds(1))

        def sequence(b):
            pe.wait_ge(sem(f"kv_full{b}"), k[f"kv_full{b}"].next(32))
            pe.wait_ge(sem("cur_ready"), k["cur_ready"].next())
            for gr in range(17):
                if gr < 16:
                    e = gr % 2
                    pe.wait_ge(sem(f"gr_read{e}"), k[f"gr_read{e}"].held(2))
                    for j in range(2):
                        for r in range(2):
                            pe.transpose(ps[:, 4 + e, (2 * j + r) * P:(2 * j + r + 1) * P], kvb[b][:, gr * 2 + r, j * P:(j + 1) * P], ident)
                    for r in range(2):
                        last = pe.transpose(ps[0:ROPE, 6 + e, r * P:(r + 1) * P], kpb[b][:, gr * 2 + r, :], ident)
                    last.then_inc(sem("gr_turned"), k["gr_turned"].adds(1))
                if gr == 0:
                    pe.wait_ge(sem("scores_read"), k["scores_read"].held())
                if gr:
                    e = (gr - 1) % 2
                    pe.wait_ge(sem(f"gr_read{e}"), k[f"gr_read{e}"].same())
                    for r in range(2):
                        c = (gr - 1) * 2 + r
                        out = ps[:, c // 8, c % 8 * HT:(c % 8 + 1) * HT]
                        pe.matmul(out, kvt[e][:, r], qcur[:, 0], start=True, stop=False)
                        pe.matmul(out, kvt[e][:, 2 + r], qcur[:, 1], start=False, stop=False)
                        pe.matmul(out, kpt[e][:, r], qpcur[:, :], start=False, stop=True)
            for i in range(2):
                pe.matmul(ps[0:NS, 6, 0:HT], kns[:, i, :], qcur[:, i], start=i == 0, stop=False)
            pe.matmul(ps[0:NS, 6, 0:HT], krs[:, :], qpcur[:, :], start=False, stop=True).then_inc(sem("scores_ready"), k["scores_ready"].adds(1))
            pe.wait_ge(sem("max_ready"), k["max_ready"].next())
            pe.matmul(ps[0:HT, 4, 0:P], mx_[:, :], ident, start=True, stop=True).then_inc(sem("maxt_ready"), k["maxt_ready"].adds(1))
            pe.wait_ge(sem("diag_ready"), k["diag_ready"].next())
            pe.matmul(ps[:, 5, 0:HT], ones[0:HT, :], mdiag[:, :], start=True, stop=True).then_inc(sem("maxb_ready"), k["maxb_ready"].adds(1))
            pe.wait_ge(sem("probs_ready"), k["probs_ready"].next())
            pe.wait_ge(sem("part_ready"), k["part_ready"].next())
            pe.matmul(ps[:, 7, 0:HT], ones, ls_[:, :], start=True, stop=True)
            for j in range(2):
                out = ps[:, 6, P + j * HT:P + (j + 1) * HT]
                for r in range(NPG):
                    pe.matmul(out, kvb[b][:, r, j * P:(j + 1) * P], pb_[:, r, :], start=r == 0, stop=False)
                last = pe.matmul(out, kts[:, j * P:(j + 1) * P], pb_[0:NS, NPG, :], start=False, stop=True)
            last.then_inc(sem("olat_ready"), k["olat_ready"].adds(1))
            pe.wait_ge(sem("olat_read"), k["olat_read"].next())

        with looped(pe, NB // 2, {k[n]: v for n, v in (("cur_ready", 2), ("gr_turned", 32), ("scores_read", 2), ("scores_ready", 2),
                    ("max_ready", 2), ("maxt_ready", 2), ("diag_ready", 2), ("maxb_ready", 2), ("probs_ready", 2),
                    ("part_ready", 2), ("olat_ready", 2), ("olat_read", 2))} | pairs(k, {"kv_full": 32, "gr_read": 32})):
            sequence(0)
            sequence(1)
        for h in range(HEADS):
            r = 64 * (h % 2)
            for j in range(2):
                last = pe.matmul(ps[r:r + 64, 0, h // 2 * NS:(h // 2 + 1) * NS], wkv[:, j, h * P + NOPE:(h + 1) * P], olat[:, j, h, :],
                                 start=j == 0, stop=j == 1)
        last.then_inc(sem("os_ready"), k["os_ready"].adds(1))
        if stop < 7:
            return

        pe.wait_ge(sem("oats_ready"), k["oats_ready"].next())
        for b in range(2):
            k[f"res_free{b}"].n -= 1
        out_free[0] = "res_free"

        def ones_times(b, src, start, stop_):
            for c, (at, width) in enumerate(all_tokens):
                last = pe.matmul(ps[:, 3 * b + c, 0:width], ones, src[:, at:at + width], start=start, stop=stop_)
            return last

        def group_squares():
            pe.wait_ge(sem("res_free0"), k["res_free0"].next())
            for j in range(4):
                pe.wait_ge(sem("ssq_ready"), k["ssq_ready"].next())
                ones_times(0, sq4[j], j == 0, j == 3).then_inc(sem("ssq_used"), k["ssq_used"].adds(1))

        def group_unit(s, half):
            pe.wait_ge(sem("unit_split"), k["unit_split"].next())
            for b in range(2):
                pe.wait_ge(sem(f"res_free{b}"), k[f"res_free{b}"].next())
                view = lambda t: lambda j: t[:, j * 256 + b * P:j * 256 + (b + 1) * P]
                last = products(b, view(whi[s]), view(wlo[s]), ahi[:, 4 * half:4 * half + 4], alo[:, 4 * half:4 * half + 4], 4, all_tokens)
                last.then_inc(sem("res_half" if b == 0 else "unit_done"), k["res_half" if b == 0 else "unit_done"].adds(1))

        group_squares()
        for b in range(2):
            k[f"yt_free{b}"].n += 8
        for g in range(6):
            if g < 4:
                pe.wait_ge(sem("g_split"), k["g_split"].next(4))
            else:
                for b in range(2):
                    pe.wait_ge(sem(f"yt_free{b}"), k[f"yt_free{b}"].next(2))
            for u in range(4):
                if g < 3 and u == 2:
                    group_squares()
                group_unit(u % 2, g % 2)
        pe.wait_ge(sem("g_split"), k["g_split"].next(8))
        dense_fours(2, ahi, alo)

        def layer_norm():
            pe.wait_ge(sem("srow_ready"), k["srow_ready"].next())
            pe.wait_ge(sem("res_free0"), k["res_free0"].next())
            ones_times(0, srow, True, True).then_inc(sem("mean_ready"), k["mean_ready"].adds(1))
            pe.wait_ge(sem("res_free1"), k["res_free1"].next())
            for e in range(KT):
                pe.wait_ge(sem("ssq_ready"), k["ssq_ready"].next())
                ones_times(1, sq2[:, e % 2], e == 0, e == KT - 1).then_inc(sem("ssq_used"), k["ssq_used"].adds(1))

        layer_norm()

        pe.wait_ge(sem("g_split"), k["g_split"].next(8))

        def gate_and_up():
            for u in range(4):
                dense(u, u % 2, ahi, alo, KT)

        def down(v):
            pe.wait_ge(sem("f_split"), k["f_split"].next(2))
            for s in range(2):
                pe.wait_ge(sem("unit_split"), k["unit_split"].next())
                for e in range(4):
                    pe.wait_ge(sem(f"res_free{e % 2}"), k[f"res_free{e % 2}"].next())
                    view = lambda t: lambda j: t[:, j * 512 + e * P:j * 512 + (e + 1) * P]
                    last = products(e % 2, view(whi[s]), view(wlo[s]), fhi[:, 2 * v:2 * v + 2], flo[:, 2 * v:2 * v + 2], 2, all_tokens)
                    last.then_inc(sem("res_half" if e < 3 else "unit_done"), k["res_half" if e < 3 else "unit_done"].adds(1))

        gate_and_up()
        with looped(pe, (NF - 1) // 2, {k["unit_split"]: 12, k["unit_done"]: 12, k["res_half"]: 12, k["f_split"]: 4,
                                        k["res_free0"]: 12, k["res_free1"]: 12}):
            for v in range(2):
                gate_and_up()
                down(v)
        down(0)
        layer_norm()
        pe.wait_ge(sem("affine_ready"), k["affine_ready"].next(2 * KT))
        for i in range(9):
            n = P if i < 8 else NS
            if i == 0:
                for b in range(2):
                    pe.wait_ge(sem(f"res_free{b}"), k[f"res_free{b}"].next())
            pe.wait_ge(sem(f"bank_read{i % 2}"), k[f"bank_read{i % 2}"].held(2))
            for e in range(KT):
                last = pe.transpose(ps[0:n, 2 * (i % 2) + e // 4, e % 4 * P:(e % 4 + 1) * P], mm[:, e, i * P:i * P + n], ident)
            last.then_inc(sem("tok_turned"), k["tok_turned"].adds(1))

    @block.scalar
    def _(act):
        k = Counts()

        def x_hi(b, at, n):
            act.wait_ge(sem("x_turned"), k["x_turned"].next())
            src = ps[:, 2 * b:2 * b + 2, :].rearrange("p a n -> p (a n)")[:, 0:KT * n].rearrange("p (j n) -> p j n", n=n)
            act.activation(xhi[:, :, bass.ds(at, n)], src, ACT.Copy).then_inc(sem("x_hi"), k["x_hi"].adds(1))

        x_hi(0, 0, P)
        x_hi(1, P, P)
        with looped(act, 3, {k["x_turned"]: 2, k["x_hi"]: 2}) as i:
            for b in range(2):
                x_hi(b, (i * 2 + 2 + b) * P, P)
        x_hi(0, SEQ, NS)
        for u, to in enumerate((small[:, :], cq[:, 0], cq[:, 1], cq[:, 2], ckv[:, 0], ckv[:, 1])):
            act.wait_ge(sem("unit_done"), k["unit_done"].next())
            if u == 0:
                act.wait_ge(sem("vecs_ready"), 2)
            act.activation(thirds(to), out3(u % 2), ACT.Copy).then_inc(sem(f"out_free{u % 2}"), k[f"out_free{u % 2}"].adds(1))
            if u == 0:
                act.wait_ge(sem("out_free0"), 1)
                act.dma_start(d_small, small[0:SH, :]).then_inc(sem("stored"), k["stored"].adds(16))
        if stop < 2:
            act.wait_ge(sem("stored"), k["stored"].same())
            return

        for j, (b, n) in enumerate(((0, QL), (1, KL))):
            act.wait_ge(sem("sq_used"), k["sq_used"].next(n // P))
            act.activation(thirds(rs[:, j]), out3(b), ACT.Sqrt, bias=epsc[:, 0:1], scale=1.0 / n).then_inc(sem(f"out_free{b}"), k[f"out_free{b}"].adds(1))
        for name, t, hi, n in (("qn", cq, qn_hi, 3), ("kn", ckv, kn_hi, 2)):
            for j in range(n):
                act.wait_ge(sem(f"{name}_normed"), k[f"{name}_normed"].next())
                act.activation(hi[:, j], t[:, j], ACT.Copy).then_inc(sem(f"{name}_hi"), k[f"{name}_hi"].adds(1))
        act.wait_ge(sem("kn_normed"), k["kn_normed"].same())
        act.dma_start(d_kvs.rearrange("(k p) n -> p k n", p=P), ckv[:, :, SEQ:TOK]).then_inc(sem("stored"), k["stored"].adds(16))
        act.wait_ge(sem("key_turned"), k["key_turned"].next())
        act.dma_start(d_kr, small[R0:R1, :]).then_inc(sem("stored"), k["stored"].adds(16))
        for i in range(9):
            n = P if i < 8 else NS
            to = (o_ckv[0][i * P:i * P + n, :], o_kpe[0][i * P:i * P + n, :]) if i < 8 else (o_ckv[1], o_kpe[1])
            act.wait_ge(sem("keys_out"), k["keys_out"].next())
            for part, dst in zip((tokst[i % 2][0:n, 0:KL], tokst[i % 2][0:n, KL:KL + ROPE]), to):
                act.dma_start(dst, part).then_inc(sem(f"keys_stored{i % 2}"), k[f"keys_stored{i % 2}"].adds(16))
        act.wait_ge(sem("qn_split"), k["qn_split"].next(3))
        k["out_free0"].n += 1
        with looped(act, 8, {k["half_done"]: 1, k["unit_done"]: 1, k["out_free0"]: 2, k["out_free1"]: 2,
                             k["q_stored0"]: 16, k["q_stored1"]: 16, k["q_turned"]: 2}) as i:
            for b in range(2):
                act.wait_ge(sem("half_done" if b == 0 else "unit_done"), k["half_done" if b == 0 else "unit_done"].next())
                act.wait_ge(sem(f"q_stored{b}"), k[f"q_stored{b}"].same())
                act.activation(thirds(qh[b][0:QH]), out3(b, QH), ACT.Copy).then_inc(sem(f"out_free{b}"), k[f"out_free{b}"].adds(1))
                k[f"out_free{b}"].n += 1
            for b in range(2):
                act.wait_ge(sem("q_turned"), k["q_turned"].next())
                act.dma_start(d_q[bass.ds(i * 2 + b, 1)].rearrange("a p n -> (a p) n"), qh[b][0:QH]).then_inc(sem(f"q_stored{b}"), k[f"q_stored{b}"].adds(16))
        act.wait_ge(sem("kn_split"), k["kn_split"].next(2))
        act.wait_ge(sem("keys_turned"), k["keys_turned"].next(9))
        act.wait_ge(sem("stored"), k["stored"].same())
        with looped(act, 4, {k["sub_done"]: 3, k["unit_done"]: 1, k["out_free0"]: 2, k["out_free1"]: 2,
                             k["k_stored0"]: 32, k["k_stored1"]: 32, k["v_stored0"]: 32, k["v_stored1"]: 32,
                             k["v_free0"]: 2, k["v_free1"]: 2}) as i:
          for pair in range(2):
            for b in range(2):
                act.wait_ge(sem("sub_done" if pair * 2 + b < 3 else "unit_done"), k["sub_done" if pair * 2 + b < 3 else "unit_done"].next())
                act.wait_ge(sem(f"k_stored{b}"), k[f"k_stored{b}"].same())
                act.wait_ge(sem(f"v_free{b}"), k[f"v_free{b}"].same())
                src = ps[:, 3 * b:3 * b + 2, :].rearrange("p a n -> p (a n)")
                act.activation(kvh[b], src, ACT.Copy).then_inc(sem(f"out_free{b}"), k[f"out_free{b}"].adds(1))
            for b in range(2):
                act.wait_ge(sem(f"out_free{b}"), k[f"out_free{b}"].same())
                act.dma_start(d_k[bass.ds(i * 4 + pair * 2 + b, 1)].rearrange("a p n -> (a p) n"), kvh[b][0:NOPE]).then_inc(sem(f"k_stored{b}"), k[f"k_stored{b}"].adds(16))
            for b in range(2):
                act.wait_ge(sem(f"v_free{b}"), k[f"v_free{b}"].next())
                act.dma_start(d_v[bass.ds(i * 4 + pair * 2 + b, 1)].rearrange("a p n -> (a p) n"), vst[b]).then_inc(sem(f"v_stored{b}"), k[f"v_stored{b}"].adds(16))
        for name in ("keys_stored", "q_stored", "k_stored", "v_stored"):
            for b in range(2):
                act.wait_ge(sem(f"{name}{b}"), k[f"{name}{b}"].same())
        if stop < 3:
            return

        with looped(act, NCONV // 2, {k["unit_done"]: 2} | {k[f"{n}{b}"]: by for b in range(2) for n, by in
                                    (("out_free", 1), ("conv_done", 1), ("cv_free", 1), ("so_stored", 16))}) as i:
            for b in range(2):
                act.wait_ge(sem("unit_done"), k["unit_done"].next())
                act.activation(thirds(xraw[b][:, CW - 1:]), out3(b), ACT.Copy).then_inc(sem(f"out_free{b}"), k[f"out_free{b}"].adds(1))
                act.wait_ge(sem(f"conv_done{b}"), k[f"conv_done{b}"].next())
                act.wait_ge(sem(f"so_stored{b}"), k[f"so_stored{b}"].same())
                act.activation(so[b][:, :], cv[b][:, :], ACT.Silu).then_inc(sem(f"cv_free{b}"), k[f"cv_free{b}"].adds(1))
                act.wait_ge(sem(f"cv_free{b}"), k[f"cv_free{b}"].same())
                act.dma_start(d_xbc[bass.ds((i * 2 + b) * P, P), :], so[b][:, :]).then_inc(sem(f"so_stored{b}"), k[f"so_stored{b}"].adds(16))
        for d, func in ((d_z, ACT.Silu), (d_g, ACT.Sigmoid)):
            with looped(act, 8, {k["unit_done"]: 2} | {k[f"{n}{b}"]: by for b in range(2) for n, by in
                                                       (("out_free", 1), ("zo_stored", 16))}) as i:
                for b in range(2):
                    act.wait_ge(sem("unit_done"), k["unit_done"].next())
                    act.wait_ge(sem(f"zo_stored{b}"), k[f"zo_stored{b}"].same())
                    bias = vecs[:, bass.ds(i * 2 + b, 1)] if func == ACT.Sigmoid else 0.0
                    act.activation(thirds(zo[b][:, :]), out3(b), func, bias=bias).then_inc(sem(f"out_free{b}"), k[f"out_free{b}"].adds(1))
                    act.wait_ge(sem(f"out_free{b}"), k[f"out_free{b}"].same())
                    act.dma_start(d[bass.ds((i * 2 + b) * P, P), :], zo[b][:, :]).then_inc(sem(f"zo_stored{b}"), k[f"zo_stored{b}"].adds(16))
            if func == ACT.Silu:
                act.wait_ge(sem("crow_ready"), k["crow_ready"].next(6))
                act.dma_start(o["conv_prompt"][0, 0], crow[0:3, :]).then_inc(sem("stored"), k["stored"].adds(16))
                act.dma_start(o["conv_sample"][0].rearrange("b t c -> (b t) c"), crow[3:27, :]).then_inc(sem("stored"), k["stored"].adds(16))
            act.wait_ge(sem("x_whole"), k["x_whole"].next(4))
            half = d_x[0:4 * P] if func == ACT.Silu else d_x[4 * P:]
            act.dma_start(half.rearrange("(j p) n -> p j n", p=P), xo[:, :, :]).then_inc(sem("x_stored"), k["x_stored"].adds(16))
        act.wait_ge(sem("stored"), k["stored"].same())
        act.wait_ge(sem("x_stored"), k["x_stored"].same())
        for name in ("zo_stored", "so_stored"):
            for b in range(2):
                act.wait_ge(sem(f"{name}{b}"), k[f"{name}{b}"].same())
        if stop < 4:
            return

        act.wait_ge(sem("prep_full"), k["prep_full"].next(48))
        act.activation(hb[:, 1], hb[:, 1], ACT.Exp).then_inc(sem("rate_ready"), k["rate_ready"].adds(1))
        act.wait_ge(sem("abs_ready"), k["abs_ready"].next())
        act.activation(sp_u[:, :, :], sp_w[:, :, :], ACT.Exp, scale=-1.0).then_inc(sem("u_exp"), k["u_exp"].adds(1))
        act.wait_ge(sem("sums_ready"), k["sums_ready"].next())
        act.activation(act_[:, :], ps[0:SH, 2:5, :].rearrange("p a n -> p (a n)")[:, 0:TOK], ACT.Copy).then_inc(sem("act_ready"), k["act_ready"].adds(1))
        act.wait_ge(sem("act_ready"), k["act_ready"].same())
        act.dma_start(d_acum, act_[:, :]).then_inc(sem("acum_stored"), k["acum_stored"].adds(16))
        act.wait_ge(sem("ends_ready"), k["ends_ready"].next())
        act.activation(cdb[:, :, :], ps[:, 1, 0:288].rearrange("p (a h) -> p a h", h=SH), ACT.Exp).then_inc(sem("prep_read"), k["prep_read"].adds(1))
        act.activation(dte[:, :, :], dte[:, :, :], ACT.Exp).then_inc(sem("prep_read"), k["prep_read"].adds(1))
        act.wait_ge(sem("rows_ready"), k["rows_ready"].next())
        act.activation(cdp[:, :, :], ps[:, 5, :].rearrange("p (j q t) -> p j q t", q=NB, t=NT)[:, :, :, NT - 1], ACT.Exp).then_inc(sem("prep_read"), k["prep_read"].adds(1))

        def ssm_exps(b, n=P):
            act.wait_ge(sem(f"step_full{b}"), k[f"step_full{b}"].next(64))
            act.activation(s_e[b][:, :, 0:n], s_a[b][:, :, 0:n], ACT.Exp).then_inc(sem("e_ready"), k["e_ready"].adds(1))
            act.wait_ge(sem("pre_ready"), k["pre_ready"].next())
            act.activation(s_bt[b][0:n, :], ps[0:n, 2 * b + 1, 0:P], ACT.Copy).then_inc(sem(f"pre_read{b}"), k[f"pre_read{b}"].adds(1))
            act.wait_ge(sem("dm_ready"), k["dm_ready"].next())
            act.activation(s_g[b][0:n, :, 0:n], s_g[b][0:n, :, 0:n], ACT.Relu, scale=-1.0).then_inc(sem("relu_ready"), k["relu_ready"].adds(1))
            act.wait_ge(sem("relu_ready"), k["relu_ready"].same())
            act.activation(s_g[b][0:n, :, 0:n], s_g[b][0:n, :, 0:n], ACT.Exp, scale=-1.0).then_inc(sem("exp_ready"), k["exp_ready"].adds(1))

        def y_store(b, g, at, n=P):
            act.wait_ge(sem(f"y_out{b}"), k[f"y_out{b}"].next())
            act.dma_start(d_y[bass.ds(g * 512, 512), bass.ds(at, n)].rearrange("(j p) n -> p j n", p=P),
                                                s_y[b][:, :, 0:n]).then_inc(sem(f"y_stored{b}"), k[f"y_stored{b}"].adds(16))

        exps = {"step_full": 64, "pre_read": 1, "y_out": 1, "y_stored": 16}
        with looped(act, SG, {k["relu_ready"]: 9, k["pre_ready"]: 9, k["e_ready"]: 9, k["dm_ready"]: 9, k["exp_ready"]: 9, k["end_read"]: 1,
                              k["st_stored"]: 16, k["it_turned"]: 8, k["off_done"]: 8} |
                    {k[f"{n}{b}"]: by * (5 - b) for n, by in exps.items() for b in range(2)} |
                    pairs(k, {"it_ready": 4, "new_out": 4, "new_stored": 64})) as g:
            ssm_exps(0)
            with looped(act, 3, {k["relu_ready"]: 2, k["pre_ready"]: 2, k["e_ready"]: 2, k["dm_ready"]: 2, k["exp_ready"]: 2} | pairs(k, exps)) as c:
                ssm_exps(1)
                y_store(0, g, c * 2 * P)
                ssm_exps(0)
                y_store(1, g, c * 2 * P + P)
            ssm_exps(1)
            y_store(0, g, 6 * P)
            ssm_exps(0, NS)
            y_store(1, g, 7 * P)
            act.wait_ge(sem("end_read"), k["end_read"].next())
            act.dma_start(o["ssm_prompt"][0, 0].rearrange("h p n -> (h p) n")[bass.ds(g * 512, 512), :]
                                             .rearrange("(j p) n -> p j n", p=P), stout[:, :, :]).then_inc(sem("st_stored"), k["st_stored"].adds(16))
            for q in range(NB + 1):
                if q < NB:
                    b = q % 2
                    act.wait_ge(sem("it_turned"), k["it_turned"].next())
                    if q >= 2:
                        act.wait_ge(sem("off_done"), k["off_done"].next())
                    act.activation(s_it[b][:, :, :], ps[:, 2 + b, :].rearrange("p (j n) -> p j n", n=P), ACT.Copy).then_inc(sem(f"it_ready{b}"), k[f"it_ready{b}"].adds(1))
                if q:
                    b = (q - 1) % 2
                    act.wait_ge(sem(f"new_out{b}"), k[f"new_out{b}"].next())
                    dst = o["ssm_sample"][0, q - 1].rearrange("h p n -> (h p) n")[bass.ds(g * 512, 512), :]
                    act.dma_start(dst.rearrange("(j p) n -> p j n", p=P), s_new[b][:, :, :]).then_inc(sem(f"new_stored{b}"), k[f"new_stored{b}"].adds(16))
            act.wait_ge(sem("off_done"), k["off_done"].next(2))
            y_store(0, g, SEQ, NS)
        act.wait_ge(sem("st_stored"), k["st_stored"].same())
        for name in ("y_stored", "new_stored"):
            for b in range(2):
                act.wait_ge(sem(f"{name}{b}"), k[f"{name}{b}"].same())
        act.sem_inc(sem("ssm_over"), 1)
        if stop < 5:
            return

        def probs(n):
            act.wait_ge(sem("m_ready"), k["m_ready"].next())
            length = (n % NQ + 1) * P
            src = ps[:, 2 * (n % 2):2 * (n % 2) + 2, :].rearrange("p a n -> p (a n)")[:, 0:length]
            act.activation(pr[n % 2][:, 0:length], src, ACT.Exp, bias=negmax[:, n:n + 1], scale=SCALE,
                                                   accum_out=rowsum[:, n:n + 1]).then_inc(sem(f"s_read{n % 2}"), k[f"s_read{n % 2}"].adds(1))

        def attention_pair(i, final):
            for n in range(16):
                if n == 0:
                    act.wait_ge(sem("t_ready0"), k["t_ready0"].same())
                else:
                    act.wait_ge(sem("t_ready0"), k["t_ready0"].next())
                if n < 15 or not final:
                    probs((n + 1) % 16)
                q = n % NQ
                if q >= 4:
                    act.wait_ge(sem("t_ready1"), k["t_ready1"].next())
                    act.activation(ptb[n % 2][:, 512:(q + 1) * P], ps[:, 5, 0:(q - 3) * P], ACT.Copy).then_inc(sem("pt_read1"), k["pt_read1"].adds(1))
            k["t_ready0"].n += 2
            act.wait_ge(sem("t_ready1"), k["t_ready1"].next())
            act.wait_ge(sem("att_stored"), k["att_stored"].same())
            act.activation(att[:, 512:], ps[:, 5, :], ACT.Copy).then_inc(sem("pt_read1"), k["pt_read1"].adds(1))
            act.wait_ge(sem("pt_read1"), k["pt_read1"].same())
            act.wait_ge(sem("pt_read0"), k["pt_read0"].next(17))
            act.dma_start(d_att[bass.ds(i * P, P), 0:SEQ], att[:, :]).then_inc(sem("att_stored"), k["att_stored"].adds(16))

        probs(0)
        with looped(act, HEADS // 2 - 1, {k["m_ready"]: 16, k["t_ready0"]: 17, k["t_ready1"]: 9, k["pt_read1"]: 9,
                                          k["pt_read0"]: 17, k["att_stored"]: 16, k["s_read0"]: 8, k["s_read1"]: 8}) as i:
            attention_pair(i, False)
        attention_pair(HEADS // 2 - 1, True)
        act.wait_ge(sem("att_stored"), k["att_stored"].same())
        act.sem_inc(sem("prompt_over"), 1)
        if stop < 6:
            return

        for i in range(8):
            act.wait_ge(sem("uk_turned"), k["uk_turned"].next())
            act.activation(ukt[:, 2 * i:2 * i + 2, :].rearrange("p h c -> p (h c)"), ps[0:NOPE, i, :], ACT.Copy).then_inc(sem("uk_ready"), k["uk_ready"].adds(1))
        act.wait_ge(sem("lat_ready"), k["lat_ready"].next())
        for j in range(2):
            act.activation(qlat[:, j].rearrange("p b (h t) -> p b h t", t=NT),
                                               ps[:, j, :].rearrange("p (h b t) -> p b h t", h=HEADS, t=NT), ACT.Copy).then_inc(sem("qlat_ready"), k["qlat_ready"].adds(1))

        def sequence(b):
            for gr in range(16):
                act.wait_ge(sem("gr_turned"), k["gr_turned"].next())
                act.activation(kvt[gr % 2][:, :, :], ps[:, 4 + gr % 2, :].rearrange("p (a n) -> p a n", n=P), ACT.Copy).then_inc(sem(f"gr_read{gr % 2}"), k[f"gr_read{gr % 2}"].adds(1))
            act.wait_ge(sem("sub_ready"), k["sub_ready"].next())
            act.activation(pb_[:, :, :], pb_[:, :, :], ACT.Exp, scale=SCALE).then_inc(sem("probs_ready"), k["probs_ready"].adds(1))

        with looped(act, NB // 2, {k["gr_turned"]: 32, k["sub_ready"]: 2, k["probs_ready"]: 2, k["gr_read0"]: 16, k["gr_read1"]: 16}):
            sequence(0)
            sequence(1)
        act.wait_ge(sem("oats_ready"), k["oats_ready"].next())
        act.dma_start(d_att[:, SEQ:TOK].rearrange("(j p) n -> p j n", p=P), oats[:, :, :]).then_inc(sem("stored"), k["stored"].adds(16))
        act.wait_ge(sem("stored"), k["stored"].same())
        if stop < 7:
            return

        act.sem_inc(sem("samples_over"), 1)

        def root(b, to, n):
            act.activation(thirds(to[:, :]), out3(b), ACT.Sqrt, bias=epsc[:, 1:2], scale=1.0 / n).then_inc(sem(f"res_free{b}"), k[f"res_free{b}"].adds(1))

        for g in range(4):
            act.wait_ge(sem("ssq_used"), k["ssq_used"].next(4))
            root(0, rsrow, DI // SG)
            for j in range(4):
                act.wait_ge(sem("yg_ready"), k["yg_ready"].next())
                act.activation(ahi[:, 4 * (g % 2) + j], yz[:, j], ACT.Copy).then_inc(sem("g_hi"), k["g_hi"].adds(1))
        done = UNITS[6]
        for b in range(2):
            k[f"yt_full{b}"].n += 8 * 32
        for g in range(2):
            act.wait_ge(sem("unit_done"), done + 12 + 4 * g)
            for j in range(4):
                act.wait_ge(sem(f"yt_full{j % 2}"), k[f"yt_full{j % 2}"].next(16))
                act.activation(ahi[:, 4 * g + j], yt[j % 2][:, :], ACT.Copy).then_inc(sem("g_hi"), k["g_hi"].adds(1))
        for b in range(2):
            k[f"gt_free{b}"].n += 8
        for e in range(KT):
            if e % 4 == 0:
                act.wait_ge(sem("unit_done"), done + 20 + e)
            act.wait_ge(sem(f"gt_free{e % 2}"), k[f"gt_free{e % 2}"].next())
            act.activation(ahi[:, e], mm[:, e], ACT.Copy).then_inc(sem("g_hi"), k["g_hi"].adds(1))

        def layer_norm(g, b, split):
            act.wait_ge(sem("mean_ready"), k["mean_ready"].next())
            act.activation(thirds(murow[:, :]), out3(0), ACT.Copy, scale=1.0 / D_MODEL).then_inc(sem("res_free0"), k["res_free0"].adds(1))
            for e in range(KT):
                act.wait_ge(sem("centred"), k["centred"].next())
                if e >= 2:
                    act.wait_ge(sem("ssq_used"), k["ssq_used"].next())
                act.activation(sq2[:, e % 2], mm[:, e], ACT.Square).then_inc(sem("ssq_ready"), k["ssq_ready"].adds(1))
            act.wait_ge(sem("ssq_used"), k["ssq_used"].next(2))
            root(1, rsrow, D_MODEL)
            for e in range(KT):
                act.wait_ge(sem("scaled"), k["scaled"].next())
                act.activation(mm[:, e], mm[:, e], ACT.Identity, bias=vecs[:, b + e:b + e + 1],
                                                     scale=vecs[:, g + e:g + e + 1]).then_inc(sem("affine_ready"), k["affine_ready"].adds(1))
                if split:
                    act.wait_ge(sem("affine_ready"), k["affine_ready"].same())
                    act.activation(ahi[:, e], mm[:, e], ACT.Copy).then_inc(sem("g_hi"), k["g_hi"].adds(1))

        k["res_free1"].n += 6 * 4 + KT // 2
        layer_norm(V_L1G, V_L1B, True)

        def gate(v, j):
            act.wait_ge(sem("unit_done"), k["unit_done"].next())
            act.activation(thirds(fg[j]), out3(0), ACT.Silu).then_inc(sem("res_free0"), k["res_free0"].adds(1))
            act.wait_ge(sem("unit_done"), k["unit_done"].next())
            act.wait_ge(sem("res_free1"), k["res_free1"].next())
            act.activation(fhi[:, 2 * v + j], ff[j][:, :], ACT.Copy).then_inc(sem("f_hi"), k["f_hi"].adds(1))

        k["unit_done"].n = TOTAL_UNITS - 6 * NF
        for j in range(2):
            gate(0, j)
        with looped(act, (NF - 1) // 2, {k["unit_done"]: 12, k["f_hi"]: 4, k["res_free0"]: 4, k["res_free1"]: 12}):
            for v in range(2):
                for j in range(2):
                    gate(1 - v, j)
                k["unit_done"].n += 2
                k["res_free1"].n += 4
        k["res_free1"].n += 4
        layer_norm(V_L2G, V_L2B, False)
        for i in range(9):
            n = P if i < 8 else NS
            act.wait_ge(sem("tok_turned"), k["tok_turned"].next())
            act.wait_ge(sem(f"tok_stored{i % 2}"), k[f"tok_stored{i % 2}"].same())
            act.activation(ytok[i % 2][0:n, 0:512], ps[0:n, 2 * (i % 2), :], ACT.Copy).then_inc(sem(f"bank_read{i % 2}"), k[f"bank_read{i % 2}"].adds(1))
            k[f"bank_read{i % 2}"].n += 1
            act.wait_ge(sem(f"bank_read{i % 2}"), k[f"bank_read{i % 2}"].same())
            dst = o["y_prompt"][0, i * P:i * P + n, :] if i < 8 else o["y_sample"].rearrange("b t d -> (b t) d")
            act.dma_start(dst, ytok[i % 2][0:n, :]).then_inc(sem(f"tok_stored{i % 2}"), k[f"tok_stored{i % 2}"].adds(16))
        for b in range(2):
            act.wait_ge(sem(f"tok_stored{b}"), k[f"tok_stored{b}"].same())

    @block.vector
    def _(dve):
        k = Counts()
        dve.wait_ge(sem("rows_full"), 16 * 9)
        dve.tensor_copy(drow2[:, :].rearrange("p (a b) -> p a b", a=2),
                        drow[:, :].unsqueeze(2).broadcast_to([16, 2, 64])).then_inc(sem("drow_wide"), 1)

        def x_lo(b, at, n):
            dve.wait_ge(sem("x_hi"), k["x_hi"].next())
            src = ps[:, 2 * b:2 * b + 2, :].rearrange("p a n -> p (a n)")[:, 0:KT * n].rearrange("p (j n) -> p j n", n=n)
            dve.tensor_tensor(xlo[:, :, bass.ds(at, n)], src,
                                               xhi[:, :, bass.ds(at, n)].bitcast(F32), ALU.subtract).then_inc(sem("x_split"), k["x_split"].adds(1))

        x_lo(0, 0, P)
        x_lo(1, P, P)
        with looped(dve, 3, {k["x_hi"]: 2, k["x_split"]: 2}) as i:
            for b in range(2):
                x_lo(b, (i * 2 + 2 + b) * P, P)
        x_lo(0, SEQ, NS)
        dve.wait_ge(sem("vecs_turned"), 1)
        dve.tensor_copy(vecs[:, 0:V_END], ps[:, 6, 0:V_END]).then_inc(sem("vecs_ready"), 1)
        dve.tensor_copy(dskip[:, :], ps[:, 6, 128:144]).then_inc(sem("vecs_ready"), 1)

        if stop < 2:
            return
        for j in range(5):
            dve.wait_ge(sem(f"out_free{(1 + j) % 2}"), k[f"out_free{(1 + j) % 2}"].next(2 if j == 1 else 1))
            if j >= 2:
                dve.wait_ge(sem("sq_used"), k["sq_used"].next())
            src = cq[:, j] if j < 3 else ckv[:, j - 3]
            dve.tensor_tensor(sq[:, j % 2], src, src, ALU.mult).then_inc(sem("sq_ready"), k["sq_ready"].adds(1))

        def norm(name, j0, t, lo, hi, n, g):
            dve.wait_ge(sem(f"out_free{j0}"), k[f"out_free{j0}"].next())
            dve.reciprocal(rs[:, j0], rs[:, j0]).then_inc(sem("dve_step"), k["dve_step"].adds(1))
            dve.wait_ge(sem("dve_step"), k["dve_step"].same())
            for j in range(n):
                dve.scalar_tensor_tensor(
                    out=t[:, j], in0=t[:, j], scalar=vecs[:, g + j:g + j + 1], in1=rs[:, j0], op0=ALU.mult, op1=ALU.mult).then_inc(sem(f"{name}_normed"), k[f"{name}_normed"].adds(1))
            for j in range(n):
                dve.wait_ge(sem(f"{name}_hi"), k[f"{name}_hi"].next())
                dve.tensor_tensor(lo[:, j], t[:, j], hi[:, j].bitcast(F32), ALU.subtract).then_inc(sem(f"{name}_split"), k[f"{name}_split"].adds(1))

        dve.wait_ge(sem("vecs_ready"), 2)
        norm("qn", 0, cq, qn_lo, qn_hi, 3, V_QN)
        norm("kn", 1, ckv, kn_lo, kn_hi, 2, V_KVN)

        def rotate(b, rows_, done):
            dve.wait_ge(sem("rot_ready"), k["rot_ready"].next())
            dve.tensor_tensor(thirds(rot[b][R0:R1]), ps[R0:R1, 3 * b:3 * b + 3, 0:CH],
                                                    thirds(rope_t[R0:R1, 1]), ALU.mult).then_inc(sem(f"out_free{b}"), k[f"out_free{b}"].adds(1))
            dve.tensor_tensor(rows_, rows_, rope_t[R0:R1, 0], ALU.mult).then_inc(sem("dve_step"), k["dve_step"].adds(1))
            dve.wait_ge(sem("dve_step"), k["dve_step"].same())
            dve.wait_ge(sem(f"out_free{b}"), k[f"out_free{b}"].same())
            dve.tensor_tensor(rows_, rows_, rot[b][R0:R1], ALU.add).then_inc(sem(done), k[done].adds(1))

        dve.wait_ge(sem("rope_full"), k["rope_full"].next(32))
        dve.wait_ge(sem("kn_split"), k["kn_split"].same())
        rotate(0, small[R0:R1, :], "key_turned")
        for i in range(9):
            n = P if i < 8 else NS
            dve.wait_ge(sem("keys_turned"), k["keys_turned"].next())
            dve.wait_ge(sem(f"keys_stored{i % 2}"), k[f"keys_stored{i % 2}"].held(32))
            if i < 2:
                dve.wait_ge(sem("sq_used"), k["sq_used"].next(1))
            dve.tensor_copy(tokst[i % 2][0:n], ps[0:n, 6 + i % 2, 0:KL + ROPE]).then_inc(sem("keys_out"), k["keys_out"].adds(1))
        with looped(dve, 8, {k["out_free0"]: 2, k["out_free1"]: 2, k["rot_ready"]: 2, k["dve_step"]: 2, k["q_turned"]: 2}):
            for b in range(2):
                k[f"out_free{b}"].n += 1
                rotate(b, qh[b][R0:R1], "q_turned")
        with looped(dve, 8, {k["v_turned"]: 2, k["v_free0"]: 1, k["v_free1"]: 1, k["v_stored0"]: 16, k["v_stored1"]: 16}):
            for b in range(2):
                dve.wait_ge(sem("v_turned"), k["v_turned"].next())
                dve.wait_ge(sem(f"v_stored{b}"), k[f"v_stored{b}"].held(16))
                dve.tensor_copy(vst[b], ps[:, 6 + b, :]).then_inc(sem(f"v_free{b}"), k[f"v_free{b}"].adds(1))
        if stop < 3:
            return

        for b in range(2):
            dve.wait_ge(sem("st_turned"), k["st_turned"].next())
            dve.tensor_copy(cw[:, b * 12:(b + 1) * 12, :],
                                              ps[:, 6 + b, 0:12 * 29].rearrange("p (j n) -> p j n", n=29)).then_inc(sem("cw_ready"), k["cw_ready"].adds(1))
            dve.memset(xraw[b][:, 0:CW - 1], 0.0).then_inc(sem("dve_step"), k["dve_step"].adds(1))
        dve.wait_ge(sem("cw_ready"), k["cw_ready"].same())
        dve.wait_ge(sem("dve_step"), k["dve_step"].same())
        for b in range(2):
            k[f"out_free{b}"].n += 8
        with looped(dve, NCONV // 2, {k["dve_step"]: 8, k["conv_a"]: 14} | {k[f"{n}{b}"]: 1 for b in range(2)
                                                             for n in ("out_free", "conv_done", "cv_free")}) as i:
            for b in range(2):
                t = i * 2 + b
                tap = lambda j: cw[:, bass.ds(t, 1), j:j + 1].rearrange("p a b -> p (a b)")
                sample = cv[b][:, SEQ:].rearrange("p (s t) -> p s t", t=NT)
                dve.wait_ge(sem(f"out_free{b}"), k[f"out_free{b}"].next())
                dve.wait_ge(sem(f"cv_free{b}"), k[f"cv_free{b}"].held())
                dve.tensor_copy(xs7[b][:, :, 0:3], cw[:, bass.ds(t, 1), 5:29].rearrange("p a (s t) -> p (a s) t", t=3)).then_inc(sem("dve_step"), k["dve_step"].adds(1))
                dve.tensor_copy(xs7[b][:, :, 3:7], xraw[b][:, 3 + SEQ:].rearrange("p (s t) -> p s t", t=NT)).then_inc(sem("dve_step"), k["dve_step"].adds(1))
                dve.tensor_copy(ccol[:, bass.ds(t, 1), 0:3].rearrange("p a b -> p (a b)"), xraw[b][:, SEQ:SEQ + 3]).then_inc(sem("dve_step"), k["dve_step"].adds(1))
                dve.tensor_scalar(cv[b][:, 0:SEQ], xraw[b][:, 0:SEQ], tap(0), tap(4), ALU.mult, ALU.add).then_inc(sem("conv_a"), 1)
                dve.wait_ge(sem("dve_step"), k["dve_step"].same())
                dve.tensor_copy(ccol[:, bass.ds(t, 1), 3:27].rearrange("p a (s t) -> p (a s) t", t=3), xs7[b][:, :, 4:7]).then_inc(sem("dve_step"), k["dve_step"].adds(1))
                dve.tensor_scalar(sample, xs7[b][:, :, 0:NT], tap(0), tap(4), ALU.mult, ALU.add).then_inc(sem("conv_a"), 1)
                k["conv_a"].n += 2
                for j in range(1, CW):
                    dve.wait_ge(sem("conv_a"), k["conv_a"].same())
                    dve.scalar_tensor_tensor(out=cv[b][:, 0:SEQ], in0=xraw[b][:, j:j + SEQ], scalar=tap(j),
                                                             in1=cv[b][:, 0:SEQ], op0=ALU.mult, op1=ALU.add).then_inc(sem("conv_a"), k["conv_a"].adds(1))
                    last = dve.scalar_tensor_tensor(out=sample, in0=xs7[b][:, :, j:j + NT], scalar=tap(j), in1=sample,
                                                    op0=ALU.mult, op1=ALU.add)
                    last.then_inc(sem("conv_a" if j < CW - 1 else f"conv_done{b}"), k["conv_a" if j < CW - 1 else f"conv_done{b}"].adds(1))
        def whole_x(half):
            for j in range(4):
                e = half * 4 + j
                dve.tensor_tensor(xo[:, j], xhi[:, e].bitcast(F32), xlo[:, e].bitcast(F32), ALU.add).then_inc(sem("x_whole"), k["x_whole"].adds(1))

        whole_x(0)
        for i in range(6):
            dve.wait_ge(sem("crow_turned"), k["crow_turned"].next())
            dve.tensor_copy(crow[:, i * 512:(i + 1) * 512], ps[0:27, 6 + i % 2, :]).then_inc(sem("crow_ready"), k["crow_ready"].adds(1))
        dve.wait_ge(sem("x_stored"), k["x_stored"].next(16))
        whole_x(1)
        if stop < 4:
            return

        step = k["dve_step"]


        dve.wait_ge(sem("prep_full"), k["prep_full"].next(48))
        dve.wait_ge(sem("dt_turned"), k["dt_turned"].next())
        dve.memset(dt_[:, 8], 0.0).then_inc(step.sem, step.adds(1))
        dve.wait_ge(step.sem, step.same())
        dve.tensor_copy(dt_[:, 0:8], ps[:, 6, 0:256].rearrange("p (a h) -> p a h", h=SH)).then_inc(step.sem, step.adds(1))
        dve.wait_ge(step.sem, step.same())
        dve.tensor_copy(dt_[0:NS, 8], ps[0:NS, 6, 256:288]).then_inc(step.sem, step.adds(1))
        dve.wait_ge(step.sem, step.same())
        dve.tensor_tensor(dt_[:, :, :], dt_[:, :, :], hb[:, 0:1].broadcast_to([P, 9, SH]), ALU.add).then_inc(step.sem, step.adds(1))
        dve.wait_ge(step.sem, step.same())
        dve.tensor_scalar(sp_w[:, :, :], dt_[:, :, :], -1.0, None, ALU.mult).then_inc(step.sem, step.adds(1))
        dve.wait_ge(step.sem, step.same())
        dve.tensor_tensor(sp_w[:, :, :], sp_w[:, :, :], dt_[:, :, :], ALU.max).then_inc(sem("abs_ready"), k["abs_ready"].adds(1))
        dve.wait_ge(sem("u_exp"), k["u_exp"].next())
        dve.tensor_scalar(sp_z[:, :, :], sp_u[:, :, :], 2.0, None, ALU.add).then_inc(step.sem, step.adds(1))
        dve.wait_ge(step.sem, step.same())
        dve.reciprocal(sp_z[:, :, :], sp_z[:, :, :]).then_inc(step.sem, step.adds(1))
        dve.wait_ge(step.sem, step.same())
        dve.tensor_tensor(sp_z[:, :, :], sp_z[:, :, :], sp_u[:, :, :], ALU.mult).then_inc(step.sem, step.adds(1))
        dve.wait_ge(step.sem, step.same())
        dve.tensor_tensor(sp_w[:, :, :], sp_z[:, :, :], sp_z[:, :, :], ALU.mult).then_inc(step.sem, step.adds(1))
        dve.wait_ge(step.sem, step.same())
        dve.tensor_scalar(sp_p[:, :, :], sp_w[:, :, :], 1.0 / 17, None, ALU.mult).then_inc(step.sem, step.adds(1))
        dve.wait_ge(step.sem, step.same())
        for n in range(15, 1, -2):
            dve.scalar_tensor_tensor(out=sp_p[:, :, :], in0=sp_p[:, :, :], scalar=1.0 / n, in1=sp_w[:, :, :],
                                          op0=ALU.add, op1=ALU.mult).then_inc(step.sem, step.adds(1))
            dve.wait_ge(step.sem, step.same())
        dve.scalar_tensor_tensor(out=sp_p[:, :, :], in0=sp_p[:, :, :], scalar=1.0, in1=sp_z[:, :, :], op0=ALU.add, op1=ALU.mult).then_inc(step.sem, step.adds(1))
        dve.wait_ge(step.sem, step.same())
        dve.tensor_scalar(dt_[:, :, :], dt_[:, :, :], 0.0, None, ALU.max).then_inc(step.sem, step.adds(1))
        dve.wait_ge(step.sem, step.same())
        dve.scalar_tensor_tensor(out=dt_[:, :, :], in0=sp_p[:, :, :], scalar=2.0, in1=dt_[:, :, :], op0=ALU.mult, op1=ALU.add).then_inc(step.sem, step.adds(1))
        dve.wait_ge(step.sem, step.same())
        dve.wait_ge(sem("rate_ready"), k["rate_ready"].next())
        dve.scalar_tensor_tensor(out=da[:, :, :], in0=dt_[:, :, :], scalar=-1.0,
                                                   in1=hb[:, 1:2].broadcast_to([P, 9, SH]), op0=ALU.mult, op1=ALU.mult).then_inc(sem("da_ready"), k["da_ready"].adds(1))
        dve.wait_ge(sem("sums_ready"), k["sums_ready"].next())
        dve.memset(acs[:, 8], 0.0).then_inc(step.sem, step.adds(1))
        dve.wait_ge(step.sem, step.same())
        dve.memset(dte[:, 8], 0.0).then_inc(step.sem, step.adds(1))
        dve.wait_ge(step.sem, step.same())
        dve.tensor_copy(acs[:, 0:8], ps[:, 0, 0:256].rearrange("p (a h) -> p a h", h=SH)).then_inc(step.sem, step.adds(1))
        dve.wait_ge(step.sem, step.same())
        dve.tensor_copy(acs[0:NS, 8], ps[0:NS, 0, 256:288]).then_inc(step.sem, step.adds(1))
        dve.wait_ge(step.sem, step.same())
        dve.tensor_tensor(dte[:, 0:8], ps[:, 1, 0:256].rearrange("p (a h) -> p a h", h=SH), acs[:, 0:8], ALU.subtract).then_inc(step.sem, step.adds(1))
        dve.wait_ge(step.sem, step.same())
        dve.tensor_tensor(dte[0:NS, 8], ps[0:NS, 1, 256:288], acs[0:NS, 8], ALU.subtract).then_inc(sem("ends_ready"), k["ends_ready"].adds(1))
        dve.wait_ge(sem("prep_read"), k["prep_read"].next(2))
        dve.tensor_tensor(dte[:, :, :], dte[:, :, :], dt_[:, :, :], ALU.mult).then_inc(step.sem, step.adds(1))
        dve.wait_ge(step.sem, step.same())
        dve.wait_ge(sem("prep_read"), k["prep_read"].next(1))

        by_head = lambda t, c, g: t.rearrange("p a h -> p (a h)")[:, bass.ds(c * SH + g * HG, HG)]

        def ssm_prep(b, g, c, n=P):
            wide = lambda t, m: by_head(t[:, :, :], c, g)[0:n].unsqueeze(2).broadcast_to([n, HG, m])
            dve.wait_ge(sem(f"step_full{b}"), k[f"step_full{b}"].next(64))
            dve.tensor_tensor(s_g[b][0:n, :, 0:n], s_a[b][0:n, :, 0:n], wide(acs, n), ALU.subtract).then_inc(sem("dm_ready"), k["dm_ready"].adds(1))
            dve.wait_ge(sem("pre_ready"), k["pre_ready"].next())
            xt = ps[0:n, 2 * b, :].rearrange("p (h q) -> p h q", q=SP_)
            dve.tensor_tensor(s_xd[b][0:n], xt, wide(dt_, SP_), ALU.mult).then_inc(step.sem, step.adds(1))
            dve.tensor_tensor(s_xe[b][0:n], xt, wide(dte, SP_), ALU.mult).then_inc(step.sem, step.adds(1))
            dve.wait_ge(sem(f"pre_read{b}"), k[f"pre_read{b}"].next())
            dve.tensor_tensor(s_cb[b][0:n, 0:n], ps[0:n, 2 * b + 1, P:P + n],
                                                    (const("causal") if n == P else const("causal_s"))[0:n, :], ALU.mult).then_inc(sem(f"pre_read{b}"), k[f"pre_read{b}"].adds(1))
            dve.wait_ge(sem(f"pre_read{b}"), k[f"pre_read{b}"].same())
            dve.wait_ge(sem("e_ready"), k["e_ready"].next())
            dve.tensor_tensor(s_e[b][:, :, 0:n], s_e[b][:, :, 0:n], s_c[b][:, 0:n].unsqueeze(1).broadcast_to([P, HG, n]), ALU.mult).then_inc(step.sem, step.adds(1))
            dve.wait_ge(sem("exp_ready"), k["exp_ready"].next())
            dve.tensor_tensor(s_g[b][0:n, :, 0:n], s_g[b][0:n, :, 0:n],
                                               s_cb[b][0:n, 0:n].unsqueeze(1).broadcast_to([n, HG, n]), ALU.mult).then_inc(sem("g_ready"), k["g_ready"].adds(1))

        def ssm_y(b, g, n=P):
            dve.wait_ge(sem(f"y_stored{b}"), k[f"y_stored{b}"].held(16))
            for j in range(4):
                last = dve.scalar_tensor_tensor(out=s_y[b][:, j, 0:n], in0=s_x[b][:, j, 0:n], scalar=dskip[:, bass.ds(g * 4 + j, 1)],
                                                in1=ps[:, 4 + b, j * n:(j + 1) * n], op0=ALU.mult, op1=ALU.add)
            last.then_inc(sem(f"y_out{b}"), k[f"y_out{b}"].adds(1))

        def ssm_post(b, g, c):
            dve.wait_ge(sem("y_ready"), k["y_ready"].next())
            ssm_y(b, g)
            dve.wait_ge(sem("prod_ready"), k["prod_ready"].next())
            dve.tensor_tensor(state[:, :, :], state[:, :, :], by_head(cdb[:, :, :], c, g).unsqueeze(2).broadcast_to([P, HG, SP_]), ALU.mult).then_inc(step.sem, step.adds(1))
            dve.wait_ge(step.sem, step.same())
            dve.tensor_tensor(state[:, :, :], state[:, :, :], ps[:, 6, :].rearrange("p (h q) -> p h q", q=SP_), ALU.add).then_inc(sem("state_ready"), k["state_ready"].adds(1))

        each = {"step_full": 64, "pre_read": 2, "y_out": 1, "y_stored": 16}
        with looped(dve, SG, {k["pre_ready"]: 9, k["e_ready"]: 9, k["dm_ready"]: 9, k["exp_ready"]: 9, k["g_ready"]: 9,
                              k["state_ready"]: 9, k["y_ready"]: 8, k["prod_ready"]: 8, step: 27 + 8 + 0, k["end_turned"]: 1,
                              k["st_stored"]: 16, k["end_read"]: 1, k["u_ready"]: 8, k["upd_ready"]: 8, k["off_done"]: 8} |
                    {k[f"{n}{b}"]: by * (5 - b) for n, by in each.items() for b in range(2)} |
                    pairs(k, {"new_out": 4, "new_stored": 64})) as g:
            dve.memset(state[:, :, :], 0.0).then_inc(sem("state_ready"), k["state_ready"].adds(1))
            ssm_prep(0, g, 0)
            with looped(dve, 3, {k[n]: 2 for n in ("pre_ready", "e_ready", "dm_ready", "exp_ready", "g_ready", "state_ready",
                                                   "y_ready", "prod_ready")} | {step: 8} | pairs(k, each)) as c:
                ssm_prep(1, g, c * 2 + 1)
                ssm_post(0, g, c * 2)
                ssm_prep(0, g, c * 2 + 2)
                ssm_post(1, g, c * 2 + 1)
            ssm_prep(1, g, 7)
            ssm_post(0, g, 6)
            ssm_prep(0, g, 8, NS)
            ssm_post(1, g, 7)
            dve.wait_ge(sem("end_turned"), k["end_turned"].next())
            dve.wait_ge(sem("st_stored"), k["st_stored"].held(16))
            dve.tensor_copy(stout[:, :, :], ps[:, 7, :].rearrange("p (j n) -> p j n", n=P)).then_inc(sem("end_read"), k["end_read"].adds(1))
            for q in range(NB + 1):
                if q < NB:
                    dve.tensor_scalar(s_u[q % 2][:, :], s_xe[0][0:NS].rearrange("p h q -> p (h q)"),
                                                       const("batch")[0:NS, q:q + 1], None, ALU.mult).then_inc(sem("u_ready"), k["u_ready"].adds(1))
                if q:
                    b = (q - 1) % 2
                    dve.wait_ge(sem("upd_ready"), k["upd_ready"].next())
                    dve.wait_ge(sem(f"new_stored{b}"), k[f"new_stored{b}"].held(16))
                    for j in range(4):
                        last = dve.scalar_tensor_tensor(
                            out=s_new[b][:, j], in0=s_in[b][:, j], in1=ps[:, 6 + b, j * P:(j + 1) * P], op0=ALU.mult, op1=ALU.add,
                            scalar=cdp[:, :, :].rearrange("p j q -> p (j q)")[:, bass.ds(g * (4 * NB) + (j * NB + q - 1), 1)])
                    last.then_inc(sem(f"new_out{b}"), k[f"new_out{b}"].adds(1))
            dve.wait_ge(sem("off_done"), k["off_done"].next(8))
            ssm_y(0, g, NS)
        if stop < 5:
            return

        dve.wait_ge(sem("pages_full"), k["pages_full"].next(16 * NB))
        dve.tensor_copy(pgf[:, :], pgi[:, :]).then_inc(step.sem, step.adds(1))
        dve.wait_ge(step.sem, step.same())
        dve.tensor_scalar(pgf[:, :], pgf[:, :], 4.0, const("quarter"), ALU.mult, ALU.add).then_inc(step.sem, step.adds(1))
        dve.wait_ge(step.sem, step.same())
        dve.tensor_copy(pgx[:, :], pgf[:, :]).then_inc(sem("index_ready"), k["index_ready"].adds(1))
        dve.tensor_copy(ident_b[:, :], ident).then_inc(sem("bf_ready"), k["bf_ready"].adds(1))
        dve.tensor_copy(after_b[:, :], const("after")).then_inc(sem("bf_ready"), k["bf_ready"].adds(1))

        def row_max(n):
            dve.wait_ge(sem("s_ready"), k["s_ready"].next())
            length = (n % NQ + 1) * P
            src = ps[:, 2 * (n % 2):2 * (n % 2) + 2, :].rearrange("p a n -> p (a n)")[:, 0:length]
            dve.tensor_reduce(rowmax[:, n:n + 1], src, AX, ALU.max).then_inc(step.sem, step.adds(1))
            dve.wait_ge(step.sem, step.same())
            dve.tensor_scalar(negmax[:, n:n + 1], rowmax[:, n:n + 1], -SCALE, None, ALU.mult).then_inc(sem("m_ready"), k["m_ready"].adds(1))

        def out_norm(n):
            b, q = n // NQ, n % NQ
            dve.wait_ge(sem("o_ready"), k["o_ready"].next())
            dve.reciprocal(rowinv[:, n:n + 1], rowsum[:, n:n + 1]).then_inc(step.sem, step.adds(1))
            dve.wait_ge(step.sem, step.same())
            dve.tensor_scalar(ob[:, q, b * VH:(b + 1) * VH], ps[:, 6 + n % 2, 0:VH], rowinv[:, n:n + 1],
                                                      None, ALU.mult).then_inc(sem(f"o_read{n % 2}"), k[f"o_read{n % 2}"].adds(1))

        def attention_pair(final):
            for n in range(16):
                if n < 15 or not final:
                    row_max((n + 1) % 16)
                if n:
                    out_norm(n - 1)
                dve.wait_ge(sem("t_ready0"), k["t_ready0"].next())
                width = min(n % NQ + 1, 4) * P
                dve.tensor_copy(ptb[n % 2][:, 0:width], ps[:, 4, 0:width]).then_inc(sem("pt_read0"), k["pt_read0"].adds(1))
            out_norm(15)
            dve.wait_ge(sem("t_ready0"), k["t_ready0"].next())
            dve.wait_ge(sem("att_stored"), k["att_stored"].held(16))
            dve.tensor_copy(att[:, 0:512], ps[:, 4, :]).then_inc(sem("pt_read0"), k["pt_read0"].adds(1))

        row_max(0)
        with looped(dve, HEADS // 2 - 1, {k["s_ready"]: 16, step: 32, k["m_ready"]: 16, k["o_ready"]: 16, k["t_ready0"]: 17,
                                          k["pt_read0"]: 17, k["att_stored"]: 16, k["o_read0"]: 8, k["o_read1"]: 8}):
            attention_pair(False)
        attention_pair(True)
        if stop < 6:
            return

        dve.wait_ge(sem("late_full"), k["late_full"].next(96))
        dve.memset(snew[:, :], -1e30).then_inc(step.sem, step.adds(1))
        dve.tensor_copy(qpb[:, :, :].rearrange("p b (h t) -> p b h t", t=NT),
                             qps[:, :, :].rearrange("p h (b t) -> p b h t", t=NT)).then_inc(step.sem, step.adds(1))
        dve.wait_ge(step.sem, step.same())
        dve.wait_ge(sem("qlat_ready"), k["qlat_ready"].next(2))

        def sequence(b, q):
            dve.tensor_copy(qcur[:, :, :], qlat[:, :, bass.ds(q, 1), :].rearrange("p k a n -> p (k a) n")).then_inc(step.sem, step.adds(1))
            dve.tensor_copy(qpcur[:, :], qpb[:, bass.ds(q, 1), :].rearrange("p a n -> p (a n)")).then_inc(sem("cur_ready"), k["cur_ready"].adds(1))
            for gr in range(16):
                dve.wait_ge(sem("gr_turned"), k["gr_turned"].next())
                dve.tensor_copy(kpt[gr % 2][:, :, :], ps[0:ROPE, 6 + gr % 2, 0:2 * P].rearrange("p (a n) -> p a n", n=P)).then_inc(sem(f"gr_read{gr % 2}"), k[f"gr_read{gr % 2}"].adds(1))
            dve.wait_ge(sem("scores_ready"), k["scores_ready"].next())
            all_scores = ps[:, 0:4, :].rearrange("p a (r n) -> p (a r) n", n=HT)
            dve.tensor_reduce(mx_[:, :], all_scores.rearrange("p r n -> p n r"), AX, ALU.max).then_inc(step.sem, step.adds(1))
            dve.tensor_tensor(snew[0:NS, :], ps[0:NS, 6, 0:HT], const("newkeys")[0:NS, bass.ds(q * HT, HT)], ALU.add).then_inc(step.sem, step.adds(1))
            dve.wait_ge(step.sem, step.same())
            dve.tensor_tensor(mx_[:, :], mx_[:, :], snew[:, :], ALU.max).then_inc(sem("max_ready"), k["max_ready"].adds(1))
            dve.wait_ge(sem("maxt_ready"), k["maxt_ready"].next())
            dve.tensor_reduce(mcol[:, :], ps[0:HT, 4, 0:P], AX, ALU.max).then_inc(step.sem, step.adds(1))
            dve.wait_ge(step.sem, step.same())
            dve.tensor_scalar(mdiag[:, :], ident[0:HT, 0:HT], mcol[:, 0:1], None, ALU.mult).then_inc(sem("diag_ready"), k["diag_ready"].adds(1))
            dve.wait_ge(sem("maxb_ready"), k["maxb_ready"].next())
            dve.tensor_copy(mb_[:, :], ps[:, 5, 0:HT]).then_inc(step.sem, step.adds(1))
            dve.wait_ge(step.sem, step.same())
            dve.tensor_tensor(pb_[:, 0:NPG, :], all_scores, mb_[:, :].unsqueeze(1).broadcast_to([P, NPG, HT]), ALU.subtract).then_inc(sem("scores_read"), k["scores_read"].adds(1))
            dve.tensor_tensor(pb_[:, NPG, :], snew[:, :], mb_[:, :], ALU.subtract).then_inc(sem("sub_ready"), k["sub_ready"].adds(1))
            dve.wait_ge(sem("probs_ready"), k["probs_ready"].next())
            dve.tensor_reduce(ls_[:, :], pb_[:, :, :].rearrange("p r n -> p n r"), AX, ALU.add).then_inc(sem("part_ready"), k["part_ready"].adds(1))
            dve.wait_ge(sem("olat_ready"), k["olat_ready"].next())
            dve.reciprocal(ri_[:, :], ps[:, 7, 0:HT]).then_inc(step.sem, step.adds(1))
            dve.wait_ge(step.sem, step.same())
            out = olat[:, :, :, bass.ds(q * NT, NT)]
            dve.tensor_tensor(out, ps[:, 6, P:2 * P].rearrange("p (k h t) -> p k h t", k=2, t=NT),
                                                 ri_[:, :].rearrange("p (h t) -> p h t", t=NT).unsqueeze(1).broadcast_to([P, 2, HEADS, NT]), ALU.mult).then_inc(sem("olat_read"), k["olat_read"].adds(1))

        with looped(dve, NB // 2, {k[n]: v for n, v in (("cur_ready", 2), ("gr_turned", 32), ("scores_read", 2), ("scores_ready", 2),
                    ("max_ready", 2), ("maxt_ready", 2), ("diag_ready", 2), ("maxb_ready", 2), ("probs_ready", 2), ("sub_ready", 2),
                    ("part_ready", 2), ("olat_ready", 2), ("olat_read", 2), ("dve_step", 12))} |
                    pairs(k, {"gr_read": 16})) as i:
            sequence(0, i * 2)
            sequence(1, i * 2 + 1)
        dve.wait_ge(sem("os_ready"), k["os_ready"].next())
        dve.tensor_copy(oats[:, :, :], ps[:, 0, 0:256].rearrange("p (j n) -> p j n", n=NS)).then_inc(sem("oats_ready"), k["oats_ready"].adds(1))
        if stop < 7:
            return

        k["unit_done"].n = UNITS[6]

        def squares():
            dve.wait_ge(sem("g_split"), k["g_split"].same())
            for j in range(4):
                dve.wait_ge(sem(f"yt_full{j % 2}"), k[f"yt_full{j % 2}"].next(32))
                dve.tensor_tensor(yz[:, j], yt[j % 2][:, :], gt[j % 2][:, :], ALU.mult).then_inc(sem(f"yt_free{j % 2}"), k[f"yt_free{j % 2}"].adds(1))
                dve.wait_ge(sem(f"yt_free{j % 2}"), k[f"yt_free{j % 2}"].same())
                dve.tensor_tensor(sq4[j], yz[:, j], yz[:, j], ALU.mult).then_inc(sem("ssq_ready"), k["ssq_ready"].adds(1))

        def group_norm(g):
            dve.wait_ge(sem("res_free0"), k["res_free0"].next())
            dve.reciprocal(rsrow[:, :], rsrow[:, :]).then_inc(step.sem, step.adds(1))
            dve.wait_ge(step.sem, step.same())
            for j in range(4):
                dve.scalar_tensor_tensor(out=yz[:, j], in0=yz[:, j], scalar=vecs[:, V_SSM + 4 * g + j:V_SSM + 4 * g + j + 1],
                                                           in1=rsrow[:, :], op0=ALU.mult, op1=ALU.mult).then_inc(sem("yg_ready"), k["yg_ready"].adds(1))

        def group_lo(g):
            for j in range(4):
                dve.wait_ge(sem("g_hi"), k["g_hi"].next())
                dve.tensor_tensor(alo[:, 4 * (g % 2) + j], yz[:, j], ahi[:, 4 * (g % 2) + j].bitcast(F32), ALU.subtract).then_inc(sem("g_split"), k["g_split"].adds(1))

        def att_lo(g, j0):
            for j in range(j0, j0 + 2):
                dve.wait_ge(sem("g_hi"), k["g_hi"].next())
                dve.wait_ge(sem(f"yt_full{j % 2}"), k[f"yt_full{j % 2}"].next(16))
                dve.tensor_tensor(alo[:, 4 * g + j], yt[j % 2][:, :], ahi[:, 4 * g + j].bitcast(F32), ALU.subtract).then_inc(sem(f"yt_free{j % 2}"), k[f"yt_free{j % 2}"].adds(1))

        def merged_lo(e0, e1):
            for e in range(e0, e1):
                dve.wait_ge(sem("g_hi"), k["g_hi"].next())
                dve.tensor_tensor(alo[:, e], mm[:, e], ahi[:, e].bitcast(F32), ALU.subtract).then_inc(sem("g_split"), k["g_split"].adds(1))

        def add_unit(u, how):
            for b in range(2):
                dve.wait_ge(sem("res_half" if b == 0 else "unit_done"), k["res_half" if b == 0 else "unit_done"].next())
                dve.wait_ge(sem(f"res_free{b}"), k[f"res_free{b}"].same())
                how(2 * u + b, b)

        def put(e, b):
            dve.tensor_copy(thirds(mm[:, e]), out3(b)).then_inc(sem(f"res_free{b}"), k[f"res_free{b}"].adds(1))

        def add(e, b):
            dve.tensor_tensor(thirds(mm[:, e]), out3(b), thirds(mm[:, e]), ALU.add).then_inc(sem(f"res_free{b}"), k[f"res_free{b}"].adds(1))

        def add_gated(e, b):
            add(e, b)
            dve.wait_ge(sem(f"res_free{b}"), k[f"res_free{b}"].same())
            dve.wait_ge(sem(f"gt_full{b}"), k[f"gt_full{b}"].next(16))
            dve.tensor_tensor(mm[:, e], mm[:, e], gt[b][:, :], ALU.mult).then_inc(sem(f"gt_free{b}"), k[f"gt_free{b}"].adds(1))

        def gate_add(e, b):
            dve.wait_ge(sem(f"gt_full{b}"), k[f"gt_full{b}"].next(16))
            dve.wait_ge(sem(f"gt_free{b}"), k[f"gt_free{b}"].same())
            dve.tensor_tensor(thirds(sq2[:, b]), out3(b), thirds(gt[b][:, :]), ALU.mult).then_inc(sem(f"res_free{b}"), k[f"res_free{b}"].adds(1))
            dve.wait_ge(sem(f"res_free{b}"), k[f"res_free{b}"].same())
            dve.tensor_tensor(mm[:, e], mm[:, e], sq2[:, b], ALU.add).then_inc(sem(f"gt_free{b}"), k[f"gt_free{b}"].adds(1))

        squares()
        group_norm(0)
        group_lo(0)
        for g in range(3):
            squares()
            how = put if g == 0 else add
            add_unit(0, how)
            add_unit(1, how)
            group_norm(g + 1)
            add_unit(2, how)
            group_lo(g + 1)
            add_unit(3, how)
        for g, how in enumerate((add_gated, gate_add)):
            for u in range(4):
                add_unit(u, how)
                if u < 2:
                    att_lo(g, 2 * u)
        for u in range(4):
            add_unit(u, gate_add)
            if u:
                merged_lo(2 * u - 2, 2 * u)
        merged_lo(6, 8)

        def into_sum(e):
            dve.wait_ge(step.sem, step.same())
            if e == 0:
                dve.tensor_copy(srow[:, :], mm[:, 0]).then_inc(step.sem, step.adds(1))
            else:
                dve.tensor_tensor(srow[:, :], srow[:, :], mm[:, e], ALU.add).then_inc(sem("srow_ready" if e == KT - 1 else "dve_step"), k["srow_ready" if e == KT - 1 else "dve_step"].adds(1))

        for e in range(KT):
            b = e % 2
            dve.wait_ge(sem(f"gt_full{b}"), k[f"gt_full{b}"].next(16))
            dve.wait_ge(sem("unit_done"), k["unit_done"].next())
            dve.wait_ge(sem("g_split"), k["g_split"].same())
            dve.scalar_tensor_tensor(out=thirds(mm[:, e]), in0=thirds(gt[b][:, :]), scalar=ALPHA,
                                                           in1=out3(b), op0=ALU.mult, op1=ALU.add).then_inc(sem(f"res_free{b}"), k[f"res_free{b}"].adds(1))
            dve.wait_ge(sem(f"res_free{b}"), k[f"res_free{b}"].same())
            dve.nop().then_inc(sem(f"gt_free{b}"), k[f"gt_free{b}"].adds(1))
            into_sum(e)

        def layer_norm():
            dve.wait_ge(sem("res_free0"), k["res_free0"].next())
            dve.wait_ge(sem("srow_ready"), k["srow_ready"].same())
            for e in range(KT):
                dve.tensor_tensor(mm[:, e], mm[:, e], murow[:, :], ALU.subtract).then_inc(sem("centred"), k["centred"].adds(1))
            dve.wait_ge(sem("res_free1"), k["res_free1"].next())
            dve.wait_ge(sem("centred"), k["centred"].same())
            dve.reciprocal(rsrow[:, :], rsrow[:, :]).then_inc(step.sem, step.adds(1))
            dve.wait_ge(step.sem, step.same())
            for e in range(KT):
                dve.tensor_tensor(mm[:, e], mm[:, e], rsrow[:, :], ALU.mult).then_inc(sem("scaled"), k["scaled"].adds(1))

        layer_norm()
        for e in range(KT):
            dve.wait_ge(sem("g_hi"), k["g_hi"].next())
            dve.tensor_tensor(alo[:, e], mm[:, e], ahi[:, e].bitcast(F32), ALU.subtract).then_inc(sem("g_split"), k["g_split"].adds(1))
        dve.wait_ge(sem("g_split"), k["g_split"].same())
        for e in range(KT):
            dve.tensor_scalar(mm[:, e], mm[:, e], ALPHA, None, ALU.mult).then_inc(step.sem, step.adds(1))

        def hidden(v):
            for j in range(2):
                dve.wait_ge(sem("unit_done"), k["unit_done"].next(2))
                dve.wait_ge(sem("res_free0"), k["res_free0"].next())
                dve.wait_ge(sem("f_split"), k["f_split"].same())
                dve.tensor_tensor(thirds(ff[j][:, :]), out3(1), thirds(fg[j]), ALU.mult).then_inc(sem("res_free1"), k["res_free1"].adds(1))
            for j in range(2):
                dve.wait_ge(sem("f_hi"), k["f_hi"].next())
                dve.tensor_tensor(flo[:, 2 * v + j], ff[j][:, :], fhi[:, 2 * v + j].bitcast(F32), ALU.subtract).then_inc(sem("f_split"), k["f_split"].adds(1))

        def down(last=False):
            for e in range(KT):
                dve.wait_ge(sem("res_half" if e % 4 < 3 else "unit_done"), k["res_half" if e % 4 < 3 else "unit_done"].next())
                if e == 0:
                    dve.wait_ge(sem("res_free1"), k["res_free1"].same())
                    dve.wait_ge(step.sem, step.same())
                    dve.wait_ge(sem("f_split"), k["f_split"].same())
                add(e, e % 2)
                if last:
                    dve.wait_ge(sem(f"res_free{e % 2}"), k[f"res_free{e % 2}"].same())
                    into_sum(e)

        hidden(0)
        with looped(dve, (NF - 1) // 2, {k["unit_done"]: 12, k["res_half"]: 12, k["f_hi"]: 4, k["f_split"]: 4,
                                         k["res_free0"]: 12, k["res_free1"]: 12}):
            for v in range(2):
                hidden(1 - v)
                down()
        down(True)
        layer_norm()
        for i in range(9):
            n = P if i < 8 else NS
            dve.wait_ge(sem("tok_turned"), k["tok_turned"].next())
            dve.wait_ge(sem(f"tok_stored{i % 2}"), k[f"tok_stored{i % 2}"].held(16))
            dve.tensor_copy(ytok[i % 2][0:n, 512:1024], ps[0:n, 2 * (i % 2) + 1, :]).then_inc(sem(f"bank_read{i % 2}"), k[f"bank_read{i % 2}"].adds(1))

    ctx.close()


def kernel(**inputs):
    import numpy as _np
    import concourse.bacc as _bacc
    from concourse import mybir as _mybir
    from concourse.bass_utils import run_bass_kernel_spmd as _run

    table, _, rope = constants()
    inputs["table"], inputs["rope"] = table, rope
    nc = _bacc.Bacc("TRN2", target_bir_lowering=False, num_devices=1)
    arrays, ins, outs = {}, {}, {}
    for name in inputs:
        arrays[f"in_{name}"] = _np.ascontiguousarray(inputs[name])
        ins[name] = nc.dram_tensor(f"in_{name}", arrays[f"in_{name}"].shape,
                                   _mybir.dt.from_np(arrays[f"in_{name}"].dtype), kind="ExternalInput").ap()
    for name, shape in OUTS.items():
        outs[name] = nc.dram_tensor(f"out_{name}", shape, _mybir.dt.float32, kind="ExternalOutput").ap()
    build(nc, ins, outs)
    r = _run(nc, [arrays], core_ids=[0])
    return tuple(r.results[0][f"out_{name}"] for name in OUTS)
```

```python
from contextlib import ExitStack, contextmanager
import math

import numpy as np
import concourse.bass as bass
from concourse import mybir

F32 = mybir.dt.float32
F32R = mybir.dt.float32r
BF16 = mybir.dt.bfloat16
I32 = mybir.dt.int32
ALU = mybir.AluOpType
ACT = mybir.ActivationFunctionType
AX = mybir.AxisListType.X

P = 128
D_MODEL, SEQ, NB, NT = 1024, 1024, 8, 4
NS = NB * NT
TOK = SEQ + NS
CH = TOK // 3
HEADS, NOPE, ROPE, VH = 16, 64, 32, 64
QH = NOPE + ROPE
QL, KL = 384, 256
PAGE, PAST = 128, 4096
NPG = PAST // PAGE
DI, SH, SP_, SG, SN = 2048, 32, 64, 4, 128
CONV, CW = DI + 2 * SG * SN, 4
FF = 2816
ALPHA = 2.0 ** 0.25
SCALE = QH ** -0.5
KT = D_MODEL // P
C_Q, C_KV, C_PE = 0, QL, QL + KL
C_Z = C_PE + ROPE
C_XBC = C_Z + DI
C_DT = C_XBC + CONV
C_G = C_DT + SH
UNIT = 1024
RAW, SPLIT = 4, 2


class Tally:

    def __init__(self, sem):
        self.sem, self.n, self.loops = sem, 0, []

    def value(self, back=0):
        v = self.n - back
        for reg, per, _ in self.loops:
            v = reg * per + v
        return v

    def adds(self, by):
        self.n += by
        return by

    def next(self, by=1):
        self.n += by
        return self.value()

    def same(self):
        return self.value()

    def held(self, by=1):
        self.n += by
        return self.value(by)

    def ahead(self):
        return self.value(-1)


def pairs(k, d):
    return {k[f"{n}{b}"]: v for n, v in d.items() for b in range(2)}


@contextmanager
def looped(eng, count, per):
    begun = {t: t.n for t in per}
    with eng.Fori(0, count) as i:
        for t, p in per.items():
            t.loops.append((i, p, t.n))
        yield i
    wrong = {t.sem.name: t.n - begun[t] for t, p in per.items() if t.n - begun[t] != p}
    assert not wrong, wrong
    for t, p in per.items():
        t.loops.pop()
        t.n += p * (count - 1)


UNITS = {1: 6, 2: 18, 3: 74, 4: 74, 5: 74, 6: 74}
TOTAL_UNITS = 74 + 6 * 4 + 8 + 6 * (FF // 256)


def constants():
    half = ROPE // 2
    inv = (np.float32(10000.0) ** (-np.arange(0, ROPE, 2, dtype=np.float32) / np.float32(ROPE))).astype(np.float32)
    pos = np.concatenate([np.arange(SEQ), np.tile(PAST + np.arange(NT), NB)]).astype(np.float32)
    ang = (inv[:, None] * pos[None, :]).astype(np.float32)
    rope = np.zeros((2, P, TOK), np.float32)
    rope[0, NOPE:QH] = np.tile(np.cos(ang), (2, 1))
    rope[1, NOPE:QH] = np.tile(np.sin(ang), (2, 1))
    c = {"ident": np.eye(P), "ones": np.ones((P, P))}
    at = np.arange(P)
    c["causal"] = (at[:, None] <= at[None, :]) * 1.0
    s = np.arange(NS)
    same = (s[:, None] // NT == s[None, :] // NT)
    c["causal_s"] = np.zeros((P, NS))
    c["causal_s"][:NS] = same & (s[:, None] <= s[None, :])
    c["same_s"] = np.zeros((P, NS))
    c["same_s"][:NS] = same
    c["after"] = np.where(at[None, :] <= at[:, None], 0.0, -1e30)
    c["turn"] = np.zeros((P, ROPE))
    for i in range(half):
        c["turn"][NOPE + half + i, i] = -1.0
        c["turn"][NOPE + i, half + i] = 1.0
    c["spread"] = np.zeros((P, DI // P, P))
    for h in range(SH):
        c["spread"][h, h // 2, 64 * (h % 2):64 * (h % 2) + 64] = 1.0
    c["quarter"] = (at % 4)[:, None] * 1.0
    c["batch"] = np.zeros((P, NB))
    c["batch"][s, s // NT] = 1.0
    c["newkeys"] = np.full((P, NB, HEADS, NT), -1e30)
    for i in s:
        for t in range(i % NT, NT):
            c["newkeys"][i, i // NT, :, t] = 0.0
    names = ["ident", "ones", "causal", "causal_s", "same_s", "after", "turn", "spread", "quarter", "batch", "newkeys"]
    parts = [c[n].reshape(P, -1).astype(np.float32) for n in names]
    where, at = {}, 0
    for n, a in zip(names, parts):
        where[n] = (at, a.shape[1])
        at += a.shape[1]
    return np.ascontiguousarray(np.concatenate(parts, 1)), where, rope


OUTS = {"y_prompt": (1, SEQ, D_MODEL), "y_sample": (NB, NT, D_MODEL), "ckv_prompt": (1, 1, SEQ, KL),
        "kpe_prompt": (1, 1, SEQ, ROPE), "ssm_prompt": (1, 1, SH, SP_, SN), "conv_prompt": (1, 1, CW - 1, CONV),
        "ckv_sample": (1, NB, NT, KL), "kpe_sample": (1, NB, NT, ROPE), "ssm_sample": (1, NB, SH, SP_, SN),
        "conv_sample": (1, NB, CW - 1, CONV)}


def build(nc, a, o, stop=99, debug=None):
    sems = {}
    taken = {"yt_full0": ("x_full0", 48), "yt_full1": ("x_full1", 32), "gt_full0": ("st_full", 48),
             "gt_full1": ("rope_full", 32), "tok_stored0": ("x_stored", 32), "tok_stored1": ("prep_full", 48),
             "tok_turned": ("x_turned", 9), "g_hi": ("x_hi", 9), "g_split": ("x_split", 9),
             "affine_ready": ("keys_turned", 9), "scaled": ("keys_out", 9), "centred": ("crow_turned", 6),
             "mean_ready": ("crow_ready", 6), "srow_ready": ("kn_split", 2), "yg_ready": ("qn_split", 3),
             "f_hi": ("cw_ready", 2), "f_split": ("st_turned", 2), "bank_read0": ("vecs_ready", 2),
             "bank_read1": ("qn_hi", 3), "ssq_ready": ("sq_ready", 5), "ssq_used": ("sq_used", 5),
             "res_half": ("x_whole", 8), "res_free0": ("half_done", 8), "res_free1": ("key_turned", 1),
             "yt_free0": ("qn_normed", 3), "yt_free1": ("kn_normed", 2), "gt_free0": ("q_turned", 16),
             "gt_free1": ("v_turned", 16), "step_full2": ("keys_stored0", 192), "step_full3": ("keys_stored1", 160),
             "step_full4": ("q_stored0", 144), "si_full2": ("k_stored0", 144), "si_full3": ("k_stored1", 144),
             "new_stored2": ("v_stored0", 144), "new_stored3": ("v_stored1", 144), "ec_ready": ("rot_ready", 17),
             "state_read": ("kn_hi", 2), "xe_ready": ("drow_wide", 1), "xd_ready": ("vecs_turned", 1)}

    def sem(name):
        if name in taken:
            return sem(taken[name][0])
        if name not in sems:
            sems[name] = nc.alloc_semaphore(name)
        return sems[name]

    credit = {f"{name}{b}": by for name, by in (("keys_stored", 32), ("q_stored", 16), ("k_stored", 16),
                                                ("v_stored", 16), ("v_free", 1), ("cv_free", 1),
                                                ("so_stored", 16), ("zo_stored", 16),
                                                ("y_out", 3), ("y_stored", 16), ("pre_read", 2),
                                                ("new_out", 2), ("new_stored", 16),
                                                ("s_read", 1), ("o_read", 1), ("pt_read", 1),
                                                ("gr_read", 2))
              for b in range(2)} | {"st_stored": 16, "att_stored": 16, "t_ready0": 1, "olat_read": 1}

    class Counts(dict):

        def __missing__(self, name):
            self[name] = Tally(sem(name))
            self[name].n = taken[name][1] if name in taken else credit.get(name, 0)
            return self[name]

    def scratch(name, shape):
        if debug is not None and name in debug:
            return nc.dram_tensor(name, shape, F32, kind="ExternalOutput").ap()
        return nc.dram_tensor(name, shape, F32, kind="Internal").ap()

    base = -(-nc.sbuf_base // 64) * 64

    class Arena:

        def __init__(self, at):
            self.at = at

        def __call__(self, name, shape, dt=F32):
            size = 2 if dt == BF16 else 4
            n = size * math.prod(shape[1:])
            t = nc.alloc_sbuf_tensor_at(name, list(shape), dt, offset=self.at)
            self.at += -(-n // 64) * 64
            assert self.at <= nc.sbuf_usable_end, (name, self.at)
            return t

    fixed = Arena(base)
    raw = fixed("raw", [P, RAW, UNIT])
    whi = [fixed(f"whi{s}", [P, UNIT], F32R) for s in range(SPLIT)]
    wlo = [fixed(f"wlo{s}", [P, UNIT], F32R) for s in range(SPLIT)]
    table, where, _ = constants()
    cst = fixed("cst", [P, table.shape[1]])
    vecs = fixed("vecs", [P, 96])
    dskip = fixed("dskip", [P, DI // P])
    epsc = fixed("epsc", [P, 4])
    xhi = fixed("xhi", [P, KT, TOK], F32R)
    xlo = fixed("xlo", [P, KT, TOK], F32R)
    floor = fixed.at

    def const(name):
        at, n = where[name]
        return cst[:, at:at + n]

    ident, ones = const("ident"), const("ones")
    V_GATE, V_QN, V_KVN, V_SSM, V_L1G, V_L1B, V_L2G, V_L2B, V_END = 0, 16, 19, 21, 37, 45, 53, 61, 69

    ps = nc.alloc_psum_tensor("ps", [P, 8, 512], F32)

    def out3(b, n=P):
        return ps[0:n, 3 * b:3 * b + 3, 0:CH]

    def thirds(ap):
        return ap.rearrange("p (c n) -> p c n", c=3)

    d_xbc = scratch("d_xbc", [CONV, TOK])
    d_z = scratch("d_z", [DI, TOK])
    d_g = scratch("d_g", [2 * D_MODEL, TOK])
    d_q = scratch("d_q", [HEADS, QH, TOK])
    d_k = scratch("d_k", [HEADS, NOPE, SEQ])
    d_v = scratch("d_v", [HEADS, P, SEQ // P * VH])
    d_kr = scratch("d_kr", [ROPE, TOK])
    d_kvs = scratch("d_kvs", [KL, NS])
    d_small = scratch("d_small", [SH, TOK])
    d_y = scratch("d_y", [DI, TOK])
    d_att = scratch("d_att", [HEADS * VH, TOK])
    d_acum = scratch("d_acum", [SH, TOK])
    d_x = scratch("d_x", [D_MODEL, TOK])

    w_in = a["w_in"][0]
    w_uq, w_ukv = a["w_uq"][0], a["w_ukv"][0]
    w_a, w_b, w_o = a["w_branch_a"][0], a["w_branch_b"][0], a["w_out"][0]
    w_g, w_u, w_d = a["w_ffn_gate"][0], a["w_ffn_up"][0], a["w_ffn_down"][0]

    ar = Arena(floor)
    xst = [ar(f"xst{b}", [P, D_MODEL]) for b in range(4)]
    rows = ar("rows", [V_END, P])
    drow = ar("drow", [DI // P, 2])
    drow2 = ar("drow2", [DI // P, P])
    ar = Arena(floor)
    small = ar("small", [P, TOK])
    cq = ar("cq", [P, 3, TOK])
    ckv = ar("ckv", [P, 2, TOK])
    qn_hi, qn_lo = ar("qn_hi", [P, 3, TOK], F32R), ar("qn_lo", [P, 3, TOK], F32R)
    kn_hi, kn_lo = ar("kn_hi", [P, 2, TOK], F32R), ar("kn_lo", [P, 2, TOK], F32R)
    rope_t = ar("rope_t", [P, 2, TOK])
    sq = ar("sq", [P, 2, TOK])
    rs = ar("rs", [P, 2, TOK])
    tokst = [sq[:, b, 0:KL + ROPE] for b in range(2)]
    qh = [cq[:, 0], cq[:, 1]]
    kvh = [ckv[:, b, 0:SEQ] for b in range(2)]
    vst = [cq[:, 2, b * 512:(b + 1) * 512] for b in range(2)]
    rot = [rs[:, b] for b in range(2)]
    R0, R1 = NOPE, QH

    ar = Arena(floor + 6 * 64 * (-(-TOK * 4 // 64)))
    NCONV = CONV // P
    st = ar("st", [CW + 1 + NB * (CW - 1), CONV])
    cw = ar("cw", [P, NCONV, CW + 1 + NB * (CW - 1)])
    xraw = [ar(f"xraw{b}", [P, CW - 1 + TOK]) for b in range(2)]
    xs7 = [ar(f"xs7{b}", [P, NB, CW - 1 + NT]) for b in range(2)]
    cv = [ar(f"cv{b}", [P, TOK]) for b in range(2)]
    so = [ar(f"so{b}", [P, TOK]) for b in range(2)]
    ccol = ar("ccol", [P, NCONV, (NB + 1) * (CW - 1)])
    crow = ar("crow", [(NB + 1) * (CW - 1), CONV])
    ar = Arena(floor)
    zo = [ar(f"zo{b}", [P, TOK]) for b in range(2)]
    xo = ar("xo", [P, 4, TOK])

    low = floor - 2 * 64 * (-(-KT * TOK * 4 // 64))
    ar = Arena(low)
    dtr = ar("dtr", [SH, TOK])
    act_ = ar("act_", [SH, TOK])
    hb = ar("hb", [P, 2, SH])
    dt_, da, acs, dte, cdb, sp_u, sp_z, sp_w, sp_p = (ar(n, [P, 9, SH]) for n in
        ("dt_", "da", "acs", "dte", "cdb", "sp_u", "sp_z", "sp_w", "sp_p"))
    cdp = ar("cdp", [P, DI // P, NB])
    HG = SH // SG
    LOADS = 4
    widths = [P] * LOADS + [NS]
    s_x = [ar(f"s_x{b}", [P, 4, n]) for b, n in enumerate(widths)]
    s_b = [ar(f"s_b{b}", [P, n]) for b, n in enumerate(widths)]
    s_c = [ar(f"s_c{b}", [P, n]) for b, n in enumerate(widths)]
    s_a = [ar(f"s_a{b}", [P, HG, n]) for b, n in enumerate(widths)]
    s_g = [ar(f"s_g{b}", [P, HG, P]) for b in range(2)]
    s_e = [ar(f"s_e{b}", [P, HG, P]) for b in range(2)]
    s_xd = [ar(f"s_xd{b}", [P, HG, SP_]) for b in range(2)]
    s_xe = [ar(f"s_xe{b}", [P, HG, SP_]) for b in range(2)]
    s_bt = [ar(f"s_bt{b}", [P, P]) for b in range(2)]
    s_cb = [ar(f"s_cb{b}", [P, P]) for b in range(2)]
    s_y = [ar(f"s_y{b}", [P, 4, P]) for b in range(2)]
    state = ar("state", [P, HG, SP_])
    stout = ar("stout", [P, 4, P])
    s_in = [ar(f"s_in{b}", [P, 4, P]) for b in range(LOADS)]
    s_it = [ar(f"s_it{b}", [P, 4, P]) for b in range(2)]
    s_u = [ar(f"s_u{b}", [NS, HG * SP_]) for b in range(2)]
    s_new = [ar(f"s_new{b}", [P, 4, P]) for b in range(LOADS)]

    ar = Arena(low)
    QG = NB * HEADS
    HT = HEADS * NT
    kvb = [ar("kvb0", [P, NPG, KL]), None]
    kpb = [ar("kpb0", [P, NPG, ROPE]), None]
    at_wkv = ar.at
    wkv = ar("wkv", [P, 2, HEADS * P])
    ukt = ar("ukt", [NOPE, HEADS, KL])
    qs = ar("qs", [NOPE, HEADS, NS])
    qps = ar("qps", [ROPE, HEADS, NS])
    qpb = ar("qpb", [ROPE, NB, HT])
    qlat = ar("qlat", [P, 2, NB, HT])
    olat = ar("olat", [P, 2, HEADS, NS])
    kns = ar("kns", [P, 2, NS])
    krs = ar("krs", [ROPE, NS])
    kts = ar("kts", [NS, KL])
    pgi, pgf = ar("pgi", [P, NB], I32), ar("pgf", [P, NB])
    pgx = ar("pgx", [P, NB], mybir.dt.uint32)
    oats = ar("oats", [P, HEADS // 2, NS])
    kvt = [ar(f"kvt{b}", [P, 4, P]) for b in range(2)]
    kpt = [ar(f"kpt{b}", [ROPE, 2, P]) for b in range(2)]
    pb_ = ar("pb_", [P, NPG + 1, HT])
    mx5 = ar("mx5", [P, 5, HT])
    snew = mx5[:, 4]
    mx_, mb_, ls_ = (ar(n, [P, HT]) for n in ("mx_", "mb_", "ls_"))
    ri_ = ar("ri_", [HT, 1])
    oseq = ar("oseq", [HT, NB, KL])
    CK = NPG // 4
    mcol = ar("mcol", [HT, 1])
    mdiag = ar("mdiag", [HT, HT])
    qcur = ar("qcur", [P, 2, HT])
    qpcur = ar("qpcur", [ROPE, HT])
    at_g = ar.at
    kvb[1], kpb[1] = ar("kvb1", [P, NPG, KL]), ar("kpb1", [P, NPG, ROPE])
    ar = Arena(at_g)
    qb = [ar(f"qb{b}", [QH, SEQ]) for b in range(2)]
    kb = [ar(f"kb{b}", [QH, SEQ]) for b in range(2)]
    vb = [ar(f"vb{b}", [P, SEQ // P, VH]) for b in range(2)]
    pr = [ar(f"pr{b}", [P, SEQ]) for b in range(2)]
    ptb = [ar(f"ptb{b}", [P, SEQ]) for b in range(2)]
    ob = ar("ob", [P, SEQ // P, 2 * VH])
    att = ar("att", [P, SEQ])
    rowmax, negmax, rowsum, rowinv = (ar(n, [P, 16]) for n in ("rowmax", "negmax", "rowsum", "rowinv"))
    ident_b, after_b = ar("ident_b", [P, P], BF16), ar("after_b", [P, P], BF16)
    NQ = SEQ // P
    ar = Arena(low)
    yt = [ar(f"yt{b}", [P, TOK]) for b in range(2)]
    gt = [ar(f"gt{b}", [P, TOK]) for b in range(2)]
    yz = ar("yz", [P, 4, TOK])
    assert ar.at <= at_wkv
    ahi, alo = ar("ahi", [P, KT, TOK], F32R), ar("alo", [P, KT, TOK], F32R)
    mm = ar("mm", [P, KT, TOK])
    assert ar.at >= at_g
    srow, sq2, murow, rsrow = ar("srow", [P, TOK]), ar("sq2", [P, 2, TOK]), ar("murow", [P, TOK]), ar("rsrow", [P, TOK])
    ar = Arena(low)
    fhi, flo = ar("fhi", [P, 4, TOK], F32R), ar("flo", [P, 4, TOK], F32R)
    sq4 = [sq2[:, 0], sq2[:, 1], srow[:, :], murow[:, :]]
    fg = [sq2[:, 0], sq2[:, 1]]
    ff = [srow, rsrow]
    ytok = [Arena(low + 9 * 4096 + b * 4096)(f"ytok{b}", [P, D_MODEL]) for b in range(2)]
    NF = FF // 256

    block = nc.Block()
    o_ckv = [o["ckv_prompt"][0, 0], o["ckv_sample"][0].rearrange("b t c -> (b t) c")]
    o_kpe = [o["kpe_prompt"][0, 0], o["kpe_sample"][0].rearrange("b t c -> (b t) c")]

    ctx = ExitStack()
    ctx.enter_context(block)

    @block.sync
    def _(sp):
        k = Counts()
        for name, by in credit.items():
            sp.sem_inc(sem(name), by)
        first = where["ones"][0] + where["ones"][1]
        sp.dma_start(cst[:, 0:first], a["table"][:, 0:first]).then_inc(sem("ident_full"), 16)

        unit = [0]

        def weights(pieces):
            s = unit[0] % RAW
            if unit[0] >= RAW:
                sp.wait_ge(sem("unit_split"), k["unit_split"].next())
            for view, src in pieces:
                sp.dma_start(view(raw[:, s]), src).then_inc(sem(f"raw_full{s}"), k[f"raw_full{s}"].adds(16))
            unit[0] += 1

        def columns(n):
            return lambda r: r.rearrange("p (k n) -> p k n", n=n)

        def tile_of(w, col, n=P):
            return w[:, bass.ds(col, n)].rearrange("(k p) n -> p k n", p=P)

        def x_tile(t):
            src = a["x_prompt"][0, t * P:(t + 1) * P, :] if t < 8 else a["x_sample"].rearrange("b t d -> (b t) d")
            sp.dma_start(xst[t % 4][0:src.shape[0], :], src).then_inc(sem(f"x_full{t % 4}"), k[f"x_full{t % 4}"].adds(16))

        for t in range(4):
            x_tile(t)
        for name, at, n in (("b_gate", V_GATE, 16), ("q_norm_g", V_QN, 3), ("kv_norm_g", V_KVN, 2),
                            ("ssm_norm_g", V_SSM, 16), ("ln1_g", V_L1G, 8), ("ln1_b", V_L1B, 8),
                            ("ln2_g", V_L2G, 8), ("ln2_b", V_L2B, 8)):
            sp.dma_start(rows[at:at + n, :], a[name][0].rearrange("(n p) -> n p", p=P)).then_inc(sem("rows_full"), 16)
        sp.dma_start(drow[:, :], a["d_skip"][0].rearrange("(n p) -> n p", p=2)).then_inc(sem("rows_full"), 16)
        for t in range(4, 9):
            sp.wait_ge(sem("x_turned"), k["x_turned"].next())
            x_tile(t)

        def small_unit():
            def part(j):
                return lambda r: r.rearrange("p (k n) -> p k n", n=P)[:, :, 32 * j:32 * j + 32]
            weights([(part(0), tile_of(w_in, C_DT, 32)), (part(1), tile_of(w_in, C_DT, 32)),
                     (part(2), tile_of(w_in, C_PE, 32)), (part(3), tile_of(w_in, C_PE, 32))])

        small_unit()
        for j in range(3):
            weights([(columns(P), tile_of(w_in, C_Q + j * P))])
        sp.dma_start(cst[:, first:], a["table"][:, first:]).then_inc(sem("cst_full"), 16)

        for j in range(2):
            weights([(columns(P), tile_of(w_in, C_KV + j * P))])
        for j in range(2):
            sp.dma_start(rope_t[R0:R1, j, :], a["rope"][j, R0:R1, :]).then_inc(sem("rope_full"), k["rope_full"].adds(16))
        with looped(sp, 2, {k["unit_split"]: 4} | {k[f"raw_full{s}"]: 16 for s in range(RAW)}) as i:
            for j in range(4):
                weights([(lambda r: r[:, 0:3 * 2 * QH].rearrange("p (k n) -> p k n", k=3),
                          tile_of(w_uq, (i * 4 + j) * 2 * QH, 2 * QH))])
        unit[0] += 4
        for j in range(4):
            weights([(columns(512), tile_of(w_ukv, j * 512, 512))])
        if stop < 3:
            return
        sp.wait_ge(sem("unit_done"), 14)
        sp.dma_start(st[0:CW, :], a["conv_w"][0]).then_inc(sem("st_full"), 16)
        sp.dma_start(st[CW:CW + 1, :], a["conv_b"]).then_inc(sem("st_full"), 16)
        sp.dma_start(st[CW + 1:, :], a["state_conv"][0].rearrange("b t c -> (b t) c")).then_inc(sem("st_full"), 16)
        all_raw = {k["unit_split"]: 4} | {k[f"raw_full{s}"]: 16 for s in range(RAW)}
        for col, n in ((C_XBC, CONV), (C_Z, DI), (C_G, 2 * D_MODEL)):
            with looped(sp, n // P // 4, all_raw) as i:
                for j in range(4):
                    weights([(columns(P), tile_of(w_in, (i * 4 + j) * P + col))])
            unit[0] += n // P - 4
        if stop < 4:
            return

        sp.wait_ge(sem("unit_done"), 74)
        for b in range(2):
            sp.wait_ge(sem(f"zo_stored{b}"), 17 * 16)
        sp.dma_start(dtr[:, :], d_small).then_inc(sem("prep_full"), k["prep_full"].adds(16))
        sp.dma_start(hb[:, 0], a["dt_bias"][0].partition_broadcast(P)).then_inc(sem("prep_full"), k["prep_full"].adds(16))
        sp.dma_start(hb[:, 1], a["a_log"][0].partition_broadcast(P)).then_inc(sem("prep_full"), k["prep_full"].adds(16))
        sp.wait_ge(sem("so_stored0"), 13 * 16)
        sp.wait_ge(sem("so_stored1"), 13 * 16)
        sp.wait_ge(sem("acum_stored"), 16)
        sp.wait_ge(sem("x_stored"), 32)

        def step(c, g, n=P):
            b, l = c % 2, c % LOADS if c < 8 else LOADS
            last_use = k[f"y_out{b}"].held() - ((2, 1, 2, 1, 1, 1, 1, 1, 4)[c])
            sp.wait_ge(sem(f"y_out{b}"), last_use)
            at = slice(c * P, c * P + n)
            for dst, src in ((s_x[l][:, :, 0:n], d_xbc[bass.ds(g * 512, 512), at].rearrange("(j p) n -> p j n", p=P)),
                             (s_b[l][:, 0:n], d_xbc[bass.ds(g * P + DI, P), at]),
                             (s_c[l][:, 0:n], d_xbc[bass.ds(g * P + DI + SG * SN, P), at]),
                             (s_a[l][:, :, 0:n], d_acum[bass.ds(g * HG, HG), at].partition_broadcast(P))):
                sp.dma_start(dst, src).then_inc(sem(f"step_full{l}"), k[f"step_full{l}"].adds(16))

        with looped(sp, SG, {k["y_out0"]: 5, k["y_out1"]: 4, k["step_full4"]: 64, k["new_out0"]: 4, k["new_out1"]: 4} |
                            {k[f"{n}{l}"]: by for l in range(LOADS) for n, by in (("step_full", 128), ("si_full", 32))}) as g:
            for c in range(8):
                step(c, g)
            step(8, g, NS)
            for q in range(NB):
                sp.wait_ge(sem(f"new_out{q % 2}"), k[f"new_out{q % 2}"].held() - 1)
                src = a["state_ssm"][0, q].rearrange("h p n -> (h p) n")
                sp.dma_start(s_in[q % LOADS][:, :, :], src[bass.ds(g * 512, 512), :].rearrange("(j p) n -> p j n", p=P)).then_inc(sem(f"si_full{q % LOADS}"), k[f"si_full{q % LOADS}"].adds(16))
        if stop < 5:
            return

        sp.wait_ge(sem("ssm_over"), 1)
        for b in range(2):
            sp.dma_start(kb[b][NOPE:QH, :], d_kr[:, 0:SEQ]).then_inc(sem("kr_full"), k["kr_full"].adds(16))

        def head(b, h):
            one = lambda d: d[bass.ds(h, 1)].rearrange("a p n -> (a p) n")
            sp.dma_start(qb[b][:, :], one(d_q)[:, 0:SEQ]).then_inc(sem(f"head_full{b}"), k[f"head_full{b}"].adds(16))
            sp.dma_start(kb[b][0:NOPE, :], one(d_k)).then_inc(sem(f"head_full{b}"), k[f"head_full{b}"].adds(16))
            sp.dma_start(vb[b][:, :, :].rearrange("p a n -> p (a n)"), one(d_v)).then_inc(sem(f"head_full{b}"), k[f"head_full{b}"].adds(16))

        head(0, 0)
        head(1, 1)
        with nc.allow_non_contiguous_dma(reason="a page number for each quarter page, 4 KB in all"):
            for q in range(NB):
                src = a["page_table"][q].unsqueeze(1).broadcast_to([NPG, P // NPG])
                sp.dma_start(pgi[:, q:q + 1], src).then_inc(sem("pages_full"), k["pages_full"].adds(16))
            for dst, src in ((wkv[:, :, :], w_ukv.rearrange("(k p) n -> p k n", p=P)),
                             (qs[:, :, :], d_q[:, 0:NOPE, SEQ:TOK].rearrange("h p n -> p h n")),
                             (qps[:, :, :], d_q[:, NOPE:QH, SEQ:TOK].rearrange("h p n -> p h n")),
                             (kns[:, :, :], d_kvs.rearrange("(k p) n -> p k n", p=P)),
                             (krs[:, :], d_kr[:, SEQ:TOK]), (kts[:, :], o_ckv[1])):
                sp.dma_start(dst, src).then_inc(sem("late_full"), k["late_full"].adds(16))
        with looped(sp, HEADS // 2 - 1, {k["o_ready"]: 16} | pairs(k, {"head_full": 48})) as i:
            for b in range(2):
                sp.wait_ge(sem("o_ready"), k["o_ready"].next(NQ))
                head(b, i * 2 + 2 + b)
        if stop < 7:
            return

        to_load = []

        def row_units(w, row, rows_, cols):
            return [[(columns(cols), w[bass.ds(row, rows_), c:c + cols].rearrange("(k p) n -> p k n", p=P))]
                    for c in range(0, D_MODEL, cols)]

        def gate_up(blk):
            return [[(columns(P), tile_of(w, blk * 256 + j * P))] for j in range(2) for w in (w_g, w_u)]

        def next_weights(n):
            for _ in range(n):
                weights(to_load.pop(0))

        for g in range(4):
            to_load += row_units(w_b, g * 512, 512, 256)
        for g in range(2):
            to_load += row_units(w_a, g * 512, 512, 256)
        to_load += [[(columns(P), tile_of(w_o, e * P))] for e in range(KT)] + gate_up(0)
        next_weights(4)
        sp.wait_ge(sem("olat_read"), 1 + NB - 1)

        def load_tile(name, buffer, j, src):
            sp.wait_ge(sem(f"{name}_free{j % 2}"), k[f"{name}_free{j % 2}"].held())
            sp.dma_start(buffer[j % 2][:, :], src).then_inc(sem(f"{name}_full{j % 2}"), k[f"{name}_full{j % 2}"].adds(16))

        def y_and_z(g):
            for j in range(4):
                at = slice((g * 4 + j) * P, (g * 4 + j + 1) * P)
                load_tile("yt", yt, j, d_y[at, :])
                sp.dma_start(gt[j % 2][:, :], d_z[at, :]).then_inc(sem(f"yt_full{j % 2}"), k[f"yt_full{j % 2}"].adds(16))

        def att_tile(g, j):
            if g == j == 0:
                sp.wait_ge(sem("samples_over"), 1)
            load_tile("yt", yt, j, d_att[(g * 4 + j) * P:(g * 4 + j + 1) * P, :])

        def features(d, row, units, att_g=None):
            for e in range(0, KT, 2):
                if att_g is not None and e in (0, 4):
                    for j in range(2):
                        att_tile(att_g, e // 2 + j)
                for j in range(2):
                    load_tile("gt", gt, j, d[row + (e + j) * P:row + (e + j + 1) * P, :])
                next_weights(units)

        y_and_z(0)
        for g in range(1, 4):
            y_and_z(g)
            next_weights(4)
        for b in range(2):
            sp.wait_ge(sem(f"yt_free{b}"), k[f"yt_free{b}"].same())
        features(d_g, D_MODEL, 1, 0)
        features(d_g, 0, 1, 1)
        features(d_g, 0, 1)
        features(d_x, 0, 2)

        with looped(sp, (NF - 1) // 2, {k["unit_split"]: 12} | {k[f"raw_full{s}"]: 48 for s in range(RAW)}) as i:
            for v in range(2):
                to_load += gate_up(i * 2 + v + 1) + row_units(w_d, (i * 2 + v) * 256, 256, 512)
                next_weights(6)
        unit[0] += 12 * ((NF - 1) // 2 - 1)
        to_load += row_units(w_d, (NF - 1) * 256, 256, 512)
        next_weights(2)

    @block.gpsimd
    def _(pool):
        k = Counts()
        pool.memset(epsc[:, 0:1], 1e-6)
        pool.memset(epsc[:, 1:2], 1e-5).then_inc(sem("eps_ready"), 1)
        pool.wait_ge(sem("ident_full"), 16)

        def split(u, s, first=False):
            pool.wait_ge(sem(f"raw_full{u}"), k[f"raw_full{u}"].next(16 * (4 if first else 1)))
            if k["unit_split"].n >= SPLIT or k["unit_split"].loops:
                pool.wait_ge(sem("unit_done"), k["unit_done"].next())
            pool.tensor_tensor(whi[s][:, :], raw[:, u], ones[:, 0:1].broadcast_to([P, UNIT]), ALU.mult).then_inc(sem("unit_hi"), k["unit_hi"].adds(1))
            pool.wait_ge(sem("unit_hi"), k["unit_hi"].same())
            pool.tensor_tensor(wlo[s][:, :], raw[:, u], whi[s][:, :].bitcast(F32), ALU.subtract).then_inc(sem("unit_split"), k["unit_split"].adds(1))

        split(0, 0, True)
        for u in range(1, 4):
            split(u % RAW, u % SPLIT)

        def split_units(first, end):
            turns, rest = divmod(end - first, RAW)
            if turns:
                with looped(pool, turns, {k["unit_split"]: 4, k["unit_hi"]: 4, k["unit_done"]: 4} |
                            {k[f"raw_full{s}"]: 16 for s in range(RAW)}):
                    for u in range(first, first + RAW):
                        split(u % RAW, u % SPLIT)
            for u in range(end - rest, end):
                split(u % RAW, u % SPLIT)

        split_units(4, UNITS.get(stop, 74))
        if stop < 4:
            return
        with looped(pool, SG, {k["e_ready"]: 9, k["ec_ready"]: 9, k["xd_ready"]: 9, k["xe_ready"]: 9}) as g:
            for c in range(9):
                b, l, n = (c % 2, c % LOADS, P) if c < 8 else (0, LOADS, NS)
                pool.wait_ge(sem("e_ready"), k["e_ready"].next())
                pool.tensor_tensor(s_e[b][:, :, 0:n], s_e[b][:, :, 0:n], s_c[l][:, 0:n].unsqueeze(1).broadcast_to([P, HG, n]),
                                   ALU.mult).then_inc(sem("ec_ready"), k["ec_ready"].adds(1))
                pool.wait_ge(sem("xd_ready"), k["xd_ready"].next())
                to_end = dte[:, :, :].rearrange("p a h -> p (a h)")[0:n, bass.ds(g * HG + c * SH, HG)]
                pool.tensor_tensor(s_xe[b][0:n], s_xd[b][0:n], to_end.unsqueeze(2).broadcast_to([n, HG, SP_]),
                                   ALU.mult).then_inc(sem("xe_ready"), k["xe_ready"].adds(1))
        if stop < 5:
            return
        pool.wait_ge(sem("index_ready"), k["index_ready"].next())

        def cached(b, col):
            if b == 1:
                pool.wait_ge(sem("prompt_over"), 1)
            for dst, src in ((kvb[b], a["cache_ckv"][0]), (kpb[b], a["cache_kpe"][0])):
                pool.indirect_dma_start(
                    out=dst[:, :, :].rearrange("p r c -> p (r c)"), out_offset=None,
                    in_=src.rearrange("n (j r) c -> (n j) (r c)", j=4),
                    in_offset=bass.IndirectOffsetOnAxis(ap=col, axis=0)).then_inc(sem(f"kv_full{b}"), k[f"kv_full{b}"].adds(16))

        for q in range(NB):
            if q >= 2:
                pool.wait_ge(sem("olat_read"), k["olat_read"].next())
            cached(q % 2, pgx[:, q:q + 1])
        if stop >= 7:
            split_units(74, TOTAL_UNITS)

    @block.tensor
    def _(pe):
        k = Counts()
        pe.wait_ge(sem("ident_full"), 16)

        for t in range(9):
            b, n = t % 2, P if t < 8 else NS
            pe.wait_ge(sem(f"x_full{t % 4}"), k[f"x_full{t % 4}"].next(16))
            if t >= 2:
                pe.wait_ge(sem("x_split"), k["x_split"].next())
            for j in range(KT):
                at = ps[:, 2 * b + j // 4, (j % 4) * n:(j % 4) * n + n] if n == P else ps[:, 2 * b, j * n:j * n + n]
                last = pe.transpose(at, xst[t % 4][0:n, j * P:(j + 1) * P], ident[0:n, 0:n])
            last.then_inc(sem("x_turned"), k["x_turned"].adds(1))
        pe.wait_ge(sem("rows_full"), 16 * 9)
        pe.transpose(ps[:, 6, 0:V_END], rows[:, :], ident[0:V_END, 0:V_END])
        pe.wait_ge(sem("drow_wide"), 1)
        pe.transpose(ps[:, 6, 128:144], drow2[:, :], ident[0:16, 0:16]).then_inc(sem("vecs_turned"), 1)
        pe.wait_ge(sem("x_split"), k["x_split"].next(2))

        out_free = ["out_free"]

        def products(b, hi, lo, xh, xl, kt, chunks, m=P, ready=None):
            n = 3 * kt
            for i in range(n):
                j, part = i // 3, i % 3
                if ready and part == 0:
                    pe.wait_ge(sem(ready(j)), k[ready(j)].next())
                w, x = ((hi, xh), (hi, xl), (lo, xh))[part]
                for c, (at, width) in enumerate(chunks):
                    last = pe.matmul(ps[0:m, 3 * b + c, 0:width], w(j), x[:, j, at:at + width],
                                     start=i == 0, stop=i == n - 1)
            return last

        all_tokens = [(c * CH, CH) for c in range(3)]

        def dense(u, b, xh, xl, kt, wait_free=True, ready=None):
            pe.wait_ge(sem("unit_split"), k["unit_split"].next())
            if wait_free:
                pe.wait_ge(sem(f"{out_free[0]}{b}"), k[f"{out_free[0]}{b}"].next())
            s = u % SPLIT
            view = lambda t: lambda j: t[:, j * P:(j + 1) * P]
            products(b, view(whi[s]), view(wlo[s]), xh, xl, kt, all_tokens, ready=ready).then_inc(sem("unit_done"), k["unit_done"].adds(1))

        def sum_rows(b, n):
            pe.wait_ge(sem(f"out_free{b}"), k[f"out_free{b}"].next())
            for i in range(n):
                pe.wait_ge(sem("sq_ready"), k["sq_ready"].next())
                for c, (at, width) in enumerate(all_tokens):
                    last = pe.matmul(ps[:, 3 * b + c, 0:width], ones, sq[:, k["sq_ready"].n % 2 ^ 1, at:at + width],
                                     start=i == 0, stop=i == n - 1)
                last.then_inc(sem("sq_used"), k["sq_used"].adds(1))

        def turn(b, src):
            for c, (at, width) in enumerate(all_tokens):
                last = pe.matmul(ps[R0:R1, 3 * b + c, 0:width], const("turn")[0:R1, :], src[0:R1, at:at + width],
                                 start=True, stop=True)
            last.then_inc(sem("rot_ready"), k["rot_ready"].adds(1))

        for u in range(5):
            dense(u, u % 2, xhi, xlo, KT, wait_free=u >= 2)
        sum_rows(1, 3)
        dense(5, 0, xhi, xlo, KT)
        pe.wait_ge(sem("out_free1"), k["out_free1"].next())
        pe.wait_ge(sem("cst_full"), 16)
        turn(1, small)
        sum_rows(0, 2)
        def query_pair(s):
            pe.wait_ge(sem("unit_split"), k["unit_split"].next())
            for b in range(2):
                pe.wait_ge(sem(f"out_free{b}"), k[f"out_free{b}"].next())
                view = lambda t: lambda j: t[:, j * 2 * QH + b * QH:j * 2 * QH + (b + 1) * QH]
                last = products(b, view(whi[s]), view(wlo[s]), qn_hi, qn_lo, 3, all_tokens, QH)
                last.then_inc(sem("half_done" if b == 0 else "unit_done"), k["half_done" if b == 0 else "unit_done"].adds(1))
            for b in range(2):
                pe.wait_ge(sem(f"out_free{b}"), k[f"out_free{b}"].next())
                turn(b, qh[b])

        pe.wait_ge(sem("qn_split"), k["qn_split"].next(3))
        with looped(pe, 4, {k["unit_split"]: 2, k["unit_done"]: 2, k["half_done"]: 2, k["out_free0"]: 4,
                            k["out_free1"]: 4, k["rot_ready"]: 4}):
            for s in range(2):
                query_pair(s)
        pe.wait_ge(sem("kn_split"), k["kn_split"].next(2))
        pe.wait_ge(sem("key_turned"), k["key_turned"].next(1))
        for i in range(9):
            n = P if i < 8 else NS
            if i >= 2:
                pe.wait_ge(sem("keys_out"), k["keys_out"].next())
            for j in range(2):
                pe.transpose(ps[0:n, 6 + i % 2, j * P:(j + 1) * P], ckv[:, j, i * P:i * P + n], ident[:, :])
            last = pe.transpose(ps[0:n, 6 + i % 2, KL:KL + ROPE], small[R0:R1, i * P:i * P + n], ident[R0:R1, R0:R1])
            last.then_inc(sem("keys_turned"), k["keys_turned"].adds(1))
        pe.wait_ge(sem("keys_out"), k["keys_out"].next(2))

        def turn_values(b):
            pe.wait_ge(sem(f"v_free{b}"), k[f"v_free{b}"].held())
            for j in range(SEQ // P):
                last = pe.matmul(ps[:, 6 + b, j * VH:(j + 1) * VH], kvh[b][:, j * P:(j + 1) * P], ident[:, NOPE:P],
                                 start=True, stop=True)
            last.then_inc(sem("v_turned"), k["v_turned"].adds(1))

        with looped(pe, 2, {k["unit_split"]: 2, k["unit_done"]: 2, k["sub_done"]: 6, k["out_free0"]: 4,
                            k["out_free1"]: 4, k["v_turned"]: 8, k["v_free0"]: 4, k["v_free1"]: 4}):
            for s in range(2):
                pe.wait_ge(sem("unit_split"), k["unit_split"].next())
                for h in range(4):
                    b = h % 2
                    pe.wait_ge(sem(f"out_free{b}"), k[f"out_free{b}"].next())
                    view = lambda t: lambda j: t[:, j * 512 + h * P:j * 512 + (h + 1) * P]
                    last = products(b, view(whi[s]), view(wlo[s]), kn_hi, kn_lo, 2, [(0, 512), (512, 512)])
                    last.then_inc(sem("sub_done" if h < 3 else "unit_done"), k["sub_done" if h < 3 else "unit_done"].adds(1))
                    if h % 2:
                        for v in range(2):
                            pe.wait_ge(sem(f"out_free{v}"), k[f"out_free{v}"].ahead())
                            turn_values(v)
        if stop < 3:
            return

        pe.wait_ge(sem("st_full"), 48)
        for v in range(2):
            pe.wait_ge(sem(f"v_free{v}"), k[f"v_free{v}"].same())
            for j in range(NCONV // 2):
                n = CW + 1 + NB * (CW - 1)
                last = pe.transpose(ps[:, 6 + v, j * n:(j + 1) * n], st[:, (v * 12 + j) * P:(v * 12 + j + 1) * P],
                                    ident[0:n, 0:n])
            last.then_inc(sem("st_turned"), k["st_turned"].adds(1))

        def dense_fours(n, xh, xl):
            with looped(pe, n, {k["unit_split"]: 4, k["unit_done"]: 4, k[out_free[0] + "0"]: 2, k[out_free[0] + "1"]: 2}):
                for u in range(4):
                    dense(u, u % 2, xh, xl, KT)

        dense_fours(NCONV // 4, xhi, xlo)
        dense_fours(4, xhi, xlo)
        pe.wait_ge(sem("cw_ready"), k["cw_ready"].next(2))
        pe.wait_ge(sem("conv_done1"), k["conv_done1"].next(NCONV // 2))
        n = (NB + 1) * (CW - 1)
        for i in range(6):
            if i >= 2:
                pe.wait_ge(sem("crow_ready"), k["crow_ready"].next())
            for j in range(4):
                last = pe.transpose(ps[0:n, 6 + i % 2, j * P:(j + 1) * P], ccol[:, i * 4 + j, :], ident)
            last.then_inc(sem("crow_turned"), k["crow_turned"].adds(1))
        dense_fours(4, xhi, xlo)
        if stop < 4:
            return

        pe.wait_ge(sem("prep_full"), k["prep_full"].next(48))
        pe.wait_ge(sem("crow_ready"), k["crow_ready"].next(2))
        for b in range(2):
            pe.wait_ge(sem(f"out_free{b}"), k[f"out_free{b}"].next())
        for i in range(9):
            n = P if i < 8 else NS
            last = pe.transpose(ps[0:n, 6, i * SH:(i + 1) * SH], dtr[:, i * P:i * P + n], ident[0:SH, 0:SH])
        last.then_inc(sem("dt_turned"), k["dt_turned"].adds(1))
        pe.wait_ge(sem("da_ready"), k["da_ready"].next())
        flat = lambda t: t[:, 0:8, :].rearrange("p a b -> p (a b)")
        pe.matmul(ps[:, 0, 0:256], const("causal"), flat(da), start=True, stop=True)
        pe.matmul(ps[0:NS, 0, 256:288], const("causal_s")[0:NS], da[0:NS, 8], start=True, stop=True)
        pe.matmul(ps[:, 1, 0:256], ones, flat(da), start=True, stop=True)
        pe.matmul(ps[0:NS, 1, 256:288], const("same_s")[0:NS], da[0:NS, 8], start=True, stop=True)
        for i in range(8):
            pe.matmul(ps[0:SH, 2 + i // 4, i % 4 * P:(i % 4 + 1) * P], da[:, i, :], const("causal"), start=True, stop=True)
        last = pe.matmul(ps[0:SH, 4, 0:NS], da[0:NS, 8, :], const("causal_s")[0:NS], start=True, stop=True)
        last.then_inc(sem("sums_ready"), k["sums_ready"].adds(1))
        pe.wait_ge(sem("act_ready"), k["act_ready"].next())
        spread = const("spread")
        for j in range(DI // P):
            last = pe.matmul(ps[:, 5, j * NS:(j + 1) * NS], spread[0:SH, j * P:(j + 1) * P], act_[:, SEQ:TOK],
                             start=True, stop=True)
        last.then_inc(sem("rows_ready"), k["rows_ready"].adds(1))
        pe.wait_ge(sem("prep_read"), k["prep_read"].next(3))

        def ssm_pre(b, l, n=P):
            pe.wait_ge(sem(f"step_full{l}"), k[f"step_full{l}"].next(64))
            pe.wait_ge(sem(f"pre_read{b}"), k[f"pre_read{b}"].held(2))
            for j in range(4):
                pe.transpose(ps[0:n, 2 * b, j * P:(j + 1) * P], s_x[l][:, j, 0:n], ident)
            pe.transpose(ps[0:n, 2 * b + 1, 0:P], s_b[l][:, 0:n], ident)
            pe.matmul(ps[0:n, 2 * b + 1, P:P + n], s_b[l][:, 0:n], s_c[l][:, 0:n], start=True, stop=True).then_inc(sem("pre_ready"), k["pre_ready"].adds(1))

        def ssm_main(b):
            pe.wait_ge(sem(f"pre_read{b}"), k[f"pre_read{b}"].same())
            pe.wait_ge(sem("xe_ready"), k["xe_ready"].next())
            pe.wait_ge(sem("state_ready"), k["state_ready"].next())
            pe.matmul(ps[:, 6, :], s_bt[b][:, :], s_xe[b][:, :].rearrange("p h q -> p (h q)"), start=True, stop=True).then_inc(sem("prod_ready"), k["prod_ready"].adds(1))
            pe.wait_ge(sem("ec_ready"), k["ec_ready"].next())
            pe.wait_ge(sem(f"y_out{b}"), k[f"y_out{b}"].held())
            out = lambda h: ps[64 * (h % 2):64 * (h % 2) + 64, 4 + b, h // 2 * P:(h // 2 + 1) * P]
            for h in range(HG):
                last = pe.matmul(out(h), state[:, h], s_e[b][:, h], start=h < 2, stop=False, skip_group_check=True)
            last.then_inc(sem("state_read"), k["state_read"].adds(1))
            pe.wait_ge(sem("g_ready"), k["g_ready"].next())
            for h in range(HG):
                last = pe.matmul(out(h), s_xd[b][:, h], s_g[b][:, h], start=False, stop=h >= HG - 2, skip_group_check=True)
            last.then_inc(sem("y_ready"), k["y_ready"].adds(1))

        def ssm_samples():
            pe.wait_ge(sem("g_ready"), k["g_ready"].next())
            pe.wait_ge(sem("ec_ready"), k["ec_ready"].next())
            pe.wait_ge(sem("xe_ready"), k["xe_ready"].next())
            pe.wait_ge(sem("y_out0"), k["y_out0"].held())
            for h in range(HG):
                r = 64 * (h % 2)
                pe.matmul(ps[r:r + 64, 4, h // 2 * NS:(h // 2 + 1) * NS], s_xd[0][0:NS, h], s_g[0][0:NS, h, 0:NS],
                          start=h < 2, stop=False, skip_group_check=True)
            for q in range(NB + 1):
                if q < NB:
                    b = q % 2
                    pe.wait_ge(sem(f"si_full{q % LOADS}"), k[f"si_full{q % LOADS}"].next(16))
                    for j in range(4):
                        last = pe.transpose(ps[:, 2 + b, j * P:(j + 1) * P], s_in[q % LOADS][:, j], ident)
                    last.then_inc(sem(f"it_turned"), k[f"it_turned"].adds(1))
                if q:
                    b = (q - 1) % 2
                    pe.wait_ge(sem(f"it_ready{b}"), k[f"it_ready{b}"].next())
                    for h in range(HG):
                        r = 64 * (h % 2)
                        c = h // 2 * NS + (q - 1) * NT
                        last = pe.matmul(ps[r:r + 64, 4, c:c + NT], s_it[b][:, h // 2, r:r + 64], s_e[0][:, h, (q - 1) * NT:q * NT],
                                         start=False, stop=h == HG - 1, skip_group_check=True)
                    last.then_inc(sem("off_done"), k["off_done"].adds(1))
                    pe.wait_ge(sem("u_ready"), k["u_ready"].next())
                    pe.wait_ge(sem(f"new_out{b}"), k[f"new_out{b}"].held())
                    for j in range(4):
                        last = pe.matmul(ps[:, 6 + b, j * P:(j + 1) * P], s_u[b][:, j * P:(j + 1) * P], s_bt[0][0:NS, :],
                                         start=True, stop=True)
                    last.then_inc(sem("upd_ready"), k["upd_ready"].adds(1))

        two = lambda d: pairs(k, d)
        with looped(pe, SG, {k[n]: 9 for n in ("pre_ready", "g_ready", "ec_ready", "xe_ready", "state_ready")} |
                            {k[n]: 8 for n in ("y_ready", "prod_ready", "state_read", "it_turned", "off_done", "u_ready", "upd_ready")} |
                            {k["end_turned"]: 1, k["step_full4"]: 64, k["pre_read0"]: 10, k["pre_read1"]: 8, k["y_out0"]: 5,
                             k["y_out1"]: 4} | two({"it_ready": 4, "new_out": 4}) |
                            {k[f"{n}{l}"]: by for l in range(LOADS) for n, by in (("step_full", 128), ("si_full", 32))}):
            ssm_pre(0, 0)
            for c in range(8):
                ssm_pre((c + 1) % 2, *(((c + 1) % LOADS,) if c < 7 else (LOADS, NS)))
                ssm_main(c % 2)
            pe.wait_ge(sem("state_ready"), k["state_ready"].next())
            for j in range(4):
                last = pe.transpose(ps[:, 7, j * P:(j + 1) * P], state[:, 2 * j:2 * j + 2].rearrange("p h q -> p (h q)"), ident)
            last.then_inc(sem("end_turned"), k["end_turned"].adds(1))
            ssm_samples()
        if stop < 5:
            return

        pe.wait_ge(sem("kr_full"), k["kr_full"].next(32))
        pe.wait_ge(sem("bf_ready"), k["bf_ready"].next(2))

        def scores(n):
            b, q = n // NQ, n % NQ
            if q == 0:
                pe.wait_ge(sem(f"head_full{b}"), k[f"head_full{b}"].next(48))
            pe.wait_ge(sem(f"s_read{n % 2}"), k[f"s_read{n % 2}"].held())
            length = (q + 1) * P
            for c in range(0, length, 512):
                w = min(512, length - c)
                pe.matmul(ps[:, 2 * (n % 2) + c // 512, 0:w], qb[b][:, q * P:(q + 1) * P], kb[b][:, c:c + w], start=True, stop=True)
            at = q * P
            last = pe.matmul(ps[:, 2 * (n % 2) + at // 512, at % 512:at % 512 + P], ident_b[:, :], after_b[:, :], start=False, stop=True,
                             skip_group_check=True)
            last.then_inc(sem("s_ready"), k["s_ready"].adds(1))

        def turn_probs(n):
            q = n % NQ
            pe.wait_ge(sem(f"s_read{n % 2}"), k[f"s_read{n % 2}"].same())
            for part in range(1 + (q >= 4)):
                pe.wait_ge(sem(f"pt_read{part}"), k[f"pt_read{part}"].held())
                for j in range(part * 4, min(q + 1, part * 4 + 4)):
                    last = pe.transpose(ps[:, 4 + part, j % 4 * P:(j % 4 + 1) * P], pr[n % 2][:, j * P:(j + 1) * P], ident)
                last.then_inc(sem(f"t_ready{part}"), k[f"t_ready{part}"].adds(1))

        def weigh(n):
            b, q = n // NQ, n % NQ
            for part in range(1 + (q >= 4)):
                pe.wait_ge(sem(f"pt_read{part}"), k[f"pt_read{part}"].same())
            pe.wait_ge(sem(f"o_read{n % 2}"), k[f"o_read{n % 2}"].held())
            for j in range(q + 1):
                last = pe.matmul(ps[:, 6 + n % 2, 0:VH], ptb[n % 2][:, j * P:(j + 1) * P], vb[b][:, j], start=j == 0, stop=j == q)
            last.then_inc(sem("o_ready"), k["o_ready"].adds(1))

        def attention_pair(final):
            for n in range(16):
                if n < 15:
                    scores(n + 1)
                elif not final:
                    scores(0)
                if n:
                    weigh(n - 1)
                turn_probs(n)
            weigh(15)
            for b in range(2):
                pe.wait_ge(sem(f"o_read{b}"), k[f"o_read{b}"].same())
            for part in range(2):
                pe.wait_ge(sem(f"pt_read{part}"), k[f"pt_read{part}"].held())
                for j in range(4):
                    last = pe.transpose(ps[:, 4 + part, j * P:(j + 1) * P], ob[:, part * 4 + j, :], ident)
                last.then_inc(sem(f"t_ready{part}"), k[f"t_ready{part}"].adds(1))

        g_per = {k["s_ready"]: 16, k["o_ready"]: 16, k["pt_read0"]: 17, k["t_ready0"]: 17,
                 k["pt_read1"]: 9, k["t_ready1"]: 9} | pairs(k, {"head_full": 48, "s_read": 8, "o_read": 8})
        scores(0)
        with looped(pe, HEADS // 2 - 1, g_per):
            attention_pair(False)
        attention_pair(True)
        if stop < 6:
            return

        pe.wait_ge(sem("late_full"), k["late_full"].next(96))
        for b in range(2):
            pe.wait_ge(sem(f"s_read{b}"), k[f"s_read{b}"].same())
            pe.wait_ge(sem(f"pt_read{b}"), k[f"pt_read{b}"].same())
            pe.wait_ge(sem(f"o_read{b}"), k[f"o_read{b}"].same())
        for h in range(HEADS):
            for j in range(2):
                last = pe.transpose(ps[0:NOPE, h // 2, (h % 2 * 2 + j) * P:(h % 2 * 2 + j + 1) * P],
                                    wkv[:, j, h * P:h * P + NOPE], ident)
            if h % 2:
                last.then_inc(sem("uk_turned"), k["uk_turned"].adds(1))
        pe.wait_ge(sem("uk_ready"), k["uk_ready"].next(8))
        for j in range(2):
            for h in range(HEADS):
                last = pe.matmul(ps[:, j, h * NS:(h + 1) * NS], ukt[:, h, j * P:(j + 1) * P], qs[:, h, :], start=True, stop=True)
        last.then_inc(sem("lat_ready"), k["lat_ready"].adds(1))

        def sequence(b):
            pe.wait_ge(sem(f"kv_full{b}"), k[f"kv_full{b}"].next(32))
            for gr in range(17):
                if gr < 16:
                    e = gr % 2
                    pe.wait_ge(sem(f"gr_read{e}"), k[f"gr_read{e}"].held(2))
                    for j in range(2):
                        for r in range(2):
                            pe.transpose(ps[:, 4 + e, (2 * j + r) * P:(2 * j + r + 1) * P], kvb[b][:, gr * 2 + r, j * P:(j + 1) * P], ident)
                    for r in range(2):
                        last = pe.transpose(ps[0:ROPE, 6 + e, r * P:(r + 1) * P], kpb[b][:, gr * 2 + r, :], ident)
                    last.then_inc(sem("gr_turned"), k["gr_turned"].adds(1))
                if gr == 0:
                    pe.wait_ge(sem("cur_ready"), k["cur_ready"].next())
                    pe.wait_ge(sem("olat_read"), k["olat_read"].held())
                if gr:
                    e = (gr - 1) % 2
                    pe.wait_ge(sem(f"gr_read{e}"), k[f"gr_read{e}"].same())
                    for r in range(2):
                        c = (gr - 1) * 2 + r
                        out = ps[:, c // 8, c % 8 * HT:(c % 8 + 1) * HT]
                        pe.matmul(out, kvt[e][:, r], qcur[:, 0], start=True, stop=False)
                        pe.matmul(out, kvt[e][:, 2 + r], qcur[:, 1], start=False, stop=False)
                        pe.matmul(out, kpt[e][:, r], qpcur[:, :], start=False, stop=True)
            for i in range(2):
                pe.matmul(ps[0:NS, 6, 0:HT], kns[:, i, :], qcur[:, i], start=i == 0, stop=False)
            pe.matmul(ps[0:NS, 6, 0:HT], krs[:, :], qpcur[:, :], start=False, stop=True).then_inc(sem("scores_ready"), k["scores_ready"].adds(1))
            pe.wait_ge(sem("max_ready"), k["max_ready"].next())
            pe.matmul(ps[0:HT, 4, 0:P], mx_[:, :], ident, start=True, stop=True).then_inc(sem("maxt_ready"), k["maxt_ready"].adds(1))
            pe.wait_ge(sem("diag_ready"), k["diag_ready"].next())
            pe.matmul(ps[:, 5, 0:HT], ones[0:HT, :], mdiag[:, :], start=True, stop=True).then_inc(sem("maxb_ready"), k["maxb_ready"].adds(1))
            for c in range(5):
                pe.wait_ge(sem("probs_ready"), k["probs_ready"].next())
                for r in range(c * CK, min(c * CK + CK, NPG)):
                    pe.matmul(ps[0:HT, 0, 0:KL], pb_[:, r, :], kvb[b][:, r, :], start=r == 0, stop=False)
            pe.matmul(ps[0:HT, 0, 0:KL], pb_[0:NS, NPG, :], kts[:, :], start=False, stop=True)
            pe.wait_ge(sem("part_ready"), k["part_ready"].next())
            pe.matmul(ps[0:HT, 1, 0:1], ls_[:, :], ones[:, 0:1], start=True, stop=True).then_inc(sem("olat_ready"), k["olat_ready"].adds(1))

        with looped(pe, NB // 2, {k[n]: v for n, v in (("cur_ready", 2), ("gr_turned", 32), ("scores_ready", 2),
                    ("max_ready", 2), ("maxt_ready", 2), ("diag_ready", 2), ("maxb_ready", 2), ("probs_ready", 10),
                    ("part_ready", 2), ("olat_ready", 2), ("olat_read", 2))} | pairs(k, {"kv_full": 32, "gr_read": 32})):
            sequence(0)
            sequence(1)
        pe.wait_ge(sem("olat_read"), k["olat_read"].same())
        for q in range(NB):
            for j in range(2):
                last = pe.transpose(ps[:, 2 + j, q * HT:(q + 1) * HT], oseq[:, q, j * P:(j + 1) * P], ident[0:HT, 0:HT])
        last.then_inc(sem("end_turned"), k["end_turned"].adds(1))
        pe.wait_ge(sem("end_read"), k["end_read"].next(SG + 2))
        for h in range(HEADS):
            r = 64 * (h % 2)
            for j in range(2):
                last = pe.matmul(ps[r:r + 64, 7, h // 2 * NS:(h // 2 + 1) * NS], wkv[:, j, h * P + NOPE:(h + 1) * P], olat[:, j, h, :],
                                 start=j == 0, stop=j == 1)
        last.then_inc(sem("os_ready"), k["os_ready"].adds(1))
        if stop < 7:
            return

        for b in range(2):
            k[f"res_free{b}"].n -= 1
        out_free[0] = "res_free"

        def ones_times(b, src, start, stop_):
            for c, (at, width) in enumerate(all_tokens):
                last = pe.matmul(ps[:, 3 * b + c, 0:width], ones, src[:, at:at + width], start=start, stop=stop_)
            return last

        def group_squares():
            pe.wait_ge(sem("res_free0"), k["res_free0"].next())
            for j in range(4):
                pe.wait_ge(sem("ssq_ready"), k["ssq_ready"].next())
                ones_times(0, sq4[j], j == 0, j == 3).then_inc(sem("ssq_used"), k["ssq_used"].adds(1))

        def group_unit(s, half, ready=None):
            pe.wait_ge(sem("unit_split"), k["unit_split"].next())
            for b in range(2):
                pe.wait_ge(sem(f"res_free{b}"), k[f"res_free{b}"].next())
                view = lambda t: lambda j: t[:, j * 256 + b * P:j * 256 + (b + 1) * P]
                last = products(b, view(whi[s]), view(wlo[s]), ahi[:, 4 * half:4 * half + 4], alo[:, 4 * half:4 * half + 4], 4, all_tokens,
                                ready=ready if b == 0 else None)
                last.then_inc(sem("res_half" if b == 0 else "unit_done"), k["res_half" if b == 0 else "unit_done"].adds(1))

        group_squares()
        for b in range(2):
            k[f"yt_free{b}"].n += 8
        for g in range(6):
            for u in range(4):
                if g < 3 and u == 2:
                    group_squares()
                if u:
                    group_unit(u % 2, g % 2)
                else:
                    group_unit(0, g % 2, ready=(lambda j: "g_split") if g < 4 else lambda j: f"yt_free{j % 2}")
        tile_split = lambda j: "g_split"
        for u in range(4):
            dense(u, u % 2, ahi, alo, KT, ready=tile_split if u == 0 else None)
        dense_fours(1, ahi, alo)

        def layer_norm():
            pe.wait_ge(sem("srow_ready"), k["srow_ready"].next())
            pe.wait_ge(sem("res_free0"), k["res_free0"].next())
            ones_times(0, srow, True, True).then_inc(sem("mean_ready"), k["mean_ready"].adds(1))
            pe.wait_ge(sem("res_free1"), k["res_free1"].next())
            for e in range(KT):
                pe.wait_ge(sem("ssq_ready"), k["ssq_ready"].next())
                ones_times(1, sq2[:, e % 2], e == 0, e == KT - 1).then_inc(sem("ssq_used"), k["ssq_used"].adds(1))

        layer_norm()

        def gate_and_up(ready=None):
            for u in range(4):
                dense(u, u % 2, ahi, alo, KT, ready=ready if u == 0 else None)

        def down(v):
            pe.wait_ge(sem("f_split"), k["f_split"].next(2))
            for s in range(2):
                pe.wait_ge(sem("unit_split"), k["unit_split"].next())
                for e in range(4):
                    pe.wait_ge(sem(f"res_free{e % 2}"), k[f"res_free{e % 2}"].next())
                    view = lambda t: lambda j: t[:, j * 512 + e * P:j * 512 + (e + 1) * P]
                    last = products(e % 2, view(whi[s]), view(wlo[s]), fhi[:, 2 * v:2 * v + 2], flo[:, 2 * v:2 * v + 2], 2, all_tokens)
                    last.then_inc(sem("res_half" if e < 3 else "unit_done"), k["res_half" if e < 3 else "unit_done"].adds(1))

        gate_and_up(tile_split)
        with looped(pe, (NF - 1) // 2, {k["unit_split"]: 12, k["unit_done"]: 12, k["res_half"]: 12, k["f_split"]: 4,
                                        k["res_free0"]: 12, k["res_free1"]: 12}):
            for v in range(2):
                gate_and_up()
                down(v)
        down(0)
        layer_norm()
        thirds_done = 0
        for i in range(9):
            n = P if i < 8 else NS
            if i == 0:
                for b in range(2):
                    pe.wait_ge(sem(f"res_free{b}"), k[f"res_free{b}"].next())
            pe.wait_ge(sem(f"bank_read{i % 2}"), k[f"bank_read{i % 2}"].held(2))
            while thirds_done * CH < i * P + n:
                pe.wait_ge(sem("affine_ready"), k["affine_ready"].next(KT))
                thirds_done += 1
            for e in range(KT):
                last = pe.transpose(ps[0:n, 2 * (i % 2) + e // 4, e % 4 * P:(e % 4 + 1) * P], mm[:, e, i * P:i * P + n], ident)
            last.then_inc(sem("tok_turned"), k["tok_turned"].adds(1))

    @block.scalar
    def _(act):
        k = Counts()

        def x_hi(b, at, n):
            act.wait_ge(sem("x_turned"), k["x_turned"].next())
            src = ps[:, 2 * b:2 * b + 2, :].rearrange("p a n -> p (a n)")[:, 0:KT * n].rearrange("p (j n) -> p j n", n=n)
            act.activation(xhi[:, :, bass.ds(at, n)], src, ACT.Copy).then_inc(sem("x_hi"), k["x_hi"].adds(1))

        for t in range(8):
            x_hi(t % 2, t * P, P)
        x_hi(0, SEQ, NS)
        def small_tile(b, to):
            act.wait_ge(sem("unit_done"), k["unit_done"].next())
            act.activation(thirds(to), out3(b), ACT.Copy).then_inc(sem(f"out_free{b}"), k[f"out_free{b}"].adds(1))

        def norm_root(b, j, n):
            act.wait_ge(sem("sq_used"), k["sq_used"].next(n // P))
            act.activation(thirds(rs[:, j]), out3(b), ACT.Sqrt, bias=epsc[:, 0:1], scale=1.0 / n).then_inc(sem(f"out_free{b}"), k[f"out_free{b}"].adds(1))

        def upper(name, t, hi, n):
            for j in range(n):
                act.wait_ge(sem(f"{name}_normed"), k[f"{name}_normed"].next())
                act.activation(hi[:, j], t[:, j], ACT.Copy).then_inc(sem(f"{name}_hi"), k[f"{name}_hi"].adds(1))

        act.wait_ge(sem("vecs_ready"), 2)
        small_tile(0, small[:, :])
        act.wait_ge(sem("out_free0"), k["out_free0"].same())
        act.dma_start(d_small, small[0:SH, :]).then_inc(sem("stored"), k["stored"].adds(16))
        for u, to in enumerate((cq[:, 0], cq[:, 1], cq[:, 2], ckv[:, 0])):
            small_tile((u + 1) % 2, to)
        norm_root(1, 0, QL)
        upper("qn", cq, qn_hi, 3)
        small_tile(0, ckv[:, 1])
        act.wait_ge(sem("key_turned"), k["key_turned"].next())
        act.dma_start(d_kr, small[R0:R1, :]).then_inc(sem("stored"), k["stored"].adds(16))
        norm_root(0, 1, KL)
        upper("kn", ckv, kn_hi, 2)
        act.wait_ge(sem("kn_normed"), k["kn_normed"].same())
        act.dma_start(d_kvs.rearrange("(k p) n -> p k n", p=P), ckv[:, :, SEQ:TOK]).then_inc(sem("stored"), k["stored"].adds(16))
        act.wait_ge(sem("qn_split"), k["qn_split"].next(3))
        k["out_free1"].n += 1
        with looped(act, 8, {k["half_done"]: 1, k["unit_done"]: 1, k["out_free0"]: 2, k["out_free1"]: 2,
                             k["q_stored0"]: 16, k["q_stored1"]: 16, k["q_turned"]: 2}) as i:
            for b in range(2):
                act.wait_ge(sem("half_done" if b == 0 else "unit_done"), k["half_done" if b == 0 else "unit_done"].next())
                act.wait_ge(sem(f"q_stored{b}"), k[f"q_stored{b}"].same())
                act.activation(thirds(qh[b][0:QH]), out3(b, QH), ACT.Copy).then_inc(sem(f"out_free{b}"), k[f"out_free{b}"].adds(1))
                k[f"out_free{b}"].n += 1
            for b in range(2):
                act.wait_ge(sem("q_turned"), k["q_turned"].next())
                act.dma_start(d_q[bass.ds(i * 2 + b, 1)].rearrange("a p n -> (a p) n"), qh[b][0:QH]).then_inc(sem(f"q_stored{b}"), k[f"q_stored{b}"].adds(16))
        for i in range(9):
            n = P if i < 8 else NS
            to = (o_ckv[0][i * P:i * P + n, :], o_kpe[0][i * P:i * P + n, :]) if i < 8 else (o_ckv[1], o_kpe[1])
            act.wait_ge(sem("keys_out"), k["keys_out"].next())
            for part, dst in zip((tokst[i % 2][0:n, 0:KL], tokst[i % 2][0:n, KL:KL + ROPE]), to):
                act.dma_start(dst, part).then_inc(sem(f"keys_stored{i % 2}"), k[f"keys_stored{i % 2}"].adds(16))
        act.wait_ge(sem("kn_split"), k["kn_split"].next(2))
        act.wait_ge(sem("keys_turned"), k["keys_turned"].next(9))
        act.wait_ge(sem("stored"), k["stored"].same())
        with looped(act, 4, {k["sub_done"]: 3, k["unit_done"]: 1, k["out_free0"]: 2, k["out_free1"]: 2,
                             k["k_stored0"]: 32, k["k_stored1"]: 32, k["v_stored0"]: 32, k["v_stored1"]: 32,
                             k["v_free0"]: 2, k["v_free1"]: 2}) as i:
          for pair in range(2):
            for b in range(2):
                act.wait_ge(sem("sub_done" if pair * 2 + b < 3 else "unit_done"), k["sub_done" if pair * 2 + b < 3 else "unit_done"].next())
                act.wait_ge(sem(f"k_stored{b}"), k[f"k_stored{b}"].same())
                act.wait_ge(sem(f"v_free{b}"), k[f"v_free{b}"].same())
                src = ps[:, 3 * b:3 * b + 2, :].rearrange("p a n -> p (a n)")
                act.activation(kvh[b], src, ACT.Copy).then_inc(sem(f"out_free{b}"), k[f"out_free{b}"].adds(1))
            for b in range(2):
                act.wait_ge(sem(f"out_free{b}"), k[f"out_free{b}"].same())
                act.dma_start(d_k[bass.ds(i * 4 + pair * 2 + b, 1)].rearrange("a p n -> (a p) n"), kvh[b][0:NOPE]).then_inc(sem(f"k_stored{b}"), k[f"k_stored{b}"].adds(16))
            for b in range(2):
                act.wait_ge(sem(f"v_free{b}"), k[f"v_free{b}"].next())
                act.dma_start(d_v[bass.ds(i * 4 + pair * 2 + b, 1)].rearrange("a p n -> (a p) n"), vst[b]).then_inc(sem(f"v_stored{b}"), k[f"v_stored{b}"].adds(16))
        for name in ("keys_stored", "q_stored", "k_stored", "v_stored"):
            for b in range(2):
                act.wait_ge(sem(f"{name}{b}"), k[f"{name}{b}"].same())
        if stop < 3:
            return

        with looped(act, NCONV // 2, {k["unit_done"]: 2} | {k[f"{n}{b}"]: by for b in range(2) for n, by in
                                    (("out_free", 1), ("conv_done", 1), ("cv_free", 1), ("so_stored", 16))}) as i:
            for b in range(2):
                act.wait_ge(sem("unit_done"), k["unit_done"].next())
                act.activation(thirds(xraw[b][:, CW - 1:]), out3(b), ACT.Copy).then_inc(sem(f"out_free{b}"), k[f"out_free{b}"].adds(1))
                act.wait_ge(sem(f"conv_done{b}"), k[f"conv_done{b}"].next())
                act.wait_ge(sem(f"so_stored{b}"), k[f"so_stored{b}"].same())
                act.activation(so[b][:, :], cv[b][:, :], ACT.Silu).then_inc(sem(f"cv_free{b}"), k[f"cv_free{b}"].adds(1))
                act.wait_ge(sem(f"cv_free{b}"), k[f"cv_free{b}"].same())
                act.dma_start(d_xbc[bass.ds((i * 2 + b) * P, P), :], so[b][:, :]).then_inc(sem(f"so_stored{b}"), k[f"so_stored{b}"].adds(16))
        for d, func in ((d_z, ACT.Silu), (d_g, ACT.Sigmoid)):
            with looped(act, 8, {k["unit_done"]: 2} | {k[f"{n}{b}"]: by for b in range(2) for n, by in
                                                       (("out_free", 1), ("zo_stored", 16))}) as i:
                for b in range(2):
                    act.wait_ge(sem("unit_done"), k["unit_done"].next())
                    act.wait_ge(sem(f"zo_stored{b}"), k[f"zo_stored{b}"].same())
                    bias = vecs[:, bass.ds(i * 2 + b, 1)] if func == ACT.Sigmoid else 0.0
                    act.activation(thirds(zo[b][:, :]), out3(b), func, bias=bias).then_inc(sem(f"out_free{b}"), k[f"out_free{b}"].adds(1))
                    act.wait_ge(sem(f"out_free{b}"), k[f"out_free{b}"].same())
                    act.dma_start(d[bass.ds((i * 2 + b) * P, P), :], zo[b][:, :]).then_inc(sem(f"zo_stored{b}"), k[f"zo_stored{b}"].adds(16))
            if func == ACT.Silu:
                act.wait_ge(sem("crow_ready"), k["crow_ready"].next(6))
                act.dma_start(o["conv_prompt"][0, 0], crow[0:3, :]).then_inc(sem("stored"), k["stored"].adds(16))
                act.dma_start(o["conv_sample"][0].rearrange("b t c -> (b t) c"), crow[3:27, :]).then_inc(sem("stored"), k["stored"].adds(16))
            act.wait_ge(sem("x_whole"), k["x_whole"].next(4))
            half = d_x[0:4 * P] if func == ACT.Silu else d_x[4 * P:]
            act.dma_start(half.rearrange("(j p) n -> p j n", p=P), xo[:, :, :]).then_inc(sem("x_stored"), k["x_stored"].adds(16))
        act.wait_ge(sem("stored"), k["stored"].same())
        act.wait_ge(sem("x_stored"), k["x_stored"].same())
        for name in ("zo_stored", "so_stored"):
            for b in range(2):
                act.wait_ge(sem(f"{name}{b}"), k[f"{name}{b}"].same())
        if stop < 4:
            return

        act.wait_ge(sem("prep_full"), k["prep_full"].next(48))
        act.activation(hb[:, 1], hb[:, 1], ACT.Exp).then_inc(sem("rate_ready"), k["rate_ready"].adds(1))
        act.wait_ge(sem("abs_ready"), k["abs_ready"].next())
        act.activation(sp_u[:, :, :], sp_w[:, :, :], ACT.Exp, scale=-1.0).then_inc(sem("u_exp"), k["u_exp"].adds(1))
        act.wait_ge(sem("sums_ready"), k["sums_ready"].next())
        act.activation(act_[:, :], ps[0:SH, 2:5, :].rearrange("p a n -> p (a n)")[:, 0:TOK], ACT.Copy).then_inc(sem("act_ready"), k["act_ready"].adds(1))
        act.wait_ge(sem("act_ready"), k["act_ready"].same())
        act.dma_start(d_acum, act_[:, :]).then_inc(sem("acum_stored"), k["acum_stored"].adds(16))
        act.wait_ge(sem("ends_ready"), k["ends_ready"].next())
        act.activation(cdb[:, :, :], ps[:, 1, 0:288].rearrange("p (a h) -> p a h", h=SH), ACT.Exp).then_inc(sem("prep_read"), k["prep_read"].adds(1))
        act.activation(dte[:, :, :], dte[:, :, :], ACT.Exp).then_inc(sem("prep_read"), k["prep_read"].adds(1))
        act.wait_ge(sem("rows_ready"), k["rows_ready"].next())
        act.activation(cdp[:, :, :], ps[:, 5, :].rearrange("p (j q t) -> p j q t", q=NB, t=NT)[:, :, :, NT - 1], ACT.Exp).then_inc(sem("prep_read"), k["prep_read"].adds(1))

        def ssm_exps(b, l, n=P):
            act.wait_ge(sem(f"step_full{l}"), k[f"step_full{l}"].next(64))
            act.activation(s_e[b][:, :, 0:n], s_a[l][:, :, 0:n], ACT.Exp).then_inc(sem("e_ready"), k["e_ready"].adds(1))
            act.wait_ge(sem("pre_ready"), k["pre_ready"].next())
            act.activation(s_bt[b][0:n, :], ps[0:n, 2 * b + 1, 0:P], ACT.Copy).then_inc(sem(f"pre_read{b}"), k[f"pre_read{b}"].adds(1))
            act.wait_ge(sem("dm_ready"), k["dm_ready"].next())
            act.activation(s_g[b][0:n, :, 0:n], s_g[b][0:n, :, 0:n], ACT.Relu, scale=-1.0).then_inc(sem("relu_ready"), k["relu_ready"].adds(1))
            act.wait_ge(sem("relu_ready"), k["relu_ready"].same())
            act.activation(s_g[b][0:n, :, 0:n], s_g[b][0:n, :, 0:n], ACT.Exp, scale=-1.0).then_inc(sem("exp_ready"), k["exp_ready"].adds(1))

        def y_store(b, g, at, n=P):
            act.wait_ge(sem(f"y_out{b}"), k[f"y_out{b}"].next())
            act.dma_start(d_y[bass.ds(g * 512, 512), bass.ds(at, n)].rearrange("(j p) n -> p j n", p=P),
                                                s_y[b][:, :, 0:n]).then_inc(sem(f"y_stored{b}"), k[f"y_stored{b}"].adds(16))

        with looped(act, SG, {k[n]: 9 for n in ("relu_ready", "pre_ready", "e_ready", "dm_ready", "exp_ready")} |
                             {k["end_read"]: 1, k["st_stored"]: 16, k["it_turned"]: 8, k["off_done"]: 8, k["step_full4"]: 64} |
                             {k[f"{n}{b}"]: by * (5 - b) for n, by in (("pre_read", 1), ("y_out", 1), ("y_stored", 16)) for b in range(2)} |
                             pairs(k, {"it_ready": 4, "new_out": 4}) |
                             {k[f"{n}{l}"]: by for l in range(LOADS) for n, by in (("step_full", 128), ("new_stored", 32))}) as g:
            ssm_exps(0, 0)
            for c in range(8):
                ssm_exps((c + 1) % 2, *(((c + 1) % LOADS,) if c < 7 else (LOADS, NS)))
                y_store(c % 2, g, c * P)
            act.wait_ge(sem("end_read"), k["end_read"].next())
            act.dma_start(o["ssm_prompt"][0, 0].rearrange("h p n -> (h p) n")[bass.ds(g * 512, 512), :]
                                             .rearrange("(j p) n -> p j n", p=P), stout[:, :, :]).then_inc(sem("st_stored"), k["st_stored"].adds(16))
            for q in range(NB + 1):
                if q < NB:
                    b = q % 2
                    act.wait_ge(sem("it_turned"), k["it_turned"].next())
                    if q >= 2:
                        act.wait_ge(sem("off_done"), k["off_done"].next())
                    act.activation(s_it[b][:, :, :], ps[:, 2 + b, :].rearrange("p (j n) -> p j n", n=P), ACT.Copy).then_inc(sem(f"it_ready{b}"), k[f"it_ready{b}"].adds(1))
                if q:
                    b = (q - 1) % 2
                    act.wait_ge(sem(f"new_out{b}"), k[f"new_out{b}"].next())
                    dst = o["ssm_sample"][0, q - 1].rearrange("h p n -> (h p) n")[bass.ds(g * 512, 512), :]
                    act.dma_start(dst.rearrange("(j p) n -> p j n", p=P), s_new[(q - 1) % LOADS][:, :, :]).then_inc(sem(f"new_stored{(q - 1) % LOADS}"), k[f"new_stored{(q - 1) % LOADS}"].adds(16))
            act.wait_ge(sem("off_done"), k["off_done"].next(2))
            y_store(0, g, SEQ, NS)
        act.wait_ge(sem("st_stored"), k["st_stored"].same())
        for b in range(2):
            act.wait_ge(sem(f"y_stored{b}"), k[f"y_stored{b}"].same())
        for l in range(LOADS):
            act.wait_ge(sem(f"new_stored{l}"), k[f"new_stored{l}"].same())
        act.sem_inc(sem("ssm_over"), 1)
        if stop < 5:
            return

        def probs(n):
            act.wait_ge(sem("m_ready"), k["m_ready"].next())
            length = (n % NQ + 1) * P
            src = ps[:, 2 * (n % 2):2 * (n % 2) + 2, :].rearrange("p a n -> p (a n)")[:, 0:length]
            act.activation(pr[n % 2][:, 0:length], src, ACT.Exp, bias=negmax[:, n:n + 1], scale=SCALE,
                                                   accum_out=rowsum[:, n:n + 1]).then_inc(sem(f"s_read{n % 2}"), k[f"s_read{n % 2}"].adds(1))

        def attention_pair(i, final):
            for n in range(16):
                if n == 0:
                    act.wait_ge(sem("t_ready0"), k["t_ready0"].same())
                else:
                    act.wait_ge(sem("t_ready0"), k["t_ready0"].next())
                if n < 15 or not final:
                    probs((n + 1) % 16)
                q = n % NQ
                if q >= 4:
                    act.wait_ge(sem("t_ready1"), k["t_ready1"].next())
                    act.activation(ptb[n % 2][:, 512:(q + 1) * P], ps[:, 5, 0:(q - 3) * P], ACT.Copy).then_inc(sem("pt_read1"), k["pt_read1"].adds(1))
            k["t_ready0"].n += 2
            act.wait_ge(sem("t_ready1"), k["t_ready1"].next())
            act.wait_ge(sem("att_stored"), k["att_stored"].same())
            act.activation(att[:, 512:], ps[:, 5, :], ACT.Copy).then_inc(sem("pt_read1"), k["pt_read1"].adds(1))
            act.wait_ge(sem("pt_read1"), k["pt_read1"].same())
            act.wait_ge(sem("pt_read0"), k["pt_read0"].next(17))
            act.dma_start(d_att[bass.ds(i * P, P), 0:SEQ], att[:, :]).then_inc(sem("att_stored"), k["att_stored"].adds(16))

        probs(0)
        with looped(act, HEADS // 2 - 1, {k["m_ready"]: 16, k["t_ready0"]: 17, k["t_ready1"]: 9, k["pt_read1"]: 9,
                                          k["pt_read0"]: 17, k["att_stored"]: 16, k["s_read0"]: 8, k["s_read1"]: 8}) as i:
            attention_pair(i, False)
        attention_pair(HEADS // 2 - 1, True)
        act.wait_ge(sem("att_stored"), k["att_stored"].same())
        act.sem_inc(sem("prompt_over"), 1)
        if stop < 6:
            return

        for i in range(8):
            act.wait_ge(sem("uk_turned"), k["uk_turned"].next())
            act.activation(ukt[:, 2 * i:2 * i + 2, :].rearrange("p h c -> p (h c)"), ps[0:NOPE, i, :], ACT.Copy).then_inc(sem("uk_ready"), k["uk_ready"].adds(1))
        act.wait_ge(sem("lat_ready"), k["lat_ready"].next())
        for j in range(2):
            act.activation(qlat[:, j].rearrange("p b (h t) -> p b h t", t=NT),
                                               ps[:, j, :].rearrange("p (h b t) -> p b h t", h=HEADS, t=NT), ACT.Copy).then_inc(sem("qlat_ready"), k["qlat_ready"].adds(1))

        def sequence(b):
            for gr in range(16):
                act.wait_ge(sem("gr_turned"), k["gr_turned"].next())
                act.activation(kvt[gr % 2][:, :, :], ps[:, 4 + gr % 2, :].rearrange("p (a n) -> p a n", n=P), ACT.Copy).then_inc(sem(f"gr_read{gr % 2}"), k[f"gr_read{gr % 2}"].adds(1))
            for c in range(5):
                act.wait_ge(sem("sub_ready"), k["sub_ready"].next())
                part = pb_[:, c * CK:min(c * CK + CK, NPG + 1), :]
                act.activation(part, part, ACT.Exp, scale=SCALE).then_inc(sem("probs_ready"), k["probs_ready"].adds(1))

        with looped(act, NB // 2, {k["gr_turned"]: 32, k["sub_ready"]: 10, k["probs_ready"]: 10, k["gr_read0"]: 16, k["gr_read1"]: 16}):
            sequence(0)
            sequence(1)
        act.wait_ge(sem("oats_ready"), k["oats_ready"].next())
        act.dma_start(d_att[:, SEQ:TOK].rearrange("(j p) n -> p j n", p=P), oats[:, :, :]).then_inc(sem("stored"), k["stored"].adds(16))
        act.wait_ge(sem("stored"), k["stored"].same())
        if stop < 7:
            return

        act.sem_inc(sem("samples_over"), 1)

        def root(b, to, n):
            act.activation(thirds(to[:, :]), out3(b), ACT.Sqrt, bias=epsc[:, 1:2], scale=1.0 / n).then_inc(sem(f"res_free{b}"), k[f"res_free{b}"].adds(1))

        for g in range(4):
            act.wait_ge(sem("ssq_used"), k["ssq_used"].next(4))
            root(0, rsrow, DI // SG)
            for j in range(4):
                act.wait_ge(sem("yg_ready"), k["yg_ready"].next())
                act.activation(ahi[:, 4 * (g % 2) + j], yz[:, j], ACT.Copy).then_inc(sem("g_hi"), k["g_hi"].adds(1))
        done = UNITS[6]
        for b in range(2):
            k[f"yt_full{b}"].n += 8 * 32
        for g in range(2):
            act.wait_ge(sem("unit_done"), done + 12 + 4 * g)
            for j in range(4):
                act.wait_ge(sem(f"yt_full{j % 2}"), k[f"yt_full{j % 2}"].next(16))
                act.activation(ahi[:, 4 * g + j], yt[j % 2][:, :], ACT.Copy).then_inc(sem("g_hi"), k["g_hi"].adds(1))
        for b in range(2):
            k[f"gt_free{b}"].n += 8
        for e in range(KT):
            if e % 4 == 0:
                act.wait_ge(sem("unit_done"), done + 20 + e)
            act.wait_ge(sem(f"gt_free{e % 2}"), k[f"gt_free{e % 2}"].next())
            act.activation(ahi[:, e], mm[:, e], ACT.Copy).then_inc(sem("g_hi"), k["g_hi"].adds(1))

        def layer_norm():
            act.wait_ge(sem("mean_ready"), k["mean_ready"].next())
            act.activation(thirds(murow[:, :]), out3(0), ACT.Copy, scale=1.0 / D_MODEL).then_inc(sem("res_free0"), k["res_free0"].adds(1))
            for e in range(KT):
                act.wait_ge(sem("centred"), k["centred"].next())
                if e >= 2:
                    act.wait_ge(sem("ssq_used"), k["ssq_used"].next())
                act.activation(sq2[:, e % 2], mm[:, e], ACT.Square).then_inc(sem("ssq_ready"), k["ssq_ready"].adds(1))
            act.wait_ge(sem("ssq_used"), k["ssq_used"].next(2))
            root(1, rsrow, D_MODEL)
        k["res_free1"].n += 6 * 4 + KT // 2
        layer_norm()
        for e in range(KT):
            act.wait_ge(sem("scaled"), k["scaled"].next())
            act.activation(ahi[:, e], mm[:, e], ACT.Identity, bias=vecs[:, V_L1B + e:V_L1B + e + 1]).then_inc(sem("g_hi"), k["g_hi"].adds(1))

        def gate(v, j):
            act.wait_ge(sem("unit_done"), k["unit_done"].next())
            act.activation(thirds(fg[j]), out3(0), ACT.Silu).then_inc(sem("res_free0"), k["res_free0"].adds(1))
            act.wait_ge(sem("unit_done"), k["unit_done"].next())
            act.wait_ge(sem("res_free1"), k["res_free1"].next())
            act.activation(fhi[:, 2 * v + j], ff[j][:, :], ACT.Copy).then_inc(sem("f_hi"), k["f_hi"].adds(1))

        k["unit_done"].n = TOTAL_UNITS - 6 * NF
        for j in range(2):
            gate(0, j)
        with looped(act, (NF - 1) // 2, {k["unit_done"]: 12, k["f_hi"]: 4, k["res_free0"]: 4, k["res_free1"]: 12}):
            for v in range(2):
                for j in range(2):
                    gate(1 - v, j)
                k["unit_done"].n += 2
                k["res_free1"].n += 4
        k["res_free1"].n += 4
        layer_norm()
        def by_token(tiles):
            for i in tiles:
                n = P if i < 8 else NS
                act.wait_ge(sem("tok_turned"), k["tok_turned"].next())
                act.wait_ge(sem(f"tok_stored{i % 2}"), k[f"tok_stored{i % 2}"].same())
                act.activation(ytok[i % 2][0:n, 0:512], ps[0:n, 2 * (i % 2), :], ACT.Copy).then_inc(sem(f"bank_read{i % 2}"), k[f"bank_read{i % 2}"].adds(1))
                k[f"bank_read{i % 2}"].n += 1
                act.wait_ge(sem(f"bank_read{i % 2}"), k[f"bank_read{i % 2}"].same())
                dst = o["y_prompt"][0, i * P:i * P + n, :] if i < 8 else o["y_sample"].rearrange("b t d -> (b t) d")
                act.dma_start(dst, ytok[i % 2][0:n, :]).then_inc(sem(f"tok_stored{i % 2}"), k[f"tok_stored{i % 2}"].adds(16))

        for c in range(3):
            for e in range(KT):
                act.wait_ge(sem("scaled"), k["scaled"].next())
                third = mm[:, e, c * CH:(c + 1) * CH]
                act.activation(third, third, ACT.Identity, bias=vecs[:, V_L2B + e:V_L2B + e + 1]).then_inc(sem("affine_ready"), k["affine_ready"].adds(1))
            if c == 1:
                by_token(range(2))
        by_token(range(2, 9))
        for b in range(2):
            act.wait_ge(sem(f"tok_stored{b}"), k[f"tok_stored{b}"].same())

    @block.vector
    def _(dve):
        k = Counts()
        def x_lo(b, at, n):
            dve.wait_ge(sem("x_hi"), k["x_hi"].next())
            src = ps[:, 2 * b:2 * b + 2, :].rearrange("p a n -> p (a n)")[:, 0:KT * n].rearrange("p (j n) -> p j n", n=n)
            dve.tensor_tensor(xlo[:, :, bass.ds(at, n)], src,
                                               xhi[:, :, bass.ds(at, n)].bitcast(F32), ALU.subtract).then_inc(sem("x_split"), k["x_split"].adds(1))

        for t in range(8):
            x_lo(t % 2, t * P, P)
        x_lo(0, SEQ, NS)
        dve.wait_ge(sem("rows_full"), 16 * 9)
        dve.tensor_copy(drow2[:, :].rearrange("p (a b) -> p a b", a=2),
                        drow[:, :].unsqueeze(2).broadcast_to([16, 2, 64])).then_inc(sem("drow_wide"), 1)
        dve.wait_ge(sem("vecs_turned"), 1)
        dve.tensor_copy(vecs[:, 0:V_END], ps[:, 6, 0:V_END]).then_inc(sem("vecs_ready"), 1)
        dve.tensor_copy(dskip[:, :], ps[:, 6, 128:144]).then_inc(sem("vecs_ready"), 1)

        def square(j, b, by=1):
            dve.wait_ge(sem(f"out_free{b}"), k[f"out_free{b}"].next(by))
            if j >= 2:
                dve.wait_ge(sem("sq_used"), k["sq_used"].next())
            src = cq[:, j] if j < 3 else ckv[:, j - 3]
            dve.tensor_tensor(sq[:, j % 2], src, src, ALU.mult).then_inc(sem("sq_ready"), k["sq_ready"].adds(1))

        def norm(name, b, r, t, lo, hi, n, g):
            dve.wait_ge(sem(f"out_free{b}"), k[f"out_free{b}"].next())
            dve.reciprocal(rs[:, r], rs[:, r]).then_inc(sem("dve_step"), k["dve_step"].adds(1))
            dve.wait_ge(sem("dve_step"), k["dve_step"].same())
            for j in range(n):
                dve.scalar_tensor_tensor(out=t[:, j], in0=t[:, j], scalar=vecs[:, g + j:g + j + 1], in1=rs[:, r],
                                         op0=ALU.mult, op1=ALU.mult).then_inc(sem(f"{name}_normed"), k[f"{name}_normed"].adds(1))
            for j in range(n):
                dve.wait_ge(sem(f"{name}_hi"), k[f"{name}_hi"].next())
                dve.tensor_tensor(lo[:, j], t[:, j], hi[:, j].bitcast(F32), ALU.subtract).then_inc(sem(f"{name}_split"), k[f"{name}_split"].adds(1))

        def rotate(b, rows_, done):
            dve.wait_ge(sem("rot_ready"), k["rot_ready"].next())
            dve.tensor_tensor(thirds(rot[b][R0:R1]), ps[R0:R1, 3 * b:3 * b + 3, 0:CH],
                                                    thirds(rope_t[R0:R1, 1]), ALU.mult).then_inc(sem(f"out_free{b}"), k[f"out_free{b}"].adds(1))
            dve.tensor_tensor(rows_, rows_, rope_t[R0:R1, 0], ALU.mult).then_inc(sem("dve_step"), k["dve_step"].adds(1))
            dve.wait_ge(sem("dve_step"), k["dve_step"].same())
            dve.wait_ge(sem(f"out_free{b}"), k[f"out_free{b}"].same())
            dve.tensor_tensor(rows_, rows_, rot[b][R0:R1], ALU.add).then_inc(sem(done), k[done].adds(1))

        square(0, 1)
        square(1, 0, 2)
        square(2, 1)
        square(3, 0)
        dve.wait_ge(sem("vecs_ready"), 2)
        norm("qn", 1, 0, cq, qn_lo, qn_hi, 3, V_QN)
        dve.wait_ge(sem("rope_full"), k["rope_full"].next(32))
        rotate(1, small[R0:R1, :], "key_turned")
        square(4, 0)
        norm("kn", 0, 1, ckv, kn_lo, kn_hi, 2, V_KVN)
        dve.wait_ge(sem("kn_split"), k["kn_split"].same())
        with looped(dve, 8, {k["out_free0"]: 2, k["out_free1"]: 2, k["rot_ready"]: 2, k["dve_step"]: 2, k["q_turned"]: 2}):
            for b in range(2):
                k[f"out_free{b}"].n += 1
                rotate(b, qh[b][R0:R1], "q_turned")
        for i in range(9):
            n = P if i < 8 else NS
            dve.wait_ge(sem("keys_turned"), k["keys_turned"].next())
            dve.wait_ge(sem(f"keys_stored{i % 2}"), k[f"keys_stored{i % 2}"].held(32))
            if i < 2:
                dve.wait_ge(sem("sq_used"), k["sq_used"].next(1))
            dve.tensor_copy(tokst[i % 2][0:n], ps[0:n, 6 + i % 2, 0:KL + ROPE]).then_inc(sem("keys_out"), k["keys_out"].adds(1))
        with looped(dve, 8, {k["v_turned"]: 2, k["v_free0"]: 1, k["v_free1"]: 1, k["v_stored0"]: 16, k["v_stored1"]: 16}):
            for b in range(2):
                dve.wait_ge(sem("v_turned"), k["v_turned"].next())
                dve.wait_ge(sem(f"v_stored{b}"), k[f"v_stored{b}"].held(16))
                dve.tensor_copy(vst[b], ps[:, 6 + b, :]).then_inc(sem(f"v_free{b}"), k[f"v_free{b}"].adds(1))
        if stop < 3:
            return

        for b in range(2):
            dve.wait_ge(sem("st_turned"), k["st_turned"].next())
            dve.tensor_copy(cw[:, b * 12:(b + 1) * 12, :],
                                              ps[:, 6 + b, 0:12 * 29].rearrange("p (j n) -> p j n", n=29)).then_inc(sem("cw_ready"), k["cw_ready"].adds(1))
            dve.memset(xraw[b][:, 0:CW - 1], 0.0).then_inc(sem("dve_step"), k["dve_step"].adds(1))
        dve.wait_ge(sem("cw_ready"), k["cw_ready"].same())
        dve.wait_ge(sem("dve_step"), k["dve_step"].same())
        for b in range(2):
            k[f"out_free{b}"].n += 8
        with looped(dve, NCONV // 2, {k["dve_step"]: 8, k["conv_a"]: 14} | {k[f"{n}{b}"]: 1 for b in range(2)
                                                             for n in ("out_free", "conv_done", "cv_free")}) as i:
            for b in range(2):
                t = i * 2 + b
                tap = lambda j: cw[:, bass.ds(t, 1), j:j + 1].rearrange("p a b -> p (a b)")
                sample = cv[b][:, SEQ:].rearrange("p (s t) -> p s t", t=NT)
                dve.wait_ge(sem(f"out_free{b}"), k[f"out_free{b}"].next())
                dve.wait_ge(sem(f"cv_free{b}"), k[f"cv_free{b}"].held())
                dve.tensor_copy(xs7[b][:, :, 0:3], cw[:, bass.ds(t, 1), 5:29].rearrange("p a (s t) -> p (a s) t", t=3)).then_inc(sem("dve_step"), k["dve_step"].adds(1))
                dve.tensor_copy(xs7[b][:, :, 3:7], xraw[b][:, 3 + SEQ:].rearrange("p (s t) -> p s t", t=NT)).then_inc(sem("dve_step"), k["dve_step"].adds(1))
                dve.tensor_copy(ccol[:, bass.ds(t, 1), 0:3].rearrange("p a b -> p (a b)"), xraw[b][:, SEQ:SEQ + 3]).then_inc(sem("dve_step"), k["dve_step"].adds(1))
                dve.tensor_scalar(cv[b][:, 0:SEQ], xraw[b][:, 0:SEQ], tap(0), tap(4), ALU.mult, ALU.add).then_inc(sem("conv_a"), 1)
                dve.wait_ge(sem("dve_step"), k["dve_step"].same())
                dve.tensor_copy(ccol[:, bass.ds(t, 1), 3:27].rearrange("p a (s t) -> p (a s) t", t=3), xs7[b][:, :, 4:7]).then_inc(sem("dve_step"), k["dve_step"].adds(1))
                dve.tensor_scalar(sample, xs7[b][:, :, 0:NT], tap(0), tap(4), ALU.mult, ALU.add).then_inc(sem("conv_a"), 1)
                k["conv_a"].n += 2
                for j in range(1, CW):
                    dve.wait_ge(sem("conv_a"), k["conv_a"].same())
                    dve.scalar_tensor_tensor(out=cv[b][:, 0:SEQ], in0=xraw[b][:, j:j + SEQ], scalar=tap(j),
                                                             in1=cv[b][:, 0:SEQ], op0=ALU.mult, op1=ALU.add).then_inc(sem("conv_a"), k["conv_a"].adds(1))
                    last = dve.scalar_tensor_tensor(out=sample, in0=xs7[b][:, :, j:j + NT], scalar=tap(j), in1=sample,
                                                    op0=ALU.mult, op1=ALU.add)
                    last.then_inc(sem("conv_a" if j < CW - 1 else f"conv_done{b}"), k["conv_a" if j < CW - 1 else f"conv_done{b}"].adds(1))
        def whole_x(half):
            for j in range(4):
                e = half * 4 + j
                dve.tensor_tensor(xo[:, j], xhi[:, e].bitcast(F32), xlo[:, e].bitcast(F32), ALU.add).then_inc(sem("x_whole"), k["x_whole"].adds(1))

        whole_x(0)
        for i in range(6):
            dve.wait_ge(sem("crow_turned"), k["crow_turned"].next())
            dve.tensor_copy(crow[:, i * 512:(i + 1) * 512], ps[0:27, 6 + i % 2, :]).then_inc(sem("crow_ready"), k["crow_ready"].adds(1))
        dve.wait_ge(sem("x_stored"), k["x_stored"].next(16))
        whole_x(1)
        if stop < 4:
            return

        step = k["dve_step"]


        dve.wait_ge(sem("prep_full"), k["prep_full"].next(48))
        dve.wait_ge(sem("dt_turned"), k["dt_turned"].next())
        dve.memset(dt_[:, 8], 0.0).then_inc(step.sem, step.adds(1))
        dve.wait_ge(step.sem, step.same())
        dve.tensor_copy(dt_[:, 0:8], ps[:, 6, 0:256].rearrange("p (a h) -> p a h", h=SH)).then_inc(step.sem, step.adds(1))
        dve.wait_ge(step.sem, step.same())
        dve.tensor_copy(dt_[0:NS, 8], ps[0:NS, 6, 256:288]).then_inc(step.sem, step.adds(1))
        dve.wait_ge(step.sem, step.same())
        dve.tensor_tensor(dt_[:, :, :], dt_[:, :, :], hb[:, 0:1].broadcast_to([P, 9, SH]), ALU.add).then_inc(step.sem, step.adds(1))
        dve.wait_ge(step.sem, step.same())
        dve.tensor_scalar(sp_w[:, :, :], dt_[:, :, :], -1.0, None, ALU.mult).then_inc(step.sem, step.adds(1))
        dve.wait_ge(step.sem, step.same())
        dve.tensor_tensor(sp_w[:, :, :], sp_w[:, :, :], dt_[:, :, :], ALU.max).then_inc(sem("abs_ready"), k["abs_ready"].adds(1))
        dve.wait_ge(sem("u_exp"), k["u_exp"].next())
        dve.tensor_scalar(sp_z[:, :, :], sp_u[:, :, :], 2.0, None, ALU.add).then_inc(step.sem, step.adds(1))
        dve.wait_ge(step.sem, step.same())
        dve.reciprocal(sp_z[:, :, :], sp_z[:, :, :]).then_inc(step.sem, step.adds(1))
        dve.wait_ge(step.sem, step.same())
        dve.tensor_tensor(sp_z[:, :, :], sp_z[:, :, :], sp_u[:, :, :], ALU.mult).then_inc(step.sem, step.adds(1))
        dve.wait_ge(step.sem, step.same())
        dve.tensor_tensor(sp_w[:, :, :], sp_z[:, :, :], sp_z[:, :, :], ALU.mult).then_inc(step.sem, step.adds(1))
        dve.wait_ge(step.sem, step.same())
        dve.tensor_scalar(sp_p[:, :, :], sp_w[:, :, :], 1.0 / 17, None, ALU.mult).then_inc(step.sem, step.adds(1))
        dve.wait_ge(step.sem, step.same())
        for n in range(15, 1, -2):
            dve.scalar_tensor_tensor(out=sp_p[:, :, :], in0=sp_p[:, :, :], scalar=1.0 / n, in1=sp_w[:, :, :],
                                          op0=ALU.add, op1=ALU.mult).then_inc(step.sem, step.adds(1))
            dve.wait_ge(step.sem, step.same())
        dve.scalar_tensor_tensor(out=sp_p[:, :, :], in0=sp_p[:, :, :], scalar=1.0, in1=sp_z[:, :, :], op0=ALU.add, op1=ALU.mult).then_inc(step.sem, step.adds(1))
        dve.wait_ge(step.sem, step.same())
        dve.tensor_scalar(dt_[:, :, :], dt_[:, :, :], 0.0, None, ALU.max).then_inc(step.sem, step.adds(1))
        dve.wait_ge(step.sem, step.same())
        dve.scalar_tensor_tensor(out=dt_[:, :, :], in0=sp_p[:, :, :], scalar=2.0, in1=dt_[:, :, :], op0=ALU.mult, op1=ALU.add).then_inc(step.sem, step.adds(1))
        dve.wait_ge(step.sem, step.same())
        dve.wait_ge(sem("rate_ready"), k["rate_ready"].next())
        dve.scalar_tensor_tensor(out=da[:, :, :], in0=dt_[:, :, :], scalar=-1.0,
                                                   in1=hb[:, 1:2].broadcast_to([P, 9, SH]), op0=ALU.mult, op1=ALU.mult).then_inc(sem("da_ready"), k["da_ready"].adds(1))
        dve.wait_ge(sem("sums_ready"), k["sums_ready"].next())
        dve.memset(acs[:, 8], 0.0).then_inc(step.sem, step.adds(1))
        dve.wait_ge(step.sem, step.same())
        dve.memset(dte[:, 8], 0.0).then_inc(step.sem, step.adds(1))
        dve.wait_ge(step.sem, step.same())
        dve.tensor_copy(acs[:, 0:8], ps[:, 0, 0:256].rearrange("p (a h) -> p a h", h=SH)).then_inc(step.sem, step.adds(1))
        dve.wait_ge(step.sem, step.same())
        dve.tensor_copy(acs[0:NS, 8], ps[0:NS, 0, 256:288]).then_inc(step.sem, step.adds(1))
        dve.wait_ge(step.sem, step.same())
        dve.tensor_tensor(dte[:, 0:8], ps[:, 1, 0:256].rearrange("p (a h) -> p a h", h=SH), acs[:, 0:8], ALU.subtract).then_inc(step.sem, step.adds(1))
        dve.wait_ge(step.sem, step.same())
        dve.tensor_tensor(dte[0:NS, 8], ps[0:NS, 1, 256:288], acs[0:NS, 8], ALU.subtract).then_inc(sem("ends_ready"), k["ends_ready"].adds(1))
        dve.wait_ge(sem("prep_read"), k["prep_read"].next(2))
        dve.wait_ge(sem("prep_read"), k["prep_read"].next(1))

        by_head = lambda t, c, g: t.rearrange("p a h -> p (a h)")[:, bass.ds(c * SH + g * HG, HG)]

        def ssm_prep(b, l, g, c, n=P):
            wide = lambda t, m: by_head(t[:, :, :], c, g)[0:n].unsqueeze(2).broadcast_to([n, HG, m])
            dve.wait_ge(sem(f"step_full{l}"), k[f"step_full{l}"].next(64))
            dve.tensor_tensor(s_g[b][0:n, :, 0:n], s_a[l][0:n, :, 0:n], wide(acs, n), ALU.subtract).then_inc(sem("dm_ready"), k["dm_ready"].adds(1))
            dve.wait_ge(sem("pre_ready"), k["pre_ready"].next())
            xt = ps[0:n, 2 * b, :].rearrange("p (h q) -> p h q", q=SP_)
            dve.tensor_tensor(s_xd[b][0:n], xt, wide(dt_, SP_), ALU.mult).then_inc(sem("xd_ready"), k["xd_ready"].adds(1))
            dve.wait_ge(sem(f"pre_read{b}"), k[f"pre_read{b}"].next())
            dve.tensor_tensor(s_cb[b][0:n, 0:n], ps[0:n, 2 * b + 1, P:P + n],
                              (const("causal") if n == P else const("causal_s"))[0:n, :], ALU.mult).then_inc(sem(f"pre_read{b}"), k[f"pre_read{b}"].adds(1))

        def ssm_decays(b, n=P):
            dve.wait_ge(sem(f"pre_read{b}"), k[f"pre_read{b}"].same())
            dve.wait_ge(sem("exp_ready"), k["exp_ready"].next())
            dve.tensor_tensor(s_g[b][0:n, :, 0:n], s_g[b][0:n, :, 0:n],
                              s_cb[b][0:n, 0:n].unsqueeze(1).broadcast_to([n, HG, n]), ALU.mult).then_inc(sem("g_ready"), k["g_ready"].adds(1))

        def ssm_y(b, l, g, n=P):
            dve.wait_ge(sem(f"y_stored{b}"), k[f"y_stored{b}"].held(16))
            for j in range(4):
                last = dve.scalar_tensor_tensor(out=s_y[b][:, j, 0:n], in0=s_x[l][:, j, 0:n], scalar=dskip[:, bass.ds(g * 4 + j, 1)],
                                                in1=ps[:, 4 + b, j * n:(j + 1) * n], op0=ALU.mult, op1=ALU.add)
            last.then_inc(sem(f"y_out{b}"), k[f"y_out{b}"].adds(1))

        def ssm_state(g, c):
            dve.wait_ge(sem("state_read"), k["state_read"].next())
            dve.tensor_tensor(state[:, :, :], state[:, :, :], by_head(cdb[:, :, :], c, g).unsqueeze(2).broadcast_to([P, HG, SP_]), ALU.mult).then_inc(step.sem, step.adds(1))
            dve.wait_ge(step.sem, step.same())
            dve.wait_ge(sem("prod_ready"), k["prod_ready"].next())
            dve.tensor_tensor(state[:, :, :], state[:, :, :], ps[:, 6, :].rearrange("p (h q) -> p h q", q=SP_), ALU.add).then_inc(sem("state_ready"), k["state_ready"].adds(1))

        with looped(dve, SG, {k[n]: 9 for n in ("pre_ready", "dm_ready", "xd_ready", "exp_ready", "g_ready", "state_ready")} |
                             {k[n]: 8 for n in ("y_ready", "prod_ready", "state_read", "u_ready", "upd_ready", "off_done")} |
                             {step: 8, k["xe_ready"]: 9, k["end_turned"]: 1, k["st_stored"]: 16, k["end_read"]: 1, k["step_full4"]: 64} |
                             {k[f"{n}{b}"]: by * (5 - b) for n, by in (("pre_read", 2), ("y_out", 1), ("y_stored", 16)) for b in range(2)} |
                             pairs(k, {"new_out": 4}) |
                             {k[f"{n}{l}"]: by for l in range(LOADS) for n, by in (("step_full", 128), ("new_stored", 32))}) as g:
            dve.memset(state[:, :, :], 0.0).then_inc(sem("state_ready"), k["state_ready"].adds(1))
            ssm_prep(0, 0, g, 0)
            ssm_decays(0)
            for c in range(8):
                b, n = (c + 1) % 2, P if c < 7 else NS
                ssm_prep(b, (c + 1) % LOADS if c < 7 else LOADS, g, c + 1, n)
                ssm_state(g, c)
                ssm_decays(b, n)
                dve.wait_ge(sem("y_ready"), k["y_ready"].next())
                ssm_y(c % 2, c % LOADS, g)
            dve.wait_ge(sem("end_turned"), k["end_turned"].next())
            dve.wait_ge(sem("st_stored"), k["st_stored"].held(16))
            dve.tensor_copy(stout[:, :, :], ps[:, 7, :].rearrange("p (j n) -> p j n", n=P)).then_inc(sem("end_read"), k["end_read"].adds(1))
            dve.wait_ge(sem("xe_ready"), k["xe_ready"].next(9))
            for q in range(NB + 1):
                if q < NB:
                    dve.tensor_scalar(s_u[q % 2][:, :], s_xe[0][0:NS].rearrange("p h q -> p (h q)"),
                                                       const("batch")[0:NS, q:q + 1], None, ALU.mult).then_inc(sem("u_ready"), k["u_ready"].adds(1))
                if q:
                    b = (q - 1) % 2
                    dve.wait_ge(sem("upd_ready"), k["upd_ready"].next())
                    l = (q - 1) % LOADS
                    dve.wait_ge(sem(f"new_stored{l}"), k[f"new_stored{l}"].held(16))
                    for j in range(4):
                        last = dve.scalar_tensor_tensor(
                            out=s_new[l][:, j], in0=s_in[l][:, j], in1=ps[:, 6 + b, j * P:(j + 1) * P], op0=ALU.mult, op1=ALU.add,
                            scalar=cdp[:, :, :].rearrange("p j q -> p (j q)")[:, bass.ds(g * (4 * NB) + (j * NB + q - 1), 1)])
                    last.then_inc(sem(f"new_out{b}"), k[f"new_out{b}"].adds(1))
            dve.wait_ge(sem("off_done"), k["off_done"].next(8))
            ssm_y(0, LOADS, g, NS)
        if stop < 5:
            return

        dve.wait_ge(sem("pages_full"), k["pages_full"].next(16 * NB))
        dve.tensor_copy(pgf[:, :], pgi[:, :]).then_inc(step.sem, step.adds(1))
        dve.wait_ge(step.sem, step.same())
        dve.tensor_scalar(pgf[:, :], pgf[:, :], 4.0, const("quarter"), ALU.mult, ALU.add).then_inc(step.sem, step.adds(1))
        dve.wait_ge(step.sem, step.same())
        dve.tensor_copy(pgx[:, :], pgf[:, :]).then_inc(sem("index_ready"), k["index_ready"].adds(1))
        dve.tensor_copy(ident_b[:, :], ident).then_inc(sem("bf_ready"), k["bf_ready"].adds(1))
        dve.tensor_copy(after_b[:, :], const("after")).then_inc(sem("bf_ready"), k["bf_ready"].adds(1))

        def row_max(n):
            dve.wait_ge(sem("s_ready"), k["s_ready"].next())
            length = (n % NQ + 1) * P
            src = ps[:, 2 * (n % 2):2 * (n % 2) + 2, :].rearrange("p a n -> p (a n)")[:, 0:length]
            dve.tensor_reduce(rowmax[:, n:n + 1], src, AX, ALU.max).then_inc(step.sem, step.adds(1))
            dve.wait_ge(step.sem, step.same())
            dve.tensor_scalar(negmax[:, n:n + 1], rowmax[:, n:n + 1], -SCALE, None, ALU.mult).then_inc(sem("m_ready"), k["m_ready"].adds(1))

        def out_norm(n):
            b, q = n // NQ, n % NQ
            dve.wait_ge(sem("o_ready"), k["o_ready"].next())
            dve.reciprocal(rowinv[:, n:n + 1], rowsum[:, n:n + 1]).then_inc(step.sem, step.adds(1))
            dve.wait_ge(step.sem, step.same())
            dve.tensor_scalar(ob[:, q, b * VH:(b + 1) * VH], ps[:, 6 + n % 2, 0:VH], rowinv[:, n:n + 1],
                                                      None, ALU.mult).then_inc(sem(f"o_read{n % 2}"), k[f"o_read{n % 2}"].adds(1))

        def attention_pair(final):
            for n in range(16):
                if n < 15 or not final:
                    row_max((n + 1) % 16)
                if n:
                    out_norm(n - 1)
                dve.wait_ge(sem("t_ready0"), k["t_ready0"].next())
                width = min(n % NQ + 1, 4) * P
                dve.tensor_copy(ptb[n % 2][:, 0:width], ps[:, 4, 0:width]).then_inc(sem("pt_read0"), k["pt_read0"].adds(1))
            out_norm(15)
            dve.wait_ge(sem("t_ready0"), k["t_ready0"].next())
            dve.wait_ge(sem("att_stored"), k["att_stored"].held(16))
            dve.tensor_copy(att[:, 0:512], ps[:, 4, :]).then_inc(sem("pt_read0"), k["pt_read0"].adds(1))

        row_max(0)
        with looped(dve, HEADS // 2 - 1, {k["s_ready"]: 16, step: 32, k["m_ready"]: 16, k["o_ready"]: 16, k["t_ready0"]: 17,
                                          k["pt_read0"]: 17, k["att_stored"]: 16, k["o_read0"]: 8, k["o_read1"]: 8}):
            attention_pair(False)
        attention_pair(True)
        if stop < 6:
            return

        dve.wait_ge(sem("late_full"), k["late_full"].next(96))
        dve.memset(snew, -1e30).then_inc(step.sem, step.adds(1))
        dve.tensor_copy(qpb[:, :, :].rearrange("p b (h t) -> p b h t", t=NT),
                             qps[:, :, :].rearrange("p h (b t) -> p b h t", t=NT)).then_inc(step.sem, step.adds(1))
        dve.wait_ge(step.sem, step.same())
        dve.wait_ge(sem("qlat_ready"), k["qlat_ready"].next(2))

        def sequence(b, q):
            dve.tensor_copy(qcur[:, :, :], qlat[:, :, bass.ds(q, 1), :].rearrange("p k a n -> p (k a) n")).then_inc(step.sem, step.adds(1))
            dve.tensor_copy(qpcur[:, :], qpb[:, bass.ds(q, 1), :].rearrange("p a n -> p (a n)")).then_inc(sem("cur_ready"), k["cur_ready"].adds(1))
            for gr in range(16):
                dve.wait_ge(sem("gr_turned"), k["gr_turned"].next())
                dve.tensor_copy(kpt[gr % 2][:, :, :], ps[0:ROPE, 6 + gr % 2, 0:2 * P].rearrange("p (a n) -> p a n", n=P)).then_inc(sem(f"gr_read{gr % 2}"), k[f"gr_read{gr % 2}"].adds(1))
                if gr % 4 == 1 and gr > 1:
                    scores = ps[:, (gr - 5) // 4, :].rearrange("p (r n) -> p n r", n=HT)
                    dve.tensor_reduce(mx5[:, (gr - 5) // 4], scores, AX, ALU.max).then_inc(step.sem, step.adds(1))
            bank = lambda c: ps[:, c, :].rearrange("p (r n) -> p r n", n=HT)
            dve.wait_ge(sem("scores_ready"), k["scores_ready"].next())
            dve.tensor_reduce(mx5[:, 3], bank(3).rearrange("p r n -> p n r"), AX, ALU.max).then_inc(step.sem, step.adds(1))
            dve.tensor_tensor(snew[0:NS, :], ps[0:NS, 6, 0:HT], const("newkeys")[0:NS, bass.ds(q * HT, HT)], ALU.add).then_inc(step.sem, step.adds(1))
            dve.wait_ge(step.sem, step.same())
            dve.tensor_reduce(mx_[:, :], mx5[:, :, :].rearrange("p r n -> p n r"), AX, ALU.max).then_inc(sem("max_ready"), k["max_ready"].adds(1))
            dve.wait_ge(sem("maxt_ready"), k["maxt_ready"].next())
            dve.tensor_reduce(mcol[:, :], ps[0:HT, 4, 0:P], AX, ALU.max).then_inc(step.sem, step.adds(1))
            dve.wait_ge(step.sem, step.same())
            dve.tensor_scalar(mdiag[:, :], ident[0:HT, 0:HT], mcol[:, 0:1], None, ALU.mult).then_inc(sem("diag_ready"), k["diag_ready"].adds(1))
            dve.wait_ge(sem("maxb_ready"), k["maxb_ready"].next())
            dve.tensor_copy(mb_[:, :], ps[:, 5, 0:HT]).then_inc(step.sem, step.adds(1))
            dve.wait_ge(step.sem, step.same())
            for c in range(4):
                dve.tensor_tensor(pb_[:, c * CK:(c + 1) * CK, :], bank(c), mb_[:, :].unsqueeze(1).broadcast_to([P, CK, HT]),
                                  ALU.subtract).then_inc(sem("sub_ready"), k["sub_ready"].adds(1))
            dve.tensor_tensor(pb_[:, NPG, :], snew, mb_[:, :], ALU.subtract).then_inc(sem("sub_ready"), k["sub_ready"].adds(1))
            dve.wait_ge(sem("probs_ready"), k["probs_ready"].next(5))
            dve.tensor_reduce(ls_[:, :], pb_[:, :, :].rearrange("p r n -> p n r"), AX, ALU.add).then_inc(sem("part_ready"), k["part_ready"].adds(1))
            dve.wait_ge(sem("olat_ready"), k["olat_ready"].next())
            dve.reciprocal(ri_[:, :], ps[0:HT, 1, 0:1]).then_inc(step.sem, step.adds(1))
            dve.wait_ge(step.sem, step.same())
            dve.tensor_scalar(oseq[:, bass.ds(q, 1), :].rearrange("p a n -> p (a n)"), ps[0:HT, 0, 0:KL], ri_[:, 0:1],
                              None, ALU.mult).then_inc(sem("olat_read"), k["olat_read"].adds(1))

        with looped(dve, NB // 2, {k[n]: v for n, v in (("cur_ready", 2), ("gr_turned", 32), ("scores_ready", 2),
                    ("max_ready", 2), ("maxt_ready", 2), ("diag_ready", 2), ("maxb_ready", 2), ("probs_ready", 10), ("sub_ready", 10),
                    ("part_ready", 2), ("olat_ready", 2), ("olat_read", 2), ("dve_step", 18))} |
                    pairs(k, {"gr_read": 16})) as i:
            sequence(0, i * 2)
            sequence(1, i * 2 + 1)
        def squares(j0, j1):
            dve.wait_ge(sem("g_split"), k["g_split"].same())
            for j in range(j0, j1):
                dve.wait_ge(sem(f"yt_full{j % 2}"), k[f"yt_full{j % 2}"].next(32))
                dve.tensor_tensor(yz[:, j], yt[j % 2][:, :], gt[j % 2][:, :], ALU.mult).then_inc(sem(f"yt_free{j % 2}"), k[f"yt_free{j % 2}"].adds(1))
                dve.wait_ge(sem(f"yt_free{j % 2}"), k[f"yt_free{j % 2}"].same())
                dve.tensor_tensor(sq4[j], yz[:, j], yz[:, j], ALU.mult).then_inc(sem("ssq_ready"), k["ssq_ready"].adds(1))

        dve.wait_ge(sem("end_turned"), k["end_turned"].next())
        for j in range(2):
            dve.tensor_copy(olat[:, j].rearrange("p h (b t) -> p b h t", t=NT),
                            ps[:, 2 + j, :].rearrange("p (b h t) -> p b h t", b=NB, t=NT)).then_inc(sem("end_read"), k["end_read"].adds(1))
        if stop >= 7:
            squares(0, 4)
        dve.wait_ge(sem("os_ready"), k["os_ready"].next())
        dve.tensor_copy(oats[:, :, :], ps[:, 7, 0:256].rearrange("p (j n) -> p j n", n=NS)).then_inc(sem("oats_ready"), k["oats_ready"].adds(1))
        if stop < 7:
            return

        k["unit_done"].n = UNITS[6]

        def group_root():
            dve.wait_ge(sem("res_free0"), k["res_free0"].next())
            dve.reciprocal(rsrow[:, :], rsrow[:, :]).then_inc(step.sem, step.adds(1))
            dve.wait_ge(step.sem, step.same())

        def group_norm(g, j0, j1):
            for j in range(j0, j1):
                dve.scalar_tensor_tensor(out=yz[:, j], in0=yz[:, j], scalar=vecs[:, V_SSM + 4 * g + j:V_SSM + 4 * g + j + 1],
                                         in1=rsrow[:, :], op0=ALU.mult, op1=ALU.mult).then_inc(sem("yg_ready"), k["yg_ready"].adds(1))

        def group_lo(g, j0, j1):
            for j in range(j0, j1):
                dve.wait_ge(sem("g_hi"), k["g_hi"].next())
                dve.tensor_tensor(alo[:, 4 * (g % 2) + j], yz[:, j], ahi[:, 4 * (g % 2) + j].bitcast(F32), ALU.subtract).then_inc(sem("g_split"), k["g_split"].adds(1))

        def att_lo(g, j0):
            for j in range(j0, j0 + 2):
                dve.wait_ge(sem("g_hi"), k["g_hi"].next())
                dve.wait_ge(sem(f"yt_full{j % 2}"), k[f"yt_full{j % 2}"].next(16))
                dve.tensor_tensor(alo[:, 4 * g + j], yt[j % 2][:, :], ahi[:, 4 * g + j].bitcast(F32), ALU.subtract).then_inc(sem(f"yt_free{j % 2}"), k[f"yt_free{j % 2}"].adds(1))

        def merged_lo(e0, e1):
            for e in range(e0, e1):
                dve.wait_ge(sem("g_hi"), k["g_hi"].next())
                dve.tensor_tensor(alo[:, e], mm[:, e], ahi[:, e].bitcast(F32), ALU.subtract).then_inc(sem("g_split"), k["g_split"].adds(1))

        def add_half(u, b, how):
            dve.wait_ge(sem("res_half" if b == 0 else "unit_done"), k["res_half" if b == 0 else "unit_done"].next())
            dve.wait_ge(sem(f"res_free{b}"), k[f"res_free{b}"].same())
            how(2 * u + b, b)

        def add_unit(u, how):
            for b in range(2):
                add_half(u, b, how)

        def put(e, b):
            dve.tensor_copy(thirds(mm[:, e]), out3(b)).then_inc(sem(f"res_free{b}"), k[f"res_free{b}"].adds(1))

        def add(e, b):
            dve.tensor_tensor(thirds(mm[:, e]), out3(b), thirds(mm[:, e]), ALU.add).then_inc(sem(f"res_free{b}"), k[f"res_free{b}"].adds(1))

        def add_gated(e, b):
            add(e, b)
            dve.wait_ge(sem(f"res_free{b}"), k[f"res_free{b}"].same())
            dve.wait_ge(sem(f"gt_full{b}"), k[f"gt_full{b}"].next(16))
            dve.tensor_tensor(mm[:, e], mm[:, e], gt[b][:, :], ALU.mult).then_inc(sem(f"gt_free{b}"), k[f"gt_free{b}"].adds(1))

        def gate_add(e, b):
            dve.wait_ge(sem(f"gt_full{b}"), k[f"gt_full{b}"].next(16))
            dve.wait_ge(sem(f"gt_free{b}"), k[f"gt_free{b}"].same())
            dve.tensor_tensor(thirds(sq2[:, b]), out3(b), thirds(gt[b][:, :]), ALU.mult).then_inc(sem(f"res_free{b}"), k[f"res_free{b}"].adds(1))
            dve.wait_ge(sem(f"res_free{b}"), k[f"res_free{b}"].same())
            dve.tensor_tensor(mm[:, e], mm[:, e], sq2[:, b], ALU.add).then_inc(sem(f"gt_free{b}"), k[f"gt_free{b}"].adds(1))

        group_root()
        for j in range(5):
            if j < 4:
                group_norm(0, j, j + 1)
            if j:
                group_lo(0, j - 1, j)
        for g in range(3):
            how = put if g == 0 else add
            for b in range(2):
                squares(2 * b, 2 * b + 2)
                add_half(0, b, how)
            add_unit(1, how)
            group_root()
            for b in range(2):
                add_half(2, b, how)
                group_norm(g + 1, 2 * b, 2 * b + 2)
            for b in range(2):
                add_half(3, b, how)
                group_lo(g + 1, 2 * b, 2 * b + 2)
        for g, how in enumerate((add_gated, gate_add)):
            for u in range(4):
                add_unit(u, how)
                if u < 2:
                    att_lo(g, 2 * u)
        for u in range(4):
            add_unit(u, gate_add)
            if u:
                merged_lo(2 * u - 2, 2 * u)
        merged_lo(6, 8)

        def into_sum(e):
            dve.wait_ge(step.sem, step.same())
            if e == 0:
                dve.tensor_copy(srow[:, :], mm[:, 0]).then_inc(step.sem, step.adds(1))
            else:
                dve.tensor_tensor(srow[:, :], srow[:, :], mm[:, e], ALU.add).then_inc(sem("srow_ready" if e == KT - 1 else "dve_step"), k["srow_ready" if e == KT - 1 else "dve_step"].adds(1))

        for e in range(KT):
            b = e % 2
            dve.wait_ge(sem(f"gt_full{b}"), k[f"gt_full{b}"].next(16))
            dve.wait_ge(sem("unit_done"), k["unit_done"].next())
            dve.wait_ge(sem("g_split"), k["g_split"].same())
            dve.scalar_tensor_tensor(out=thirds(mm[:, e]), in0=thirds(gt[b][:, :]), scalar=ALPHA,
                                                           in1=out3(b), op0=ALU.mult, op1=ALU.add).then_inc(sem(f"res_free{b}"), k[f"res_free{b}"].adds(1))
            dve.wait_ge(sem(f"res_free{b}"), k[f"res_free{b}"].same())
            dve.nop().then_inc(sem(f"gt_free{b}"), k[f"gt_free{b}"].adds(1))
            into_sum(e)

        def layer_norm():
            dve.wait_ge(sem("res_free0"), k["res_free0"].next())
            dve.wait_ge(sem("srow_ready"), k["srow_ready"].same())
            for e in range(KT):
                dve.tensor_tensor(mm[:, e], mm[:, e], murow[:, :], ALU.subtract).then_inc(sem("centred"), k["centred"].adds(1))
            dve.wait_ge(sem("res_free1"), k["res_free1"].next())
            dve.wait_ge(sem("centred"), k["centred"].same())

        def scale(e, g, at=0, n=TOK):
            dve.scalar_tensor_tensor(out=mm[:, e, at:at + n], in0=mm[:, e, at:at + n], scalar=vecs[:, g + e:g + e + 1], in1=rsrow[:, at:at + n],
                                     op0=ALU.mult, op1=ALU.mult).then_inc(sem("scaled"), k["scaled"].adds(1))

        layer_norm()
        dve.reciprocal(rsrow[:, :], rsrow[:, :]).then_inc(step.sem, step.adds(1))
        dve.wait_ge(step.sem, step.same())
        for e in range(KT + 1):
            if e < KT:
                scale(e, V_L1G)
            if e:
                dve.wait_ge(sem("g_hi"), k["g_hi"].next())
                dve.scalar_tensor_tensor(out=alo[:, e - 1], in0=mm[:, e - 1], scalar=vecs[:, V_L1B + e - 1:V_L1B + e], in1=ahi[:, e - 1].bitcast(F32),
                                         op0=ALU.add, op1=ALU.subtract).then_inc(sem("g_split"), k["g_split"].adds(1))
        dve.wait_ge(sem("g_split"), k["g_split"].same())
        for e in range(KT):
            dve.tensor_scalar(mm[:, e], mm[:, e], vecs[:, V_L1B + e:V_L1B + e + 1], ALPHA, ALU.add, ALU.mult).then_inc(step.sem, step.adds(1))

        def hidden(v):
            for j in range(2):
                dve.wait_ge(sem("unit_done"), k["unit_done"].next(2))
                dve.wait_ge(sem("res_free0"), k["res_free0"].next())
                dve.wait_ge(sem("f_split"), k["f_split"].same())
                dve.tensor_tensor(thirds(ff[j][:, :]), out3(1), thirds(fg[j]), ALU.mult).then_inc(sem("res_free1"), k["res_free1"].adds(1))
            for j in range(2):
                dve.wait_ge(sem("f_hi"), k["f_hi"].next())
                dve.tensor_tensor(flo[:, 2 * v + j], ff[j][:, :], fhi[:, 2 * v + j].bitcast(F32), ALU.subtract).then_inc(sem("f_split"), k["f_split"].adds(1))

        def down(last=False):
            for e in range(KT):
                dve.wait_ge(sem("res_half" if e % 4 < 3 else "unit_done"), k["res_half" if e % 4 < 3 else "unit_done"].next())
                if e == 0:
                    dve.wait_ge(sem("res_free1"), k["res_free1"].same())
                    dve.wait_ge(step.sem, step.same())
                    dve.wait_ge(sem("f_split"), k["f_split"].same())
                add(e, e % 2)
                if last:
                    dve.wait_ge(sem(f"res_free{e % 2}"), k[f"res_free{e % 2}"].same())
                    into_sum(e)

        hidden(0)
        with looped(dve, (NF - 1) // 2, {k["unit_done"]: 12, k["res_half"]: 12, k["f_hi"]: 4, k["f_split"]: 4,
                                         k["res_free0"]: 12, k["res_free1"]: 12}):
            for v in range(2):
                hidden(1 - v)
                down()
        down(True)
        layer_norm()
        def by_token(tiles):
            for i in tiles:
                n = P if i < 8 else NS
                dve.wait_ge(sem("tok_turned"), k["tok_turned"].next())
                dve.wait_ge(sem(f"tok_stored{i % 2}"), k[f"tok_stored{i % 2}"].held(16))
                dve.tensor_copy(ytok[i % 2][0:n, 512:1024], ps[0:n, 2 * (i % 2) + 1, :]).then_inc(sem(f"bank_read{i % 2}"), k[f"bank_read{i % 2}"].adds(1))

        for c in range(3):
            third = rsrow[:, c * CH:(c + 1) * CH]
            dve.reciprocal(third, third).then_inc(step.sem, step.adds(1))
            dve.wait_ge(step.sem, step.same())
            for e in range(KT):
                scale(e, V_L2G, c * CH, CH)
            if c == 1:
                by_token(range(2))
        by_token(range(2, 9))

    ctx.close()


def kernel(**inputs):
    import numpy as _np
    import concourse.bacc as _bacc
    from concourse import mybir as _mybir
    from concourse.bass_utils import run_bass_kernel_spmd as _run

    table, _, rope = constants()
    inputs["table"], inputs["rope"] = table, rope
    nc = _bacc.Bacc("TRN2", target_bir_lowering=False, num_devices=1)
    arrays, ins, outs = {}, {}, {}
    for name in inputs:
        arrays[f"in_{name}"] = _np.ascontiguousarray(inputs[name])
        ins[name] = nc.dram_tensor(f"in_{name}", arrays[f"in_{name}"].shape,
                                   _mybir.dt.from_np(arrays[f"in_{name}"].dtype), kind="ExternalInput").ap()
    for name, shape in OUTS.items():
        outs[name] = nc.dram_tensor(f"out_{name}", shape, _mybir.dt.float32, kind="ExternalOutput").ap()
    build(nc, ins, outs)
    r = _run(nc, [arrays], core_ids=[0])
    return tuple(r.results[0][f"out_{name}"] for name in OUTS)
```
